# Optimizing a Trainium2 kernel written in Bass

```python
import math
import jax, jax.numpy as jnp
from jax import lax
import numpy as np

D_MODEL = 1024
BATCH = 1
SEQ = 512
DEPTH = 2

HEAD_DIM = 64
BLOCK = 128
DIFF_HEADS = 6
DIFF_QK_DIM = HEAD_DIM // 2
DIFF_V_DIM = HEAD_DIM
DIFF_WIDTH = DIFF_HEADS * DIFF_V_DIM
GMLP_GROUPS = 4
GMLP_GROUP_DIM = 64
GMLP_WIDTH = GMLP_GROUPS * GMLP_GROUP_DIM
CHUNK = 128
SWA_HEADS = 6
SWA_KV_HEADS = 2
SWA_GROUP = SWA_HEADS // SWA_KV_HEADS
SWA_WIDTH = SWA_HEADS * HEAD_DIM
WINDOW = 128
MIX_WIDTH = DIFF_WIDTH + GMLP_WIDTH + SWA_WIDTH
IN_SIZES = (DIFF_HEADS * 2 * DIFF_QK_DIM, DIFF_HEADS * 2 * DIFF_QK_DIM, DIFF_WIDTH,
            GMLP_WIDTH, GMLP_WIDTH,
            SWA_WIDTH, SWA_KV_HEADS * HEAD_DIM, SWA_KV_HEADS * HEAD_DIM)
IN_WIDTH = 384 + 384 + 384 + 256 + 256 + 384 + 128 + 128
D_FF = ((-(-8 * D_MODEL // 3) + 255) // 256) * 256
PLE_DIM = 256
N_ATTN_HEADS = DIFF_HEADS + SWA_HEADS
ALIBI_MAX_EXP = 8.0
EPS = 1e-6
NEG_INF = -1e30


def rmsnorm(x, g):
    x32 = x.astype(jnp.float32)
    y = x32 * lax.rsqrt(jnp.mean(x32 * x32, axis=-1, keepdims=True) + EPS)
    return (y * g.astype(jnp.float32)).astype(x.dtype)

def alibi_slopes():
    k = jnp.arange(1, N_ATTN_HEADS + 1, dtype=jnp.float32)
    s = jnp.exp2(-ALIBI_MAX_EXP * k / N_ATTN_HEADS)
    return s[SWA_HEADS:], s[:SWA_HEADS]

def diff_attention(q, k, v, lam, lam_init, g_sub, slopes):
    b, s_len = q.shape[0], q.shape[1]
    nb = s_len // BLOCK
    scale = DIFF_QK_DIM ** -0.5
    key_pos = jnp.arange(s_len)
    qb = q.reshape(b, nb, BLOCK, DIFF_HEADS, 2, DIFF_QK_DIM).transpose(1, 0, 2, 3, 4, 5)

    def one_block(args):
        q_blk, j = args
        sc = jnp.einsum('bqhcd,bkhcd->bhcqk', q_blk, k,
                        preferred_element_type=jnp.float32) * scale
        q_pos = j * BLOCK + jnp.arange(BLOCK)
        dist = jnp.abs(q_pos[:, None] - key_pos[None, :]).astype(jnp.float32)
        sc = sc - slopes[None, :, None, None, None] * dist
        pr = jax.nn.softmax(sc, axis=-1)
        attn = pr[:, :, 0] - lam * pr[:, :, 1]
        return jnp.einsum('bhqk,bkhd->bqhd', attn.astype(v.dtype), v)

    o = lax.map(one_block, (qb, jnp.arange(nb)))
    o = o.transpose(1, 0, 2, 3, 4).reshape(b, s_len, DIFF_HEADS, DIFF_V_DIM)
    o = rmsnorm(o, g_sub) * (1.0 - lam_init)
    return o.reshape(b, s_len, DIFF_WIDTH)

def spatial_gating(u, v, ln_g, ln_b, w_s, b_s):
    b, s_len = u.shape[0], u.shape[1]
    v32 = v.astype(jnp.float32)
    mu = jnp.mean(v32, axis=-1, keepdims=True)
    var = jnp.mean(jnp.square(v32 - mu), axis=-1, keepdims=True)
    vn = ((v32 - mu) * lax.rsqrt(var + EPS) * ln_g.astype(jnp.float32)
          + ln_b.astype(jnp.float32)).astype(v.dtype)
    nc = s_len // CHUNK
    vc = vn.reshape(b, nc, CHUNK, GMLP_GROUPS, GMLP_GROUP_DIM)
    mixed = jnp.einsum('gts,bnsgd->bntgd', w_s, vc) + b_s.T[:, :, None]
    return u * mixed.reshape(b, s_len, GMLP_WIDTH)

def window_gqa(q, k, v, sinks, slopes):
    b, s_len = q.shape[0], q.shape[1]
    nb = s_len // BLOCK
    k = k.reshape(b, s_len, SWA_KV_HEADS, HEAD_DIM)
    v = v.reshape(b, s_len, SWA_KV_HEADS, HEAD_DIM)
    pad = ((0, 0), (BLOCK, BLOCK), (0, 0), (0, 0))
    kp = jnp.pad(k, pad).reshape(b, nb + 2, BLOCK, SWA_KV_HEADS, HEAD_DIM)
    vp = jnp.pad(v, pad).reshape(b, nb + 2, BLOCK, SWA_KV_HEADS, HEAD_DIM)
    kb = jnp.concatenate([kp[:, :-2], kp[:, 1:-1], kp[:, 2:]], axis=2)
    vb = jnp.concatenate([vp[:, :-2], vp[:, 1:-1], vp[:, 2:]], axis=2)
    qb = q.reshape(b, nb, BLOCK, SWA_KV_HEADS, SWA_GROUP, HEAD_DIM)
    sc = jnp.einsum('bnqkgd,bnckd->bnkgqc', qb, kb,
                    preferred_element_type=jnp.float32) * (HEAD_DIM ** -0.5)
    rel = jnp.arange(3 * BLOCK)[None, :] - BLOCK - jnp.arange(BLOCK)[:, None]
    dist = jnp.abs(rel)
    key_pos = (jnp.arange(nb)[:, None] - 1) * BLOCK + jnp.arange(3 * BLOCK)[None, :]
    valid = (dist <= WINDOW)[None] & ((key_pos >= 0) & (key_pos < s_len))[:, None, :]
    sl = slopes.reshape(SWA_KV_HEADS, SWA_GROUP)
    sc = sc - sl[:, :, None, None] * dist.astype(jnp.float32)
    sc = jnp.where(valid[None, :, None, None], sc, NEG_INF)
    sink = sinks.astype(jnp.float32).reshape(SWA_KV_HEADS, SWA_GROUP)[:, :, None, None]
    m = jnp.maximum(jnp.max(sc, axis=-1, keepdims=True), sink)
    e = jnp.exp(sc - m)
    pr = e / (jnp.sum(e, axis=-1, keepdims=True) + jnp.exp(sink - m))
    o = jnp.einsum('bnkgqc,bnckd->bnqkgd', pr.astype(v.dtype), vb)
    return o.reshape(b, s_len, SWA_WIDTH)

def first_inputs(seed: int = 0) -> dict:
    key = jax.random.key(seed)
    ks = jax.random.split(key, 24)

    def nrm(k, shape, scale):
        return jax.random.normal(k, shape, jnp.float32) * scale

    def gain(k, shape):
        return 1.0 + 0.05 * jax.random.normal(k, shape, jnp.float32)

    L = DEPTH
    return {
        'x': nrm(ks[0], (BATCH, SEQ, D_MODEL), 1.0),
        'p': nrm(ks[1], (DEPTH, BATCH, SEQ, PLE_DIM), 1.0),
        'g_pre_mix': gain(ks[2], (L, D_MODEL)),
        'w_in': nrm(ks[3], (L, D_MODEL, IN_WIDTH), D_MODEL ** -0.5),
        'lam_q1': nrm(ks[4], (L, DIFF_QK_DIM), 0.1),
        'lam_k1': nrm(ks[5], (L, DIFF_QK_DIM), 0.1),
        'lam_q2': nrm(ks[6], (L, DIFF_QK_DIM), 0.1),
        'lam_k2': nrm(ks[7], (L, DIFF_QK_DIM), 0.1),
        'g_diff_sub': gain(ks[8], (L, DIFF_V_DIM)),
        'gmlp_ln_g': gain(ks[9], (L, GMLP_WIDTH)),
        'gmlp_ln_b': nrm(ks[10], (L, GMLP_WIDTH), 0.02),
        'w_spatial': nrm(ks[11], (L, GMLP_GROUPS, CHUNK, CHUNK), CHUNK ** -0.5),
        'b_spatial': gain(ks[12], (L, GMLP_GROUPS, CHUNK)),
        'swa_sinks': nrm(ks[13], (L, SWA_HEADS), 0.5),
        'w_out': nrm(ks[14], (L, MIX_WIDTH, D_MODEL), MIX_WIDTH ** -0.5),
        'g_post_mix': gain(ks[15], (L, D_MODEL)),
        'g_pre_ffn': gain(ks[16], (L, D_MODEL)),
        'w_ffn_in': nrm(ks[17], (L, D_MODEL, 2 * D_FF), D_MODEL ** -0.5),
        'w_ffn_out': nrm(ks[18], (L, D_FF, D_MODEL), D_FF ** -0.5),
        'g_post_ffn': gain(ks[19], (L, D_MODEL)),
        'w_ple_up': nrm(ks[20], (L, PLE_DIM, D_MODEL), PLE_DIM ** -0.5),
        'w_ple_gate': nrm(ks[21], (L, D_MODEL, D_MODEL), D_MODEL ** -0.5),
        'g_ple_gate': gain(ks[22], (L, D_MODEL)),
        'g_ple_post': gain(ks[23], (L, D_MODEL)),
    }

def first_block(x, p, g_pre_mix, w_in, lam_q1, lam_k1, lam_q2, lam_k2, g_diff_sub,
              gmlp_ln_g, gmlp_ln_b, w_spatial, b_spatial, swa_sinks, w_out, g_post_mix,
              g_pre_ffn, w_ffn_in, w_ffn_out, g_post_ffn, w_ple_up, w_ple_gate,
              g_ple_gate, g_ple_post):
    b, s_len = x.shape[0], x.shape[1]
    diff_slopes, swa_slopes = alibi_slopes()
    split_at = np.cumsum(IN_SIZES)[:-1].tolist()
    for l in range(DEPTH):
        h = rmsnorm(x, g_pre_mix[l])
        proj = h @ w_in[l]
        a_q, a_k, a_v, b_u, b_v, c_q, c_k, c_v = jnp.split(proj, split_at, axis=-1)
        lam_init = 0.8 - 0.6 * math.exp(-0.3 * l)
        f32 = jnp.float32
        lam = (jnp.exp(jnp.sum(lam_q1[l].astype(f32) * lam_k1[l].astype(f32)))
               - jnp.exp(jnp.sum(lam_q2[l].astype(f32) * lam_k2[l].astype(f32)))
               + lam_init)
        y_a = diff_attention(
            a_q.reshape(b, s_len, DIFF_HEADS, 2, DIFF_QK_DIM),
            a_k.reshape(b, s_len, DIFF_HEADS, 2, DIFF_QK_DIM),
            a_v.reshape(b, s_len, DIFF_HEADS, DIFF_V_DIM),
            lam, lam_init, g_diff_sub[l], diff_slopes)
        y_b = spatial_gating(b_u, b_v, gmlp_ln_g[l], gmlp_ln_b[l], w_spatial[l], b_spatial[l])
        y_c = window_gqa(c_q, c_k, c_v, swa_sinks[l], swa_slopes)
        y = jnp.concatenate([y_a, y_b, y_c], axis=-1) @ w_out[l]
        x = x + rmsnorm(y, g_post_mix[l])
        h = rmsnorm(x, g_pre_ffn[l])
        gate, up = jnp.split(h @ w_ffn_in[l], 2, axis=-1)
        f = (jax.nn.silu(gate) * up) @ w_ffn_out[l]
        x = x + rmsnorm(f, g_post_ffn[l])
        e = p[l] @ w_ple_up[l]
        g = jax.nn.sigmoid(rmsnorm(x, g_ple_gate[l]) @ w_ple_gate[l])
        x = x + rmsnorm(e * g, g_ple_post[l])
    return x


RET_HEADS = 4
RET_DK = 128
RET_DV = 128
RET_CHUNK = 128
RET_THETA = 10000.0
DIL_HEADS = 8
DIL_DH = 64
DIL_PATTERNS = ((128, 1), (512, 4), (2048, 16))
DIL_BLOCK = 128
ROPE_THETA = 500000.0
ROT_DIM = DIL_DH // 4
GLA_HEADS = 4
GLA_DK = (D_MODEL // 2) // GLA_HEADS
GLA_DV = D_MODEL // GLA_HEADS
GLA_LOWRANK = 16
GLA_TAU = 16.0
GLA_CHUNK = 64
FFN_HIDDEN = 2816

EVEN_SIZES = (RET_HEADS * RET_DK, RET_HEADS * RET_DK, RET_HEADS * RET_DV, RET_HEADS * RET_DV,
              DIL_HEADS * DIL_DH, DIL_HEADS * DIL_DH, DIL_HEADS * DIL_DH)
EVEN_IN = sum(EVEN_SIZES)
EVEN_MIX = RET_HEADS * RET_DV + DIL_HEADS * DIL_DH
GLA_SIZES = (GLA_HEADS * GLA_DK, GLA_HEADS * GLA_DK, GLA_HEADS * GLA_DV, GLA_HEADS * GLA_DV, GLA_LOWRANK)
GLA_IN = sum(GLA_SIZES)
GLA_MIX = GLA_HEADS * GLA_DV


def _split(p, sizes):
    out, start = [], 0
    for s in sizes:
        out.append(p[..., start:start + s])
        start += s
    return out

def _rmsnorm(x, g):
    xf = x.astype(jnp.float32)
    y = xf * lax.rsqrt(jnp.mean(xf * xf, axis=-1, keepdims=True) + EPS)
    return (y * g.astype(jnp.float32)).astype(x.dtype)

def _head_norm(o):
    mu = jnp.mean(o, axis=-1, keepdims=True)
    var = jnp.mean(jnp.square(o - mu), axis=-1, keepdims=True)
    return (o - mu) * lax.rsqrt(var + EPS)

def _swiglu(h, wg, wu, wd):
    return (jax.nn.silu(h @ wg) * (h @ wu)) @ wd

def _rotary(x, inv_freq):
    rot = 2 * inv_freq.shape[0]
    pos = jnp.arange(x.shape[1], dtype=jnp.float32)
    ang = pos[:, None] * inv_freq[None, :]
    cos = jnp.cos(ang)[None, :, None, :].astype(x.dtype)
    sin = jnp.sin(ang)[None, :, None, :].astype(x.dtype)
    x1 = x[..., :rot // 2]
    x2 = x[..., rot // 2:rot]
    return jnp.concatenate([x1 * cos - x2 * sin, x2 * cos + x1 * sin, x[..., rot:]], axis=-1)

def _retention(q, k, v):
    B, S, H, Dk = q.shape
    Dv = v.shape[-1]
    C = RET_CHUNK
    N = S // C
    log_g = jnp.log(1.0 - 2.0 ** (-5.0 - jnp.arange(H, dtype=jnp.float32)))
    to_chunks = lambda t: t.reshape(B, N, C, H, t.shape[-1]).transpose(0, 3, 1, 2, 4)
    qc, kc, vc = to_chunks(q), to_chunks(k), to_chunks(v)
    i = jnp.arange(C, dtype=jnp.float32)
    rel = i[:, None] - i[None, :]
    dmask = jnp.where(rel >= 0, jnp.exp(log_g[:, None, None] * jnp.maximum(rel, 0.0)), 0.0)
    scores = jnp.einsum('bhnid,bhnjd->bhnij', qc, kc) * dmask[None, :, None]
    inner = jnp.einsum('bhnij,bhnje->bhnie', scores, vc)
    k_dec = kc * jnp.exp(log_g[:, None] * (C - 1 - i))[None, :, None, :, None]
    kv = jnp.einsum('bhnjd,bhnje->nbhde', k_dec, vc)
    chunk_decay = jnp.exp(log_g * C)[None, :, None, None]

    def step(s, kv_n):
        return s * chunk_decay + kv_n, s

    _, s_prev = lax.scan(step, jnp.zeros((B, H, Dk, Dv), jnp.float32), kv)
    q_dec = qc * jnp.exp(log_g[:, None] * (i + 1.0))[None, :, None, :, None]
    cross = jnp.einsum('bhnid,nbhde->bhnie', q_dec, s_prev)
    o = inner + cross
    return o.transpose(0, 2, 3, 1, 4).reshape(B, S, H, Dv)

def _dilated_branch(q, k, v, window, dil):
    B, S, H, Dh = q.shape
    L = S // dil
    W = window // dil
    c = DIL_BLOCK
    nb = -(-L // c)
    Lp = nb * c

    def split(t):
        return t.reshape(B, L, dil, H, Dh).transpose(0, 2, 3, 1, 4).reshape(B * dil, H, L, Dh)

    qs = jnp.pad(split(q), ((0, 0), (0, 0), (0, Lp - L), (0, 0))).reshape(B * dil, H, nb, c, Dh)

    def kblocks(t):
        t = jnp.pad(split(t), ((0, 0), (0, 0), (c, Lp - L), (0, 0))).reshape(B * dil, H, nb + 1, c, Dh)
        return jnp.concatenate([t[:, :, :-1], t[:, :, 1:]], axis=3)

    kb, vb = kblocks(k), kblocks(v)
    s = jnp.einsum('zhnqd,zhnkd->zhnqk', qs, kb).astype(jnp.float32) * (Dh ** -0.5)
    qi = jnp.arange(c)[:, None]
    kj = jnp.arange(2 * c)[None, :]
    dist = qi + c - kj
    blk = jnp.arange(nb)[:, None, None]
    valid = (dist >= 0) & (dist <= W) & (blk * c + kj - c >= 0)
    s = jnp.where(valid, s, -jnp.inf)
    m = jnp.max(s, axis=-1, keepdims=True)
    p = jnp.exp(s - m)
    l = jnp.sum(p, axis=-1, keepdims=True)
    o = jnp.einsum('zhnqk,zhnkd->zhnqd', p, vb.astype(jnp.float32)) / l
    lse = (m + jnp.log(l))[..., 0]
    o = o.reshape(B, dil, H, Lp, Dh)[:, :, :, :L].transpose(0, 3, 1, 2, 4).reshape(B, S, H, Dh)
    lse = lse.reshape(B, dil, H, Lp)[..., :L].transpose(0, 3, 1, 2).reshape(B, S, H)
    return o, lse

def _dilated_attention(q, k, v):
    outs, lses = [], []
    for window, dil in DIL_PATTERNS:
        o, lse = _dilated_branch(q, k, v, window, dil)
        outs.append(o)
        lses.append(lse)
    w = jax.nn.softmax(jnp.stack(lses, axis=0), axis=0)
    return jnp.sum(w[..., None] * jnp.stack(outs, axis=0), axis=0)

def _retention_dilated_mixer(h, w_in, w_out):
    B, S, _ = h.shape
    rq, rk, rv, rg, dq, dk, dv = _split(h @ w_in, EVEN_SIZES)
    ret_freq = RET_THETA ** (-jnp.linspace(0.0, 1.0, RET_DK // 2, dtype=jnp.float32))
    rq = _rotary(rq.reshape(B, S, RET_HEADS, RET_DK), ret_freq).astype(jnp.float32)
    rk = _rotary(rk.reshape(B, S, RET_HEADS, RET_DK), ret_freq).astype(jnp.float32) * (RET_DK ** -0.5)
    rv = rv.reshape(B, S, RET_HEADS, RET_DV).astype(jnp.float32)
    o_r = _head_norm(_retention(rq, rk, rv)).reshape(B, S, RET_HEADS * RET_DV)
    o_r = o_r * jax.nn.silu(rg.astype(jnp.float32))
    rope_freq = ROPE_THETA ** (-jnp.arange(0, ROT_DIM, 2, dtype=jnp.float32) / ROT_DIM)
    dq = _rotary(dq.reshape(B, S, DIL_HEADS, DIL_DH), rope_freq)
    dk = _rotary(dk.reshape(B, S, DIL_HEADS, DIL_DH), rope_freq)
    dv = dv.reshape(B, S, DIL_HEADS, DIL_DH)
    o_d = _dilated_attention(dq, dk, dv).reshape(B, S, DIL_HEADS * DIL_DH)
    cat = jnp.concatenate([o_r.astype(h.dtype), o_d.astype(h.dtype)], axis=-1)
    return cat @ w_out

def _gla(q, k, v, log_a):
    B, S, H, Dk = q.shape
    Dv = v.shape[-1]
    C = GLA_CHUNK
    N = S // C
    to_chunks = lambda t: t.reshape(B, N, C, H, t.shape[-1]).transpose(0, 3, 1, 2, 4)
    qc, kc, vc, lac = to_chunks(q), to_chunks(k), to_chunks(v), to_chunks(log_a)
    b = jnp.cumsum(lac, axis=3)
    b_last = b[:, :, :, -1:]
    q_t = qc * jnp.exp(b)
    k_t = kc * jnp.exp(-b)
    causal = jnp.tril(jnp.ones((C, C), dtype=bool))
    scores = jnp.where(causal, jnp.einsum('bhnid,bhnjd->bhnij', q_t, k_t), 0.0)
    inner = jnp.einsum('bhnij,bhnje->bhnie', scores, vc)
    kv = jnp.einsum('bhnjd,bhnje->nbhde', kc * jnp.exp(b_last - b), vc)
    decay = jnp.exp(b_last[:, :, :, 0]).transpose(2, 0, 1, 3)

    def step(s, inp):
        kv_n, d_n = inp
        return s * d_n[..., None] + kv_n, s

    _, s_prev = lax.scan(step, jnp.zeros((B, H, Dk, Dv), jnp.float32), (kv, decay))
    cross = jnp.einsum('bhnid,nbhde->bhnie', q_t, s_prev)
    o = inner + cross
    return o.transpose(0, 2, 3, 1, 4).reshape(B, S, H, Dv)

def _gla_mixer(h, w_in, w_a2, b_a, w_out):
    B, S, _ = h.shape
    q, k, v, r, a_low = _split(h @ w_in, GLA_SIZES)
    log_a = jax.nn.log_sigmoid((a_low @ w_a2 + b_a).astype(jnp.float32)) / GLA_TAU
    q = q.reshape(B, S, GLA_HEADS, GLA_DK).astype(jnp.float32) * (GLA_DK ** -0.5)
    k = k.reshape(B, S, GLA_HEADS, GLA_DK).astype(jnp.float32)
    v = v.reshape(B, S, GLA_HEADS, GLA_DV).astype(jnp.float32)
    log_a = log_a.reshape(B, S, GLA_HEADS, GLA_DK)
    o = _head_norm(_gla(q, k, v, log_a)).reshape(B, S, GLA_MIX)
    o = o * jax.nn.silu(r.astype(jnp.float32))
    return o.astype(h.dtype) @ w_out

def second_inputs(seed: int = 0) -> dict:
    key = jax.random.key(seed)
    ks = jax.random.split(key, 24)
    n_even = (DEPTH + 1) // 2
    n_odd = DEPTH // 2
    f32 = jnp.float32

    def w(k, shape, fan_in):
        return jax.random.normal(k, shape, f32) * (fan_in ** -0.5)

    def gain(k, shape):
        return 1.0 + 0.05 * jax.random.normal(k, shape, f32)

    return {
        "x": jax.random.normal(ks[0], (BATCH, SEQ, D_MODEL), f32),
        "ffn_pre_norm": gain(ks[1], (DEPTH, D_MODEL)),
        "ffn_pre_w_gate": w(ks[2], (DEPTH, D_MODEL, FFN_HIDDEN), D_MODEL),
        "ffn_pre_w_up": w(ks[3], (DEPTH, D_MODEL, FFN_HIDDEN), D_MODEL),
        "ffn_pre_w_down": w(ks[4], (DEPTH, FFN_HIDDEN, D_MODEL), FFN_HIDDEN),
        "mix_norm": gain(ks[5], (DEPTH, D_MODEL)),
        "ab_w_in": w(ks[6], (n_even, D_MODEL, EVEN_IN), D_MODEL),
        "ab_w_out": w(ks[7], (n_even, EVEN_MIX, D_MODEL), EVEN_MIX),
        "gla_w_in": w(ks[8], (n_odd, D_MODEL, GLA_IN), D_MODEL),
        "gla_w_a2": w(ks[9], (n_odd, GLA_LOWRANK, GLA_HEADS * GLA_DK), GLA_LOWRANK),
        "gla_b_a": 0.1 * jax.random.normal(ks[10], (n_odd, GLA_HEADS * GLA_DK), f32),
        "gla_w_out": w(ks[11], (n_odd, GLA_MIX, D_MODEL), GLA_MIX),
        "ffn_post_norm": gain(ks[12], (DEPTH, D_MODEL)),
        "ffn_post_w_gate": w(ks[13], (DEPTH, D_MODEL, FFN_HIDDEN), D_MODEL),
        "ffn_post_w_up": w(ks[14], (DEPTH, D_MODEL, FFN_HIDDEN), D_MODEL),
        "ffn_post_w_down": w(ks[15], (DEPTH, FFN_HIDDEN, D_MODEL), FFN_HIDDEN),
        "final_norm": gain(ks[16], (D_MODEL,)),
    }

def second_block(x, ffn_pre_norm, ffn_pre_w_gate, ffn_pre_w_up, ffn_pre_w_down, mix_norm,
              ab_w_in, ab_w_out, gla_w_in, gla_w_a2, gla_b_a, gla_w_out,
              ffn_post_norm, ffn_post_w_gate, ffn_post_w_up, ffn_post_w_down, final_norm):
    for l in range(DEPTH):
        h = _rmsnorm(x, ffn_pre_norm[l])
        x = x + 0.5 * _swiglu(h, ffn_pre_w_gate[l], ffn_pre_w_up[l], ffn_pre_w_down[l])
        h = _rmsnorm(x, mix_norm[l])
        if l % 2 == 0:
            x = x + _retention_dilated_mixer(h, ab_w_in[l // 2], ab_w_out[l // 2])
        else:
            x = x + _gla_mixer(h, gla_w_in[l // 2], gla_w_a2[l // 2], gla_b_a[l // 2], gla_w_out[l // 2])
        h = _rmsnorm(x, ffn_post_norm[l])
        x = x + 0.5 * _swiglu(h, ffn_post_w_gate[l], ffn_post_w_up[l], ffn_post_w_down[l])
    return _rmsnorm(x, final_norm)


def setup_inputs(seed=0):
    out = dict(first_inputs(seed))
    for name, value in second_inputs(seed + 1).items():
        if name != "x":
            out[name + "_2"] = value
    return out


def reference(
    x, p, g_pre_mix, w_in, lam_q1, lam_k1, lam_q2, lam_k2, g_diff_sub, gmlp_ln_g, gmlp_ln_b,
    w_spatial, b_spatial, swa_sinks, w_out, g_post_mix, g_pre_ffn, w_ffn_in, w_ffn_out,
    g_post_ffn, w_ple_up, w_ple_gate, g_ple_gate, g_ple_post, ffn_pre_norm_2, ffn_pre_w_gate_2,
    ffn_pre_w_up_2, ffn_pre_w_down_2, mix_norm_2, ab_w_in_2, ab_w_out_2, gla_w_in_2, gla_w_a2_2,
    gla_b_a_2, gla_w_out_2, ffn_post_norm_2, ffn_post_w_gate_2, ffn_post_w_up_2,
    ffn_post_w_down_2, final_norm_2,
):
    x = first_block(
        x, p, g_pre_mix, w_in, lam_q1, lam_k1, lam_q2, lam_k2, g_diff_sub, gmlp_ln_g, gmlp_ln_b,
        w_spatial, b_spatial, swa_sinks, w_out, g_post_mix, g_pre_ffn, w_ffn_in, w_ffn_out,
        g_post_ffn, w_ple_up, w_ple_gate, g_ple_gate, g_ple_post,
    )
    return second_block(
        x, ffn_pre_norm_2, ffn_pre_w_gate_2, ffn_pre_w_up_2, ffn_pre_w_down_2, mix_norm_2,
        ab_w_in_2, ab_w_out_2, gla_w_in_2, gla_w_a2_2, gla_b_a_2, gla_w_out_2, ffn_post_norm_2,
        ffn_post_w_gate_2, ffn_post_w_up_2, ffn_post_w_down_2, final_norm_2,
    )


_drawn_inputs = setup_inputs


def setup_inputs(seed=0):
    import zlib

    import numpy as np

    out = dict(_drawn_inputs(seed))
    spreads = {}
    factors = {'lam_q2': 6.723,
     'gmlp_ln_b': 4.587,
     'swa_sinks': 5.18,
     'g_ple_gate': 3.877,
     'ffn_pre_norm_2': 4.539,
     'gla_b_a_2': 5.654,
     'ffn_post_norm_2': 4.741}
    for name, (base, spread) in spreads.items():
        noise = np.random.default_rng([zlib.crc32(name.encode()), seed]).standard_normal(out[name].shape)
        drawn = base * np.exp(spread * noise) if base else spread * noise
        out[name] = __import__('jax').numpy.asarray(drawn.astype(out[name].dtype))
    for name, factor in factors.items():
        out[name] = (out[name] * factor).astype(out[name].dtype)
    return out
```

```python
import math
from contextlib import ExitStack

import numpy as np

import concourse.bass as bass
from concourse import mybir

F32 = mybir.dt.float32
F32R = mybir.dt.float32r
I32 = mybir.dt.int32
ACT = mybir.ActivationFunctionType
ALU = mybir.AluOpType
AX = mybir.AxisListType

P = 128
D = 1024
S = 512
KT = D // P
TB = S // P
EPS = 1e-6
NEG = -1e30
FT = 2816 // P
LAYERS = 2
RING = 4
UNIT = 8 * P

DIFF_H, SWA_H, DIL_H, RET_H, GLA_H = 6, 6, 8, 4, 4
GLA_CHUNK = 64
GLA_DV = 256
AQ, AK, AV, BU, BV, CQ, CK, CV = 0, 3, 6, 9, 11, 13, 16, 17
RQ, RK, RV, RG, DQ, DK, DV = 0, 4, 8, 12, 16, 20, 24
GQ, GK, GV, GR, GA = 0, 4, 8, 16, 24
STAT, BCAST = 0, 1
LIN = (2, 3, 4, 5)
BACK = (2, 0, 3, 4, 5, 1, 6, 7)


def slopes():
    k = np.arange(1, 13, dtype=np.float32)
    s = np.exp2(-8.0 * k / 12)
    return s[6:], s[:6]


def linears():
    out = []
    for l in range(LAYERS):
        out += [(f"a_in{l}", 18, 18, 8), (f"a_out{l}", 8, 0, 10), (f"a_ffn_in{l}", 2 * FT, 2 * FT, 8),
                (f"a_ffn_out{l}", FT, 0, FT), (f"a_ple_up{l}", 2, 8, 0), (f"a_gate{l}", 8, 8, 8)]
    for l in range(LAYERS):
        n, cat = ((28, 8), (25, 4))[l]
        out += [(f"b_pre_in{l}", 2 * FT, 2 * FT, 8), (f"b_pre_out{l}", FT, 0, FT),
                (f"b_mix_in{l}", n, n, 8), (f"b_mix_out{l}", 8, 0, cat),
                (f"b_post_in{l}", 2 * FT, 2 * FT, 8), (f"b_post_out{l}", FT, 0, FT)]
    return out


class Linear:

    def __init__(self, n, u0, e0, m0, moving):
        self.n, self.u0, self.e0, self.m0, self.moving = n, u0, e0, m0, moving


def plan():
    u, e, m, out = 0, len(LIN), 0, {}
    for name, n, banks, moving in linears():
        out[name] = Linear(n, u, e, m, moving)
        u, e, m = u + n, e + banks, m + moving
    return out, u


def column_layout():
    at, n = {}, 0
    for name in ("a_pre", "a_post", "a_pre_ffn", "a_post_ffn", "a_gate", "a_ple", "b_pre", "b_mix", "b_post"):
        for l in range(LAYERS):
            at[f"{name}{l}"] = n
            n += 8
    at["final"] = n
    n += 8
    for name, w in (("diff_rows", 2 * DIFF_H), ("swa_rows", SWA_H), ("dil_rows", 2)):
        at[name] = n
        n += w
    for l in range(LAYERS):
        for name, w in (("g_sub", 1), ("sinks", SWA_H), ("lam", 4 * 32)):
            at[f"{name}{l}"] = n
            n += w
    return at, n


def program(nc, x_in, p_in, weights, cols_in, gmlp_in, dist_in, ident_in, rot_in, rotary_in,
            ret_dil_in, gla_in, wa2_in, y_out):
    lin, UNITS = plan()
    col_at, NCOL = column_layout()

    with ExitStack() as ctx:
        def sb(name, shape, dt=F32):
            return ctx.enter_context(nc.sbuf_tensor(name, shape, dt))

        def sem(name):
            return ctx.enter_context(nc.semaphore(name))

        x = sb("x", [P, KT, S])
        mvh = sb("mvh", [P, KT, S], F32R)
        mvl = sb("mvl", [P, KT, S], F32R)
        big = sb("big", [P, 28, S])
        y = sb("y", [P, KT, S])
        w_raw = sb("w_raw", [P, RING, UNIT])
        w_hi = sb("w_hi", [P, RING, UNIT], F32R)
        w_lo = sb("w_lo", [P, RING, UNIT], F32R)
        tab = sb("tab", [P, 2560])
        scr = sb("scr", [P, 10, S])
        cols = sb("cols", [P, NCOL])
        ident = sb("ident", [P, P])
        ones = sb("ones", [P, P])
        rot = sb("rot", [P, 2, P])
        rstd_b = sb("rstd_b", [P, S])
        diag = sb("diag", [P, TB, P])
        small = sb("small", [P, 256])

        g1, u1, s1 = scr[:, 0:2, :], scr[:, 2:4, :], scr[:, 4:6, :]
        sq = scr[:, 6:10, :]
        scaled, expo = y[:, 0:4, :], y[:, 4:8, :]
        comb, ptile, onorm, osq = scr[:, 0:2, :], scr[:, 2:4, :], scr[:, 4:6, :], scr[:, 6, :]
        gtmp = scr[:, 7:9, :]
        sm_x, sm_t, sm_y = small[:, 0:16], small[:, 16:32], small[:, 32:48]
        neg_max, row_sum = small[:, 48:64], small[:, 64:80]
        inv = small[:, 80:96]
        lam_s = small[:, 96:104]
        stats6 = small[:, 104:128]
        mean_var = small[:, 128:144]
        neg_sinks = small[:, 144:144 + SWA_H]
        sink_c = small[:, 160:168]
        decay = small[:, 168:200]

        banks = [ctx.enter_context(nc.psum_tensor(f"bank{i}", [P, 512], F32)) for i in range(8)]

        x_loaded, p_loaded = [sem(f"x_loaded{i}") for i in range(4)], sem("p_loaded")
        cols_loaded = sem("cols_loaded")
        tables, consts = sem("tables"), sem("consts")
        out_stored = sem("out_stored")
        w_loaded = [sem(f"w_loaded{i}") for i in range(RING)]
        w_hi_ready, w_lo_ready = sem("w_hi_ready"), sem("w_lo_ready")
        unit_done = sem("unit_done")
        bank_free = sem("bank_free")
        mv_hi, mv_lo = sem("mv_hi"), sem("mv_lo")
        x_ready = sem("x_ready")
        y_ready = sem("y_ready")
        ones_set = sem("ones_set")
        dve_chain, act_chain = sem("dve_chain"), sem("act_chain")
        sq_ready, sq_used = sem("sq_ready"), sem("sq_used")
        diag_ready, bcast_done = sem("diag_ready"), sem("bcast_done")
        silu_done, hidden_ready = sem("silu_done"), sem("hidden_ready")
        p_hi, p_lo = sem("p_hi"), sem("p_lo")
        gate_sig, z_ready = sem("gate_sig"), sem("z_ready")
        vt_done, vt_copied = sem("vt_done"), sem("vt_copied")
        scores_done, scores_scaled, exp_done = sem("scores_done"), sem("scores_scaled"), sem("exp_done")
        probs_ready, pt_done, pt_copied = sem("probs_ready"), sem("pt_done"), sem("pt_copied")
        pv_done = sem("pv_done")
        osq_ready, onorm_ready, ot_done = sem("osq_ready"), sem("onorm_ready"), sem("ot_done")
        gated_ready = sem("gated_ready")
        lam_sum, lam_exp = sem("lam_sum"), sem("lam_exp")
        sink_sum, sink_exp = sem("sink_sum"), sem("sink_exp")
        keys_masked = sem("keys_masked")
        vn_ready, mixed_done = sem("vn_ready"), sem("mixed_done")
        rot_done, rotated = sem("rot_done"), sem("rotated")
        ret_scores, ret_decayed, ret_pv = sem("ret_scores"), sem("ret_decayed"), sem("ret_pv")
        alow_ready, z_done, z_soft, log_a = sem("alow_ready"), sem("z_done"), sem("z_soft"), sem("log_a")
        b_done, b_exp, b_used, kdec_ready = sem("b_done"), sem("b_exp"), sem("b_used"), sem("kdec_ready")
        kt_done, kt_copied = sem("kt_done"), sem("kt_copied")
        gsc_done, gsc_masked = sem("gsc_done"), sem("gsc_masked")
        kv_done, state_ready, gla_o = sem("kv_done"), sem("state_ready"), sem("gla_o")

        def ge(eng, s, v):
            if not isinstance(v, int) or v > 0:
                eng.wait_ge(s, v)

        def unit_loop(eng, n, body, tail=0):
            head = (n - tail) % RING
            for i in range(head):
                body(0, i)
            turns = (n - tail - head) // RING
            if turns:
                with eng.Fori(0, turns) as t:
                    for j in range(RING):
                        body(t, head + j)
            for i in range(n - tail, n):
                body(0, i)

        class Chain:

            def __init__(self, eng, s):
                self.eng, self.s, self.n = eng, s, 0

            def __call__(self, ins):
                ins.then_inc(self.s, 1)
                self.n += 1
                self.eng.wait_ge(self.s, self.n)

        def col(name, k=0, n=1):
            return cols[:, col_at[name] + k:col_at[name] + k + n]

        diff_slopes, swa_slopes = slopes()

        class Pair:
            pass

        def tok(tile, tb, c0, n):
            return big[:, tile, tb * P + c0:tb * P + c0 + n]

        def state(n, h):
            return y[:, 2 * (n % 2) + h // 2, (h % 2) * GLA_DV:(h % 2 + 1) * GLA_DV]

        diff_dist, swa_dist = tab[:, 1280:2176], tab[:, 2176:2560]
        logc = tab[:, 2048:2560]

        diff_keys = [big[:, 18 + i, :] for i in range(10)] + [scr[:, 7, :], scr[:, 8, :]]
        swa_keys = diff_keys[0:SWA_H]

        def diff_pairs():
            out = []
            for qb in range(TB):
                for h in range(DIFF_H):
                    q = Pair()
                    q.qb, q.h, q.kb0, q.nkb = qb, h, 0, TB
                    q.parts = []
                    for c in range(2):
                        q.parts.append((big[:, AQ + h // 2, qb * P:(qb + 1) * P], diff_keys[2 * h + c]))
                    q.masked = 2 * h + 2
                    q.bias, q.scale = diff_dist[:, 384 - qb * P:896 - qb * P], float(diff_slopes[h])
                    q.v = lambda kb, h=h: tok(AV + h // 2, kb, 64 * (h % 2), 64)
                    q.first = 3e38
                    out.append(q)
            return out

        def swa_pairs(l):
            out = []
            for qb in range(TB):
                for h in range(SWA_H):
                    q = Pair()
                    kv, t = h // 3, h % 3
                    kb1 = min(TB, qb + 2)
                    q.qb, q.h, q.kb0 = qb, h, max(0, qb - 1)
                    q.nkb = kb1 - q.kb0
                    q.parts = [(big[:, CQ + t, qb * P:(qb + 1) * P], swa_keys[h][:, q.kb0 * P:kb1 * P])]
                    q.masked = h + 1
                    c0 = (q.kb0 - qb + 1) * P
                    q.bias, q.scale = swa_dist[:, c0:c0 + q.nkb * P], float(swa_slopes[h])
                    q.v = lambda kb, kv=kv: tok(CV, kb, 64 * kv, 64)
                    q.first = neg_sinks[:, h:h + 1]
                    out.append(q)
            return out

        def dil_pairs():
            out = []
            for qb in range(TB):
                for h in range(DIL_H):
                    q = Pair()
                    q.qb, q.h, q.kb0, q.nkb = qb, h, 0, qb + 1
                    q.parts = [(big[:, DQ + h // 2, qb * P:(qb + 1) * P], big[:, RQ + h, 0:(qb + 1) * P])]
                    q.masked = h + 1
                    q.bias, q.scale = logc[:, 384 - qb * P:512], 0.125
                    q.v = lambda kb, h=h: tok(DV + h // 2, kb, 64 * (h % 2), 64)
                    q.first = 3e38
                    out.append(q)
            return out

        class Attention:

            def __init__(self, pairs, heads, comps, tile0, item0, pair0, block0):
                self.pairs, self.heads, self.comps, self.tile0 = pairs, heads, comps, tile0
                self.item0, self.pair0, self.block0 = item0, pair0, block0
                self.tiles = heads // 2

            def stat(self, t, c):
                q = self.pairs[t]
                return 2 * (t % 4) + c if self.comps == 2 else 8 * (q.qb % 2) + q.h

            def steps(self):
                return len(self.pairs) + 7

            def due(self, t, lag):
                q = t - lag
                if q >= 0 and (q + 1) % self.heads == 0 and q < len(self.pairs):
                    return q // self.heads
                return None

        atts, i0, p0, b0, probs0, keys0 = [], 0, 0, 0, 0, 0
        for kind, l in (("diff", 0), ("swa", 0), ("diff", 1), ("swa", 1), ("dil", 0)):
            pairs = {"diff": diff_pairs, "swa": lambda: swa_pairs(l), "dil": dil_pairs}[kind]()
            comps = 2 if kind == "diff" else 1
            heads, tile0 = {"diff": (6, 0), "swa": (6, 5), "dil": (8, 4)}[kind]
            if kind == "dil":
                RET_BLOCK0, b0 = b0, b0 + TB
            a = Attention(pairs, heads, comps, tile0, i0, p0, b0)
            a.kind, a.layer, a.probs0, a.keys0 = kind, l, probs0, keys0
            keys0 += {"diff": 2 * DIFF_H, "swa": SWA_H, "dil": DIL_H}[kind]
            a.m0 = {"diff": lin[f"a_out{l}"].m0, "swa": lin[f"a_out{l}"].m0 + TB + 2,
                    "dil": lin["b_mix_out0"].m0 + TB}[kind]
            probs0 += len(pairs) if comps == 2 else 0
            atts.append(a)
            i0, p0, b0 = i0 + comps * len(pairs), p0 + len(pairs), b0 + TB
        DIFF_ATT, SWA_ATT, DIL_ATT = (atts[0], atts[2]), (atts[1], atts[3]), atts[4]
        GLA_BLOCK0 = b0
        VT = {"a0": ([AV, AV + 1, AV + 2, BV, BV + 1, CV], 0), "a1": ([AV, AV + 1, AV + 2, BV, BV + 1, CV], 6),
              "b0": ([RV + i for i in range(4)] + [DV + i for i in range(4)], 12),
              "b1": ([GV + i for i in range(8)], 20)}
        NORM = {}
        for l in range(LAYERS):
            for n in ("a_in", "a_out", "a_ffn_in", "a_ffn_out", "a_gate", "a_ple"):
                NORM[f"{n}{l}"] = len(NORM)
        for l in range(LAYERS):
            for n in ("b_pre_in", "b_mix_in", "b_post_in"):
                NORM[f"{n}{l}"] = len(NORM)
        NORM["final"] = len(NORM)
        XR = {}
        for n in [f"a_{k}{l}" for l in range(LAYERS) for k in ("mix", "ffn", "ple")] + [
                f"b_{k}{l}" for l in range(LAYERS) for k in ("pre", "mix", "post")]:
            XR[n] = 8 * len(XR)
        XIN = {"a_in1": "a_ple0", "b_pre_in0": "a_ple1", "b_pre_in1": "b_post0"}
        for l in range(LAYERS):
            XIN.update({f"a_ffn_in{l}": f"a_mix{l}", f"a_gate{l}": f"a_ffn{l}", f"b_mix_in{l}": f"b_pre{l}",
                        f"b_post_in{l}": f"b_mix{l}"})
        XIN = {k: XR[v] for k, v in XIN.items()}
        FFN = {n: FT * i for i, n in enumerate(("a_ffn_in0", "a_ffn_in1", "b_pre_in0", "b_post_in0", "b_pre_in1",
                                                "b_post_in1"))}

        block = ctx.enter_context(nc.Block())

        @block.sync
        def _(sp):
            def load(u, slot):
                return sp.dma_start(w_raw[:, slot, :], weights[bass.ds(u, 1), :, :].rearrange("u p n -> p (u n)"))

            sp.dma_start(cols[:, :], cols_in).then_inc(cols_loaded, 16)
            for u in range(RING):
                load(u, u).then_inc(w_loaded[u], 16)
                sp.dma_start(x[:, 2 * u:2 * u + 2, :], x_in[:, 2 * u:2 * u + 2, :]).then_inc(x_loaded[u], 16)
            sp.dma_start(ident[:, :], ident_in).then_inc(consts, 16)
            sp.dma_start(rot[:, :, :], rot_in).then_inc(consts, 16)
            turns = (UNITS - RING) // RING
            with sp.Fori(0, turns) as t:
                for j in range(RING):
                    sp.wait_ge(w_lo_ready, t * RING + j + 1)
                    load(t * RING + RING + j, j).then_inc(w_loaded[j], 16)
            for u in range(RING + turns * RING, UNITS):
                sp.wait_ge(w_lo_ready, u - RING + 1)
                load(u, u % RING).then_inc(w_loaded[u % RING], 16)
            sp.wait_ge(y_ready, 8)
            sp.dma_start(y_out, y[:, :, :]).then_inc(out_stored, 16)
            sp.wait_ge(out_stored, 16)

        @block.gpsimd
        def _(pool):
            def split(u, slot):
                pool.wait_ge(w_hi_ready, u + 1)
                nc.gpsimd.tensor_tensor(w_lo[:, slot, :], w_raw[:, slot, :], w_hi[:, slot, :].bitcast(F32),
                                        ALU.subtract).then_inc(w_lo_ready, 1)

            done = [0]

            def splits(until):
                u0 = done[0]
                turns = (until - u0) // RING
                if turns:
                    with pool.Fori(0, turns) as t:
                        for j in range(RING):
                            split(t * RING + u0 + j, (u0 + j) % RING)
                for u in range(u0 + turns * RING, until):
                    split(u, u % RING)
                done[0] = until

            def mask(dst, src, factor):
                nc.gpsimd.tensor_scalar(dst, src, factor, None, ALU.mult).then_inc(keys_masked, 1)

            for l in range(LAYERS):
                a, out = lin[f"a_in{l}"], lin[f"a_out{l}"]
                for i in range(DIFF_H // 2):
                    splits(a.u0 + 8 + 3 * i)
                    pool.wait_ge(bank_free, a.e0 + AK + i + 1)
                    pool.wait_ge(sq_used, 8 * (NORM[f"a_in{l}"] + 1))
                    for c in range(4):
                        mask(diff_keys[4 * i + c], big[:, AK + i, :], col("diff_rows", 4 * i + c))
                splits(out.u0 + 4)
                pool.wait_ge(bank_free, a.e0 + CK + 1)
                pool.wait_ge(scores_done, DIFF_ATT[l].item0 + 48)
                for h in range(SWA_H):
                    mask(swa_keys[h], big[:, CK, :], col("swa_rows", h))
            splits(lin["b_mix_out0"].u0 + 4)
            pool.wait_ge(ret_scores, TB * RET_H)
            pool.wait_ge(rotated, 16)
            for h in range(DIL_H):
                mask(big[:, RQ + h, :], big[:, DK + h // 2, :], col("dil_rows", h % 2))
            splits(UNITS)

        @block.scalar
        def _(act):
            chain = Chain(act, act_chain)

            def weight_hi(slot, loads):
                act.wait_ge(w_loaded[slot], loads)
                nc.scalar.activation(w_hi[:, slot, :], w_raw[:, slot, :], ACT.Copy).then_inc(w_hi_ready, 1)

            def after_unit(L, t, s):
                act.wait_ge(unit_done, t * RING + L.u0 + s + 1)
                loads = (L.u0 + s + RING) // RING + 1
                weight_hi((L.u0 + s) % RING, t * 16 + 16 * loads)

            def plain_units(L):
                unit_loop(act, L.n, lambda t, s: after_unit(L, t, s))

            def square(norm, k, src):
                ge(act, sq_used, 8 * norm + k - 3)
                nc.scalar.activation(sq[:, k % 4, :], src, ACT.Square).then_inc(sq_ready, 1)

            def moving_from_x(name, gain):
                L = lin[name]
                gate = name.startswith("a_gate")
                ge(act, unit_done, L.u0 - 2 if gate else L.u0)
                for k in range(KT):
                    if gate and k in (1, 4):
                        after_unit(lin[f"a_ple_up{name[-1]}"], 0, k // 4)
                    if name in XIN:
                        act.wait_ge(x_ready, XIN[name] + k + 1)
                    else:
                        act.wait_ge(x_loaded[k // 2], 16)
                    nc.scalar.activation(mvh[:, k, :], x[:, k, :], ACT.Copy, scale=col(gain, k)).then_inc(mv_hi, 1)
                    square(NORM[name], k, x[:, k, :])
                    if name == "a_in0" and k in (0, 2, 4):
                        weight_hi(k // 2 + 1, 16)

            def ffn_in(name):
                L, f0 = lin[name], FFN[name]

                def body(t, s):
                    after_unit(L, t, s)
                    if s % 2 == 0:
                        act.wait_ge(bank_free, t * RING + L.e0 + s + 1)
                        ring = (s // 2) % 2
                        nc.scalar.activation(s1[:, ring, :], g1[:, ring, :], ACT.Silu).then_inc(silu_done, 1)

                unit_loop(act, L.n, body)

            def ffn_out(name, in_name, tail=0):
                L, f0 = lin[name], FFN[in_name]

                def cast(t, s):
                    act.wait_ge(hidden_ready, t * RING + f0 + s + 1)
                    src = big[:, bass.ds(t * RING + s, 1), :].rearrange("p a b -> p (a b)")
                    nc.scalar.activation(mvh[:, s % 4, :], src, ACT.Copy).then_inc(mv_hi, 1)

                act.wait_ge(unit_done, L.u0)
                for f in range(4):
                    cast(0, f)
                if name[0] == "a":
                    l = int(name[-1])
                    act.wait_ge(p_loaded, 16 * (l + 1))
                    nc.scalar.activation(mvh[:, 4:6, :], y[:, 0:2, :], ACT.Copy).then_inc(p_hi, 1)

                def body(t, s):
                    after_unit(L, t, s)
                    cast(t, s + 4)

                unit_loop(act, FT - 4, body)
                for f in range(FT - 4, FT - tail):
                    after_unit(L, 0, f)

            def emit(block_n, b, bank, tile0, tiles, scale):
                act.wait_ge(ot_done, block_n + 1)
                src = bank[:, 0:tiles * P].rearrange("p (a b) -> p a b", b=P)
                dst = mvh[:, tile0:tile0 + tiles, b * P:(b + 1) * P]
                if scale is None:
                    nc.scalar.activation(dst, src, ACT.Copy).then_inc(mv_hi, 1)
                else:
                    nc.scalar.activation(dst, src, ACT.Copy, scale=scale).then_inc(mv_hi, 1)

            def attention(a):
                n = len(a.pairs)
                for t in range(a.steps()):
                    if t < n:
                        q = a.pairs[t]
                        for c in range(a.comps):
                            slot, sc = 2 * (t % 2) + c, a.stat(t, c)
                            act.wait_ge(scores_scaled, a.item0 + a.comps * t + c + 1)
                            if a.comps == 1:
                                ge(act, pt_done, a.pair0 + t - 1)
                            else:
                                ge(act, probs_ready, a.probs0 + t - 1)
                            nc.scalar.activation(expo[:, slot, 0:q.nkb * P], scaled[:, slot, 0:q.nkb * P], ACT.Exp,
                                                 scale=-1.0, bias=neg_max[:, sc:sc + 1],
                                                 accum_out=row_sum[:, sc:sc + 1]).then_inc(exp_done, 1)
                    if 1 <= t <= n:
                        r = t - 1
                        act.wait_ge(pt_done, a.pair0 + r + 1)
                        ge(act, pv_done, a.pair0 + r - 1)
                        w = a.pairs[r].nkb * P
                        nc.scalar.activation(ptile[:, r % 2, 0:w], banks[4 + r % 2][:, 0:w],
                                             ACT.Copy).then_inc(pt_copied, 1)
                    b = a.due(t, 3)
                    if b is not None and a.kind == "diff":
                        act.wait_ge(pv_done, a.pair0 + (b + 1) * a.heads)
                        ge(act, onorm_ready, a.block0 + b)
                        nc.scalar.activation(osq[:, 0:384], banks[6 + b % 2][:, 0:384],
                                             ACT.Square).then_inc(osq_ready, 1)
                    if b is not None and a.kind == "swa":
                        act.wait_ge(sink_sum, a.layer * TB + b + 1)
                        nc.scalar.activation(sink_c[:, 0:a.heads], sink_c[:, 0:a.heads],
                                             ACT.Exp).then_inc(sink_exp, 1)
                    b = a.due(t, 6)
                    if b is not None:
                        emit(a.block0 + b, b, banks[6 + b % 2], a.tile0, a.tiles,
                             col(f"g_sub{a.layer}") if a.kind == "diff" else None)

            def transposed_values(key):
                tiles, n0 = VT[key]
                for i, m in enumerate(tiles):
                    act.wait_ge(vt_done, n0 + i + 1)
                    nc.scalar.activation(big[:, m, :], banks[6 + i % 2][:, :], ACT.Copy).then_inc(vt_copied, 1)

            def emit_gated(n, tile0, tiles, b):
                act.wait_ge(gated_ready, n + 1)
                src = (scr[:, 8:10, :] if tiles == 8 else gtmp[:, b % 2:b % 2 + 1, :]).rearrange(
                    "p a (b c) -> p (a b) c", c=P)
                nc.scalar.activation(mvh[:, tile0:tile0 + tiles, b * P:(b + 1) * P], src,
                                     ACT.Copy).then_inc(mv_hi, 1)

            def gla():
                act.wait_ge(bank_free, lin["b_mix_in1"].e0 + 25)
                for m in range(8):
                    chain(nc.scalar.activation(big[:, GR + m, :], big[:, GR + m, :], ACT.Silu))
                transposed_values("b1")
                for b in range(TB):
                    act.wait_ge(z_done, b + 1)
                    chain(nc.scalar.activation(scr[:, 4 + b, :], banks[b][:, :], ACT.Abs))
                for b in range(TB):
                    chain(nc.scalar.activation(scr[:, 4 + b, :], scr[:, 4 + b, :], ACT.Exp, scale=-1.0))
                for b in range(TB):
                    nc.scalar.activation(scr[:, 4 + b, :], scr[:, 4 + b, :], ACT.Ln, bias=1.0).then_inc(z_soft, 1)
                for h in range(GLA_H):
                    act.wait_ge(b_done, h + 1)
                    ge(act, b_used, h)
                    nc.scalar.activation(scr[:, 8, :], banks[4 + h % 2][:, :], ACT.Exp)
                    nc.scalar.activation(scr[:, 9, :], banks[4 + h % 2][:, :], ACT.Exp, scale=-1.0).then_inc(b_exp, 1)
                for h in range(GLA_H):
                    act.wait_ge(kt_done, h + 1)
                    nc.scalar.activation(y[:, 4 + h, :], banks[h % 2][:, :], ACT.Copy).then_inc(kt_copied, 1)
                for b in range(TB):
                    emit_gated(2 * LAYERS + TB + b, 0, 8, b)

            weight_hi(0, 16)
            act.wait_ge(cols_loaded, 16)
            for l in range(LAYERS):
                moving_from_x(f"a_in{l}", f"a_pre{l}")
                act.dma_start(tab[:, 1280:2560], dist_in).then_inc(tables, 16)
                act.dma_start(tab[:, 0:1280], gmlp_in[l]).then_inc(tables, 16)
                plain_units(lin[f"a_in{l}"])
                transposed_values(f"a{l}")
                act.wait_ge(lam_sum, l + 1)
                nc.scalar.activation(lam_s[:, 2:4], lam_s[:, 0:2], ACT.Exp).then_inc(lam_exp, 1)
                attention(DIFF_ATT[l])
                for g in range(2):
                    act.wait_ge(gated_ready, 2 * l + g + 1)
                    nc.scalar.activation(mvh[:, 3 + g, :], gtmp[:, g, :], ACT.Copy).then_inc(mv_hi, 1)
                attention(SWA_ATT[l])
                L = lin[f"a_out{l}"]
                for i in range(8):
                    after_unit(L, 0, i)
                    nc.scalar.activation(y[:, i, :], banks[BACK[i]][:, :], ACT.Copy)
                    square(NORM[f"a_out{l}"], i, banks[BACK[i]][:, :])
                moving_from_x(f"a_ffn_in{l}", f"a_pre_ffn{l}")
                act.dma_start(y[:, 0:2, :], p_in[l]).then_inc(p_loaded, 16)
                ffn_in(f"a_ffn_in{l}")
                ffn_out(f"a_ffn_out{l}", f"a_ffn_in{l}")
                act.wait_ge(p_lo, l + 1)
                for n in range(8):
                    nc.scalar.activation(y[:, n, :], banks[BACK[n]][:, :], ACT.Copy)
                    square(NORM[f"a_ffn_out{l}"], n, banks[BACK[n]][:, :])
                moving_from_x(f"a_gate{l}", f"a_gate{l}")
                L = lin[f"a_gate{l}"]
                for i in range(8):
                    after_unit(L, 0, i)
                    act.wait_ge(bank_free, L.e0 + i + 1)
                    nc.scalar.activation(s1[:, i % 2, :], g1[:, i % 2, :], ACT.Sigmoid).then_inc(gate_sig, 1)
                    if i:
                        act.wait_ge(z_ready, 8 * l + i)
                        square(NORM[f"a_ple{l}"], i - 1, y[:, i - 1, :])
                act.wait_ge(z_ready, 8 * l + 8)
                square(NORM[f"a_ple{l}"], 7, y[:, 7, :])

            for l in range(LAYERS):
                moving_from_x(f"b_pre_in{l}", f"b_pre{l}")
                if l == 0:
                    act.dma_start(tab[:, :], ret_dil_in).then_inc(tables, 16)
                    act.dma_start(y[:, 0:4, :], rotary_in).then_inc(tables, 16)
                else:
                    act.dma_start(tab[:, 0:256], gla_in).then_inc(tables, 16)
                    act.dma_start(tab[0:33, 256:768], wa2_in).then_inc(tables, 16)
                ffn_in(f"b_pre_in{l}")
                ffn_out(f"b_pre_out{l}", f"b_pre_in{l}")
                moving_from_x(f"b_mix_in{l}", f"b_mix{l}")
                plain_units(lin[f"b_mix_in{l}"])
                if l == 0:
                    act.wait_ge(bank_free, lin["b_mix_in0"].e0 + 28)
                    for h in range(RET_H):
                        chain(nc.scalar.activation(big[:, RG + h, :], big[:, RG + h, :], ACT.Silu))
                    transposed_values("b0")
                    for b in range(TB):
                        emit_gated(2 * LAYERS + b, 0, 4, b)
                    attention(DIL_ATT)
                else:
                    gla()
                plain_units(lin[f"b_mix_out{l}"])
                moving_from_x(f"b_post_in{l}", f"b_post{l}")
                ffn_in(f"b_post_in{l}")
                ffn_out(f"b_post_out{l}", f"b_post_in{l}", tail=4 if l else 0)
            for k in range(KT):
                act.wait_ge(x_ready, XR["b_post1"] + k + 1)
                square(NORM["final"], k, x[:, k, :])

        @block.vector
        def _(dve):
            chain = Chain(dve, dve_chain)

            def rsqrt(out, src, scale, n):
                v, t = sm_x[:, 0:n], sm_t[:, 0:n]
                chain(nc.vector.tensor_scalar(v, src, scale, EPS, ALU.mult, ALU.add))
                chain(nc.vector.tensor_scalar(t.bitcast(I32), v.bitcast(I32), 1, None, ALU.logical_shift_right))
                chain(nc.vector.tensor_scalar(out.bitcast(I32), t.bitcast(I32), -1.0, float(0x5F3759DF),
                                              ALU.mult, ALU.add))
                for _ in range(3):
                    chain(nc.vector.scalar_tensor_tensor(out=t, in0=out, scalar=-0.5, in1=out,
                                                         op0=ALU.mult, op1=ALU.mult))
                    chain(nc.vector.tensor_tensor(t, t, v, ALU.mult))
                    chain(nc.vector.scalar_tensor_tensor(out=out, in0=t, scalar=1.5, in1=out,
                                                         op0=ALU.add, op1=ALU.mult))

            def rstd_diag(norm):
                dve.wait_ge(sq_used, 8 * (norm + 1))
                rsqrt(sm_y[:, 0:TB], banks[STAT][:, 0:TB], 1.0 / D, TB)
                nc.vector.tensor_tensor(diag[:, :, :], ident[:, :].unsqueeze(1).broadcast_to([P, TB, P]),
                                        sm_y[:, 0:TB].unsqueeze(2).broadcast_to([P, TB, P]),
                                        ALU.mult).then_inc(diag_ready, 1)

            def rstd_spread(norm):
                dve.wait_ge(bcast_done, norm + 1)
                chain(nc.vector.tensor_copy(rstd_b[:, :], banks[BCAST][:, :]))

            def rstd(norm):
                rstd_diag(norm)
                rstd_spread(norm)

            def enter(name, gain, update=None):
                L = lin[name]
                for k in range(KT + 1):
                    if update is not None and k < KT:
                        update(k)
                    if k:
                        dve.wait_ge(mv_hi, L.m0 + k)
                        nc.vector.scalar_tensor_tensor(out=mvl[:, k - 1, :], in0=x[:, k - 1, :],
                                                       scalar=col(gain, k - 1), in1=mvh[:, k - 1, :].bitcast(F32),
                                                       op0=ALU.mult, op1=ALU.subtract).then_inc(mv_lo, 1)

            def post(gain):
                def update(k):
                    if k == 0:
                        nc.vector.scalar_tensor_tensor(out=y[:, 0, :], in0=y[:, 0, :], scalar=col(gain, 0),
                                                       in1=rstd_b[:, :], op0=ALU.mult, op1=ALU.mult
                                                       ).then_inc(dve_chain, 1)
                        chain.n += 1
                    own = chain.n
                    if k + 1 < KT:
                        nc.vector.scalar_tensor_tensor(out=y[:, k + 1, :], in0=y[:, k + 1, :],
                                                       scalar=col(gain, k + 1), in1=rstd_b[:, :],
                                                       op0=ALU.mult, op1=ALU.mult).then_inc(dve_chain, 1)
                        chain.n += 1
                    dve.wait_ge(dve_chain, own)
                    nc.vector.tensor_tensor(x[:, k, :], x[:, k, :], y[:, k, :], ALU.add).then_inc(x_ready, 1)
                return update

            def add_down(L):
                def update(k):
                    if k == 0:
                        dve.wait_ge(unit_done, L.u0 + FT)
                    nc.vector.scalar_tensor_tensor(out=x[:, k, :], in0=banks[BACK[k]][:, :], scalar=0.5,
                                                   in1=x[:, k, :], op0=ALU.mult, op1=ALU.add).then_inc(x_ready, 1)
                return update

            def add_mix(L):
                def update(k):
                    dve.wait_ge(unit_done, L.u0 + k + 1)
                    nc.vector.tensor_tensor(x[:, k, :], banks[BACK[k]][:, :], x[:, k, :],
                                            ALU.add).then_inc(x_ready, 1)
                return update

            def project(name):
                L = lin[name]

                def body(t, s):
                    dve.wait_ge(unit_done, t * RING + L.u0 + s + 1)
                    dst = big[:, bass.ds(t * RING + s, 1), :].rearrange("p a b -> p (a b)")
                    nc.vector.tensor_tensor(dst, banks[LIN[s % 4]][:, :], rstd_b[:, :], ALU.mult).then_inc(bank_free, 1)

                unit_loop(dve, L.n, body)

            def ffn_in(name):
                L, f0 = lin[name], FFN[name]

                def body(t, s):
                    ring = (s // 2) % 2
                    dve.wait_ge(unit_done, t * RING + L.u0 + s + 1)
                    dst = (g1 if s % 2 == 0 else u1)[:, ring, :]
                    nc.vector.tensor_tensor(dst, banks[LIN[s % 4]][:, :], rstd_b[:, :], ALU.mult).then_inc(bank_free, 1)
                    if s % 2:
                        dve.wait_ge(silu_done, t * 2 + f0 + s // 2 + 1)
                        dve.wait_ge(bank_free, t * RING + L.e0 + s + 1)
                        dst = big[:, bass.ds(t * 2 + s // 2, 1), :].rearrange("p a b -> p (a b)")
                        nc.vector.tensor_tensor(dst, s1[:, ring, :], u1[:, ring, :], ALU.mult).then_inc(hidden_ready, 1)

                unit_loop(dve, L.n, body)

            def ffn_out(name):
                L = lin[name]

                def body(t, s):
                    dve.wait_ge(mv_hi, t * RING + L.m0 + s + 1)
                    src = big[:, bass.ds(t * RING + s, 1), :].rearrange("p a b -> p (a b)")
                    nc.vector.tensor_tensor(mvl[:, s % 4, :], src, mvh[:, s % 4, :].bitcast(F32),
                                            ALU.subtract).then_inc(mv_lo, 1)

                for f in range(4):
                    body(0, f)
                if name[0] == "a":
                    dve.wait_ge(p_hi, int(name[-1]) + 1)
                    nc.vector.tensor_tensor(mvl[:, 4:6, :], y[:, 0:2, :], mvh[:, 4:6, :].bitcast(F32),
                                            ALU.subtract).then_inc(p_lo, 1)
                for f in range(4, 6):
                    body(0, f)
                with dve.Fori(0, (FT - 6) // RING) as t:
                    for j in range(RING):
                        body(t, 6 + j)

            def emit(m0, block_n, b, bank, tile0, tiles, scale):
                dve.wait_ge(mv_hi, m0 + 1)
                src = bank[:, 0:tiles * P].rearrange("p (a b) -> p a b", b=P)
                at = (slice(None), slice(tile0, tile0 + tiles), slice(b * P, (b + 1) * P))
                if scale is None:
                    nc.vector.tensor_tensor(mvl[at], src, mvh[at].bitcast(F32), ALU.subtract).then_inc(mv_lo, 1)
                else:
                    nc.vector.scalar_tensor_tensor(out=mvl[at], in0=src, scalar=scale, in1=mvh[at].bitcast(F32),
                                                   op0=ALU.mult, op1=ALU.subtract).then_inc(mv_lo, 1)

            def attention(a, m0):
                n, H = len(a.pairs), a.heads
                for t in range(a.steps()):
                    if a.kind == "diff" and t < 13:
                        gmlp_norm(t)
                    if a.kind == "diff" and t == n + 3:
                        gmlp_gate(a.layer)
                    if t < n:
                        q = a.pairs[t]
                        for c in range(a.comps):
                            i, slot, sc = a.item0 + a.comps * t + c, 2 * (t % 2) + c, a.stat(t, c)
                            w = q.nkb * P
                            dve.wait_ge(scores_done, i + 1)
                            ge(dve, exp_done, a.item0 + a.comps * (t - 1))
                            nc.vector.tensor_tensor_reduce(out=scaled[:, slot, 0:w], in0=banks[slot][:, 0:w],
                                                           in1=q.bias, scale=-q.scale, scalar=q.first,
                                                           op0=ALU.add, op1=ALU.min,
                                                           accum_out=neg_max[:, sc:sc + 1]).then_inc(scores_scaled, 1)
                    if a.comps == 2 and 1 <= t <= n:
                        r = t - 1
                        s0, sl, ring = 2 * (r % 2), a.stat(r, 0), r % 2
                        dve.wait_ge(exp_done, a.item0 + 2 * t)
                        ge(dve, pt_done, a.pair0 + r - 1)
                        chain(nc.vector.reciprocal(inv[:, 0:2], row_sum[:, sl:sl + 2]))
                        nc.vector.tensor_scalar(inv[:, 2:3], inv[:, 1:2], lam_s[:, 4:5], None, ALU.mult)
                        chain(nc.vector.tensor_scalar(comb[:, ring, :], expo[:, s0, :], inv[:, 0:1], None, ALU.mult))
                        nc.vector.scalar_tensor_tensor(out=comb[:, ring, :], in0=expo[:, s0 + 1, :],
                                                       scalar=inv[:, 2:3], in1=comb[:, ring, :],
                                                       op0=ALU.mult, op1=ALU.add).then_inc(probs_ready, 1)
                    b = a.due(t, 2)
                    if b is not None and a.kind == "swa":
                        chain(nc.vector.tensor_copy(sink_c[:, 0:8], neg_max[:, 8 * (b % 2):8 * (b % 2) + 8]))
                        nc.vector.tensor_tensor(sink_c[:, 0:H], sink_c[:, 0:H], col(f"sinks{a.layer}", 0, H),
                                                ALU.add).then_inc(sink_sum, 1)
                    b = a.due(t, 3)
                    if b is not None:
                        o = banks[6 + b % 2][:, 0:64 * H].rearrange("p (h d) -> p h d", d=64)
                        on = onorm[:, b % 2, 0:64 * H].rearrange("p (h d) -> p h d", d=64)
                        if a.kind == "diff":
                            dve.wait_ge(osq_ready, a.layer * TB + b + 1)
                            sums = sm_t[:, 8:8 + H]
                            chain(nc.vector.reduce_sum(sums, osq[:, 0:384].rearrange("p (h d) -> p h d", d=64),
                                                       AX.X))
                            rsqrt(sm_y[:, 0:H], sums, 1.0 / 64, H)
                        else:
                            dve.wait_ge(pv_done, a.pair0 + (b + 1) * H)
                            ls = row_sum[:, 8 * (b % 2):8 * (b % 2) + H]
                            dve.wait_ge(exp_done, a.item0 + (b + 1) * H)
                            if a.kind == "swa":
                                dve.wait_ge(sink_exp, a.layer * TB + b + 1)
                                chain(nc.vector.tensor_tensor(sink_c[:, 0:H], sink_c[:, 0:H], ls, ALU.add))
                                ls = sink_c[:, 0:H]
                            chain(nc.vector.reciprocal(sm_y[:, 0:H], ls))
                        ge(dve, ot_done, a.block0 + b - 1)
                        nc.vector.tensor_tensor(on, o, sm_y[:, 0:H].unsqueeze(2).broadcast_to([P, H, 64]),
                                                ALU.mult).then_inc(onorm_ready, 1)
                    b = a.due(t, 6)
                    if b is not None:
                        emit(m0 + b, a.block0 + b, b, banks[6 + b % 2], a.tile0, a.tiles,
                             col(f"g_sub{a.layer}") if a.kind == "diff" else None)

            def lam(l):
                init = 0.8 - 0.6 * math.exp(-0.3 * l)
                v = col(f"lam{l}", 0, 128).rearrange("p (a b c) -> p a b c", b=2, c=32)
                prod = onorm[:, 0, 0:64].rearrange("p (a c) -> p a c", c=32)
                chain(nc.vector.tensor_tensor(prod, v[:, :, 0, :], v[:, :, 1, :], ALU.mult))
                nc.vector.reduce_sum(lam_s[:, 0:2], prod, AX.X).then_inc(lam_sum, 1)
                dve.wait_ge(lam_exp, l + 1)
                chain(nc.vector.tensor_tensor(lam_s[:, 5:6], lam_s[:, 3:4], lam_s[:, 2:3], ALU.subtract))
                chain(nc.vector.tensor_scalar(lam_s[:, 4:5], lam_s[:, 5:6], -init, None, ALU.add))
                chain(nc.vector.tensor_scalar(neg_sinks, col(f"sinks{l}", 0, SWA_H), -1.0, None, ALU.mult))
                chain(nc.vector.tensor_scalar(col(f"g_sub{l}"), col(f"g_sub{l}"), 1.0 - init, None, ALU.mult))

            def gmlp_norm(i):
                if i < 4:
                    for m in range(2):
                        last = nc.vector.bn_stats(stats6[:, 6 * m:6 * m + 6], tok(BV + m, i, 0, P))
                    chain(last)
                    chain(nc.vector.bn_aggr(mean_var[:, 2 * i:2 * i + 2], stats6[:, 0:12]))
                elif i == 4:
                    rsqrt(sm_y[:, 0:TB], mean_var[:, 1:8:2], 1.0, TB)
                elif i < 9:
                    b = i - 5
                    vn = big[:, BV:BV + 2, b * P:(b + 1) * P]
                    chain(nc.vector.tensor_scalar(vn, vn, mean_var[:, 2 * b:2 * b + 1], sm_y[:, b:b + 1],
                                                  ALU.subtract, ALU.mult))
                else:
                    m = (i - 9) % 2
                    row, op = (tab[:, 0:256], ALU.mult) if i < 11 else (tab[:, 256:512], ALU.add)
                    vn = big[:, BV + m, :].rearrange("p (b c) -> p b c", c=P)
                    last = nc.vector.tensor_tensor(vn, vn, row[:, m * P:(m + 1) * P].unsqueeze(1).broadcast_to(
                        [P, TB, P]), op)
                    if i == 12:
                        last.then_inc(vn_ready, 1)
                    else:
                        chain(last)

            def gmlp_gate(l):
                for g in range(2):
                    dve.wait_ge(mixed_done, 2 * l + g + 1)
                    t = gtmp[:, g, :].rearrange("p (b c) -> p b c", c=P)
                    chain(nc.vector.tensor_tensor(t, banks[1 + 2 * g][:, :].rearrange("p (b c) -> p b c", c=P),
                                                  tab[:, 1024 + g * P:1024 + (g + 1) * P].unsqueeze(1).broadcast_to(
                                                      [P, TB, P]), ALU.add))
                    nc.vector.tensor_tensor(gtmp[:, g, :], gtmp[:, g, :], big[:, BU + g, :],
                                            ALU.mult).then_inc(gated_ready, 1)

            def gmlp_low(m0):
                for g in range(2):
                    dve.wait_ge(mv_hi, m0 + g + 1)
                    nc.vector.tensor_tensor(mvl[:, 3 + g, :], gtmp[:, g, :], mvh[:, 3 + g, :].bitcast(F32),
                                            ALU.subtract).then_inc(mv_lo, 1)

            def head_norm(src, dst, heads, width):
                for h in range(heads):
                    chain(nc.vector.bn_stats(stats6[:, 6 * h:6 * h + 6], src(h)))
                for h in range(heads):
                    chain(nc.vector.bn_aggr(mean_var[:, 2 * h:2 * h + 2], stats6[:, 6 * h:6 * h + 6]))
                rsqrt(sm_y[:, 0:heads], mean_var[:, 1:2 * heads:2], 1.0, heads)
                for h in range(heads):
                    last = nc.vector.tensor_scalar(dst(h), src(h), mean_var[:, 2 * h:2 * h + 1], sm_y[:, h:h + 1],
                                                   ALU.subtract, ALU.mult)
                last.then_inc(onorm_ready, 1)

            def rotary():
                tiles = [(RQ + i, 0) for i in range(8)] + [(DQ + i, 1) for i in range(8)]
                for i, (m, kind) in enumerate(tiles):
                    dve.wait_ge(rot_done, i + 1)
                    chain(nc.vector.tensor_tensor(scr[:, i % 2, :], banks[i % 4][:, :], y[:, 2 * kind + 1, :], ALU.mult))
                    chain(nc.vector.tensor_tensor(big[:, m, :], big[:, m, :], y[:, 2 * kind, :], ALU.mult))
                    nc.vector.tensor_tensor(big[:, m, :], big[:, m, :], scr[:, i % 2, :], ALU.add).then_inc(rotated, 1)

            def retention(m0):
                i = 0
                for h in range(RET_H):
                    for jt in range(TB):
                        w = S - jt * P
                        dve.wait_ge(ret_scores, i + 1)
                        if h >= 2:
                            dve.wait_ge(ret_pv, h - 1)
                        nc.vector.tensor_tensor(y[:, 4 * (h % 2) + jt, 0:w], banks[i % 4][:, 0:w],
                                                tab[:, h * S:h * S + w], ALU.mult).then_inc(ret_decayed, 1)
                        i += 1
                for b in range(TB + 1):
                    if b < TB:
                        dve.wait_ge(ret_pv, RET_H)
                        bank = banks[4 + b]
                        ge(dve, ot_done, RET_BLOCK0 + b - 1 if b >= 2 else 0)
                        head_norm(lambda h: bank[:, h * P:(h + 1) * P],
                                  lambda h: onorm[:, b % 2, h * P:(h + 1) * P], RET_H, P)
                    if b:
                        gated(b - 1, m0, [banks[4 + b - 1]], RG, gtmp[:, (b - 1) % 2:(b - 1) % 2 + 1, :], RET_BLOCK0,
                              2 * LAYERS)

            def gated(b, m0, src, gate, dst, block0, g0):
                n = 4 * len(src)
                dve.wait_ge(ot_done, block0 + b + 1)
                for i, bank in enumerate(src):
                    if i + 1 == len(src) and i:
                        chain(last)
                    last = nc.vector.tensor_tensor(dst[:, i, :].rearrange("p (a c) -> p a c", c=P),
                                                   bank[:, :].rearrange("p (a c) -> p a c", c=P),
                                                   big[:, gate + 4 * i:gate + 4 * i + 4, b * P:(b + 1) * P], ALU.mult)
                last.then_inc(gated_ready, 1)
                dve.wait_ge(mv_hi, m0 + b + 1)
                at = (slice(None), slice(0, n), slice(b * P, (b + 1) * P))
                nc.vector.tensor_tensor(mvl[at], dst.rearrange("p a (b c) -> p (a b) c", c=P),
                                        mvh[at].bitcast(F32), ALU.subtract).then_inc(mv_lo, 1)

            def gla(m0):
                nc.vector.memset(big[32:33, GA, :], 1.0).then_inc(alow_ready, 1)
                for b in range(TB):
                    dve.wait_ge(z_soft, b + 1)
                    nc.vector.scalar_tensor_tensor(out=scr[:, b, :], in0=banks[b][:, :], scalar=0.0,
                                                   in1=scr[:, 4 + b, :], op0=ALU.min,
                                                   op1=ALU.subtract).then_inc(log_a, 1)
                for h in range(GLA_H):
                    q, k, dec = big[:, GQ + h, :], big[:, GK + h, :], decay[:, 8 * h:8 * h + 8]
                    dve.wait_ge(b_exp, h + 1)
                    chain(nc.vector.tensor_copy(dec, scr[:, 8, GLA_CHUNK - 1:S:GLA_CHUNK]))
                    chain(nc.vector.scalar_tensor_tensor(out=q, in0=q, scalar=128 ** -0.5, in1=scr[:, 8, :],
                                                         op0=ALU.mult, op1=ALU.mult))
                    nc.vector.tensor_tensor(k, k, scr[:, 9, :], ALU.mult).then_inc(b_used, 1)
                    dve.wait_ge(b_used, h + 1)
                    nc.vector.tensor_tensor(y[:, h, :].rearrange("p (n c) -> p n c", c=GLA_CHUNK),
                                            k.rearrange("p (n c) -> p n c", c=GLA_CHUNK),
                                            dec.unsqueeze(2).broadcast_to([P, 8, GLA_CHUNK]),
                                            ALU.mult).then_inc(kdec_ready, 1)
                for h in range(GLA_H):
                    dve.wait_ge(gsc_done, h + 1)
                    nc.vector.tensor_tensor(scr[:, h, :].rearrange("p (b c) -> p b c", c=P),
                                            banks[2 + h % 2][:, :].rearrange("p (b c) -> p b c", c=P),
                                            tab[:, 128:256].unsqueeze(1).broadcast_to([P, TB, P]),
                                            ALU.mult).then_inc(gsc_masked, 1)
                for b in range(TB):
                    for n in (2 * b, 2 * b + 1):
                        if n == 7:
                            break
                        for h in range(GLA_H):
                            dve.wait_ge(kv_done, 4 * n + 2 * (h // 2) + 2)
                            kv = banks[2 * (n % 2) + h // 2][:, (h % 2) * GLA_DV:(h % 2 + 1) * GLA_DV]
                            if n == 0:
                                nc.vector.tensor_copy(state(1, h), kv).then_inc(state_ready, 1)
                                continue
                            dve.wait_ge(state_ready, 4 * (n - 1) + h + 1)
                            if n >= 2 or n == 1:
                                ge(dve, gla_o, 4 * ((n - 1) // 2) + h + 1 if n >= 2 else 0)
                            nc.vector.scalar_tensor_tensor(out=state(n + 1, h), in0=state(n, h),
                                                           scalar=decay[:, 8 * h + n:8 * h + n + 1], in1=kv,
                                                           op0=ALU.mult, op1=ALU.add).then_inc(state_ready, 1)
                    dve.wait_ge(gla_o, 4 * (b + 1))
                    ob = [banks[4 + 2 * (b % 2)], banks[5 + 2 * (b % 2)]]
                    head_norm(lambda h: ob[h // 2][:, (h % 2) * GLA_DV:(h % 2 + 1) * GLA_DV],
                              lambda h: scr[:, 4 + 2 * (b % 2) + h // 2, (h % 2) * GLA_DV:(h % 2 + 1) * GLA_DV],
                              GLA_H, GLA_DV)
                    if b:
                        gated(b - 1, m0, [banks[4 + 2 * ((b - 1) % 2)], banks[5 + 2 * ((b - 1) % 2)]], GR,
                              scr[:, 8:10, :], GLA_BLOCK0, 2 * LAYERS + TB)
                dve.wait_ge(mv_lo, m0 + TB - 1)
                gated(TB - 1, m0, [banks[6], banks[7]], GR, scr[:, 8:10, :], GLA_BLOCK0, 2 * LAYERS + TB)

            nc.vector.memset(ones[:, :], 1.0).then_inc(ones_set, 1)
            nc.vector.memset(small[:, :], 0.0).then_inc(bank_free, len(LIN))
            update = None
            n_tables = 0
            for l in range(LAYERS):
                enter(f"a_in{l}", f"a_pre{l}", update)
                dve.wait_ge(consts, 32)
                rstd(NORM[f"a_in{l}"])
                project(f"a_in{l}")
                lam(l)
                m0 = lin[f"a_out{l}"].m0
                dve.wait_ge(vt_copied, 6 * (l + 1))
                dve.wait_ge(tables, 16 * (2 * l + 2))
                attention(DIFF_ATT[l], m0)
                gmlp_low(m0 + TB)
                attention(SWA_ATT[l], m0 + TB + 2)
                rstd(NORM[f"a_out{l}"])
                enter(f"a_ffn_in{l}", f"a_pre_ffn{l}", post(f"a_post{l}"))
                rstd(NORM[f"a_ffn_in{l}"])
                ffn_in(f"a_ffn_in{l}")
                ffn_out(f"a_ffn_out{l}")
                rstd_diag(NORM[f"a_ffn_out{l}"])
                up = lin[f"a_ple_up{l}"]
                for n in range(4):
                    if n == 0:
                        dve.wait_ge(unit_done, up.u0 + 1)
                    nc.vector.tensor_copy(big[:, n, :], banks[LIN[n]][:, :]).then_inc(bank_free, 1)
                rstd_spread(NORM[f"a_ffn_out{l}"])
                add = post(f"a_post_ffn{l}")

                def update(k):
                    add(k)
                    if k == 1:
                        dve.wait_ge(unit_done, up.u0 + 2)
                        for n in range(4):
                            nc.vector.tensor_copy(big[:, 4 + n, :], banks[LIN[n]][:, :]).then_inc(bank_free, 1)

                enter(f"a_gate{l}", f"a_gate{l}", update)
                rstd(NORM[f"a_gate{l}"])
                L = lin[f"a_gate{l}"]
                for i in range(9):
                    if i < 8:
                        dve.wait_ge(unit_done, L.u0 + i + 1)
                        nc.vector.tensor_tensor(g1[:, i % 2, :], banks[LIN[i % 4]][:, :], rstd_b[:, :],
                                                ALU.mult).then_inc(bank_free, 1)
                    if i:
                        dve.wait_ge(gate_sig, 8 * l + i)
                        nc.vector.tensor_tensor(y[:, i - 1, :], s1[:, (i - 1) % 2, :], big[:, i - 1, :],
                                                ALU.mult).then_inc(z_ready, 1)
                rstd(NORM[f"a_ple{l}"])
                update = post(f"a_ple{l}")

            for l in range(LAYERS):
                enter(f"b_pre_in{l}", f"b_pre{l}", update)
                rstd(NORM[f"b_pre_in{l}"])
                ffn_in(f"b_pre_in{l}")
                ffn_out(f"b_pre_out{l}")
                enter(f"b_mix_in{l}", f"b_mix{l}", add_down(lin[f"b_pre_out{l}"]))
                rstd(NORM[f"b_mix_in{l}"])
                project(f"b_mix_in{l}")
                m0 = lin[f"b_mix_out{l}"].m0
                dve.wait_ge(tables, 16 * (6 + 2 * l))
                if l == 0:
                    dve.wait_ge(bank_free, lin["b_mix_in0"].e0 + 28)
                    rotary()
                    retention(m0)
                    dve.wait_ge(vt_copied, 20)
                    attention(DIL_ATT, m0 + TB)
                else:
                    dve.wait_ge(bank_free, lin["b_mix_in1"].e0 + 25)
                    gla(m0)
                L = lin[f"b_mix_out{l}"]
                enter(f"b_post_in{l}", f"b_post{l}", add_mix(L))
                rstd(NORM[f"b_post_in{l}"])
                ffn_in(f"b_post_in{l}")
                ffn_out(f"b_post_out{l}")
                update = add_down(lin[f"b_post_out{l}"])
            for k in range(KT):
                update(k)
            rstd(NORM["final"])
            for k in range(KT):
                nc.vector.scalar_tensor_tensor(out=y[:, k, :], in0=x[:, k, :], scalar=col("final", k),
                                               in1=rstd_b[:, :], op0=ALU.mult, op1=ALU.mult).then_inc(y_ready, 1)

        @block.tensor
        def _(pe):
            def three(bank, slot, tile, k, first, last):
                hi, lo = w_hi[:, slot, tile * P:(tile + 1) * P], w_lo[:, slot, tile * P:(tile + 1) * P]
                nc.tensor.matmul(bank[:, :], hi, mvh[:, k, :], start=first, stop=False)
                nc.tensor.matmul(bank[:, :], hi, mvl[:, k, :], start=False, stop=False)
                return nc.tensor.matmul(bank[:, :], lo, mvh[:, k, :], start=False, stop=last)

            def wide(name):
                L = lin[name]
                back = [f"a_out{l}" for l in range(LAYERS)] + [f"b_mix_out{l}" for l in range(LAYERS)]

                def body(t, s):
                    slot = (L.u0 + s) % RING
                    pe.wait_ge(w_lo_ready, t * RING + L.u0 + s + 1)
                    bank = banks[BACK[s] if name in back else LIN[s % 4]]
                    if name not in back:
                        pe.wait_ge(bank_free, t * RING + L.e0 + s - 3)
                    for k in range(8):
                        last = three(bank, slot, k, k, k == 0, k == 7)
                    last.then_inc(unit_done, 1)

                return L, body

            def sum_squares(norm, k):
                pe.wait_ge(sq_ready, 8 * norm + k + 1)
                for b in range(TB):
                    last = nc.tensor.matmul(banks[STAT][:, b:b + 1], sq[:, k % 4, b * P:(b + 1) * P],
                                            ones[:, 0:1], start=(k == 0 and b == 0), stop=(k == 7),
                                            skip_group_check=True)
                last.then_inc(sq_used, 1)

            def stats(norm):
                pe.wait_ge(sq_ready, 8 * norm + 2)
                for k in range(KT):
                    sum_squares(norm, k)

            def spread(norm):
                pe.wait_ge(diag_ready, norm + 1)
                nc.tensor.matmul(banks[BCAST][:, :], ones[:, :], diag[:, :, :].rearrange("p a b -> p (a b)"),
                                 start=True, stop=True).then_inc(bcast_done, 1)

            def from_x(name, norm):
                L, body = wide(name)

                def product(j, k):
                    last = three(banks[LIN[j]], (L.u0 + j) % RING, k, k, k == 0, k == KT - 1)
                    if k == KT - 1:
                        last.then_inc(unit_done, 1)

                for k in range(KT - 3):
                    pe.wait_ge(mv_lo, L.m0 + k + 1)
                    for j in range(min(k, RING)):
                        product(j, k)
                    if k < RING:
                        pe.wait_ge(w_lo_ready, L.u0 + k + 1)
                        pe.wait_ge(bank_free, L.e0 + k - 3)
                        for i in range(k + 1):
                            product(k, i)
                    sum_squares(norm, k)
                for j in range(RING):
                    for k in range(KT - 3, KT):
                        if j == 0:
                            pe.wait_ge(mv_lo, L.m0 + k + 1)
                        product(j, k)
                        if j == 0:
                            sum_squares(norm, k)
                    if j == 2:
                        spread(norm)
                rest(L, body, RING)

            def rest(L, body, done):
                head = (L.n - done) % RING
                for i in range(done, done + head):
                    body(0, i)
                turns = (L.n - done - head) // RING
                if turns:
                    with pe.Fori(0, turns) as t:
                        for j in range(RING):
                            body(t, done + head + j)

            def from_cat(name):
                L, body = wide(name)
                pe.wait_ge(mv_lo, L.m0 + L.moving)
                return L, body

            def down(name):
                L = lin[name]

                def body(t, s, first=False):
                    slot = (L.u0 + s) % RING
                    pe.wait_ge(w_lo_ready, t * RING + L.u0 + s + 1)
                    pe.wait_ge(mv_lo, t * RING + L.m0 + s + 1)
                    for n in range(8):
                        if first and BACK[n] in LIN:
                            pe.wait_ge(bank_free, L.e0 - 3 + LIN.index(BACK[n]))
                        last = three(banks[BACK[n]], slot, n, s % 4, first, s == FT - 1)
                    last.then_inc(unit_done, 1)

                body(0, 0, True)
                body(0, 1)
                with pe.Fori(0, (FT - 6) // RING) as t:
                    for j in range(RING):
                        body(t, 2 + j)
                for f in range(FT - 4, FT):
                    body(0, f)

            def ple_unit(l, n0):
                L = lin[f"a_ple_up{l}"]
                i = n0 // 4
                pe.wait_ge(w_lo_ready, L.u0 + i + 1)
                pe.wait_ge(p_lo, l + 1)
                for n in range(4):
                    pe.wait_ge(bank_free, L.e0 + n0 + n - 3)
                    for k in range(2):
                        last = three(banks[LIN[n]], (L.u0 + i) % RING, 2 * n + k, 4 + k, k == 0, k == 1)
                last.then_inc(unit_done, 1)

            def transpose_values(key):
                tiles, n0 = VT[key]
                for i, m in enumerate(tiles):
                    ge(pe, vt_copied, n0 + i - 1)
                    for b in range(TB):
                        last = nc.tensor.transpose(banks[6 + i % 2][:, b * P:(b + 1) * P],
                                                   big[:, m, b * P:(b + 1) * P], ident[:, :])
                    last.then_inc(vt_done, 1)

            def attention(a):
                n, H = len(a.pairs), a.heads

                def scores(t):
                    q = a.pairs[t]
                    ge(pe, scores_scaled, a.item0 + a.comps * (t - 1))
                    if q.qb == 0:
                        pe.wait_ge(keys_masked, a.keys0 + q.masked)
                    for c, (lhs, rhs) in enumerate(q.parts):
                        nc.tensor.matmul(banks[2 * (t % 2) + c][:, 0:q.nkb * P], lhs, rhs, start=True,
                                         stop=True).then_inc(scores_done, 1)

                scores(0)
                for t in range(a.steps()):
                    if t + 1 < n:
                        scores(t + 1)
                    if 1 <= t <= n:
                        r = t - 1
                        q = a.pairs[r]
                        if a.comps == 2:
                            pe.wait_ge(probs_ready, a.probs0 + r + 1)
                            src = comb[:, r % 2, :]
                        else:
                            pe.wait_ge(exp_done, a.item0 + r + 1)
                            src = expo[:, 2 * (r % 2), :]
                        ge(pe, pt_copied, a.pair0 + r - 1)
                        for kb in range(q.nkb):
                            last = nc.tensor.transpose(banks[4 + r % 2][:, kb * P:(kb + 1) * P],
                                                       src[:, kb * P:(kb + 1) * P], ident[:, :])
                        last.then_inc(pt_done, 1)
                    if 2 <= t <= n + 1:
                        r = t - 2
                        q = a.pairs[r]
                        pe.wait_ge(pt_copied, a.pair0 + r + 1)
                        if q.h == 0 and q.qb >= 2:
                            pe.wait_ge(mv_lo, a.m0 + q.qb - 1)
                        elif q.h == 0 and a.kind == "swa":
                            pe.wait_ge(mv_lo, a.m0 - 2 - TB + q.qb + 3)
                        for kb in range(q.nkb):
                            last = nc.tensor.matmul(banks[6 + q.qb % 2][:, q.h * 64:(q.h + 1) * 64],
                                                    ptile[:, r % 2, kb * P:(kb + 1) * P], q.v(q.kb0 + kb),
                                                    start=(kb == 0), stop=(kb == q.nkb - 1))
                        last.then_inc(pv_done, 1)
                    if a.kind == "diff" and t == n + 1:
                        gmlp(a.layer)
                    b = a.due(t, 5)
                    if b is not None:
                        transpose_out(a.block0 + b, [banks[6 + b % 2]], a.tiles, onorm[:, b % 2:b % 2 + 1, :])

            def transpose_out(block_n, dst, tiles, src):
                pe.wait_ge(onorm_ready, block_n + 1)
                for m in range(tiles):
                    last = nc.tensor.transpose(dst[m // 4][:, (m % 4) * P:(m % 4 + 1) * P],
                                               src[:, m // 4, (m % 4) * P:(m % 4 + 1) * P], ident[:, :])
                last.then_inc(ot_done, 1)

            def gmlp(l):
                pe.wait_ge(tables, 16 * (2 * l + 2))
                pe.wait_ge(vn_ready, l + 1)
                for g in range(4):
                    p0 = 64 * (g % 2)
                    for b in range(TB):
                        last = nc.tensor.matmul(banks[1 + 2 * (g // 2)][p0:p0 + 64, b * P:(b + 1) * P],
                                                tok(BV + g // 2, b, p0, 64), tab[:, 512 + g * P:512 + (g + 1) * P],
                                                start=True, stop=True)
                    if g % 2:
                        last.then_inc(mixed_done, 1)

            def rotary():
                tiles = [(RQ + i, 0) for i in range(8)] + [(DQ + i, 1) for i in range(8)]
                for i, (m, kind) in enumerate(tiles):
                    ge(pe, rotated, i - 3)
                    nc.tensor.matmul(banks[i % 4][:, :], rot[:, kind, :], big[:, m, :], start=True,
                                     stop=True).then_inc(rot_done, 1)

            def retention():
                pe.wait_ge(rotated, 16)
                for h in range(RET_H + 1):
                    if h < RET_H:
                        for jt in range(TB):
                            i = TB * h + jt
                            ge(pe, ret_decayed, i - 3)
                            nc.tensor.matmul(banks[i % 4][:, 0:S - jt * P], big[:, RK + h, jt * P:(jt + 1) * P],
                                             big[:, RQ + h, jt * P:S], start=True, stop=True).then_inc(ret_scores, 1)
                    if h:
                        r = h - 1
                        pe.wait_ge(ret_decayed, TB * (r + 1))
                        for b in range(TB):
                            for jt in range(b + 1):
                                last = nc.tensor.matmul(banks[4 + b][:, r * P:(r + 1) * P],
                                                        y[:, 4 * (r % 2) + jt, (b - jt) * P:(b - jt + 1) * P],
                                                        tok(RV + r, jt, 0, P), start=(jt == 0), stop=(jt == b))
                        last.then_inc(ret_pv, 1)
                for b in range(TB):
                    transpose_out(RET_BLOCK0 + b, [banks[4 + b]], 4, onorm[:, b % 2:b % 2 + 1, :])

            def gla():
                pe.wait_ge(alow_ready, 1)
                for b in range(TB):
                    nc.tensor.matmul(banks[b][:, :], big[0:33, GA, b * P:(b + 1) * P], tab[0:33, 256:768],
                                     start=True, stop=True).then_inc(z_done, 1)
                pe.wait_ge(log_a, TB)
                for h in range(GLA_H):
                    ge(pe, b_exp, h - 1)
                    for b in range(TB):
                        last = nc.tensor.matmul(banks[4 + h % 2][:, b * P:(b + 1) * P],
                                                scr[:, b, h * P:(h + 1) * P], tab[:, 0:128], start=True, stop=True)
                    last.then_inc(b_done, 1)
                for h in range(GLA_H):
                    pe.wait_ge(kdec_ready, h + 1)
                    ge(pe, kt_copied, h - 1)
                    for b in range(TB):
                        last = nc.tensor.transpose(banks[h % 2][:, b * P:(b + 1) * P], y[:, h, b * P:(b + 1) * P],
                                                   ident[:, :])
                    last.then_inc(kt_done, 1)
                    ge(pe, gsc_masked, h - 1)
                    for b in range(TB):
                        last = nc.tensor.matmul(banks[2 + h % 2][:, b * P:(b + 1) * P],
                                                big[:, GK + h, b * P:(b + 1) * P], big[:, GQ + h, b * P:(b + 1) * P],
                                                start=True, stop=True)
                    last.then_inc(gsc_done, 1)
                pe.wait_ge(kt_copied, GLA_H)
                pe.wait_ge(gsc_masked, GLA_H)
                for b in range(TB + 1):
                    if b < TB:
                        for n in (2 * b, 2 * b + 1):
                            if n == 7:
                                break
                            p0 = 64 * (n % 2)
                            ge(pe, state_ready, 4 * (n - 1))
                            for h in range(GLA_H):
                                nc.tensor.matmul(banks[2 * (n % 2) + h // 2][:, (h % 2) * GLA_DV:(h % 2 + 1) * GLA_DV],
                                                 y[p0:p0 + 64, 4 + h, b * P:(b + 1) * P],
                                                 big[p0:p0 + 64, GV + 2 * h:GV + 2 * h + 2, b * P:(b + 1) * P],
                                                 start=True, stop=True).then_inc(kv_done, 1)
                        if b >= 2:
                            pe.wait_ge(gated_ready, 2 * LAYERS + TB + b - 1)
                        for h in range(GLA_H):
                            bank = banks[4 + 2 * (b % 2) + h // 2]
                            c0 = (h % 2) * GLA_DV
                            last = nc.tensor.matmul(bank[:, c0:c0 + GLA_DV], scr[:, h, b * P:(b + 1) * P],
                                                    big[:, GV + 2 * h:GV + 2 * h + 2, b * P:(b + 1) * P],
                                                    start=True, stop=False, skip_group_check=True)
                            for n in (2 * b, 2 * b + 1):
                                if n == 0:
                                    continue
                                pe.wait_ge(state_ready, 4 * (n - 1) + h + 1)
                                p0 = 64 * (n % 2)
                                last = nc.tensor.matmul(bank[p0:p0 + 64, c0:c0 + GLA_DV],
                                                        big[:, GQ + h, n * 64:(n + 1) * 64], state(n, h),
                                                        start=False, stop=True, skip_group_check=True)
                            last.then_inc(gla_o, 1)
                    if b:
                        r = b - 1
                        transpose_out(GLA_BLOCK0 + r, [banks[4 + 2 * (r % 2)], banks[5 + 2 * (r % 2)]], 8,
                                      scr[:, 4 + 2 * (r % 2):6 + 2 * (r % 2), :])

            pe.wait_ge(ones_set, 1)
            for l in range(LAYERS):
                from_x(f"a_in{l}", NORM[f"a_in{l}"])
                pe.wait_ge(bank_free, lin[f"a_in{l}"].e0 + 18)
                pe.wait_ge(consts, 32)
                transpose_values(f"a{l}")
                pe.wait_ge(vt_copied, 6 * (l + 1))
                attention(DIFF_ATT[l])
                attention(SWA_ATT[l])
                L, body = from_cat(f"a_out{l}")
                for i in range(8):
                    body(0, i)
                stats(NORM[f"a_out{l}"])
                spread(NORM[f"a_out{l}"])
                from_x(f"a_ffn_in{l}", NORM[f"a_ffn_in{l}"])
                down(f"a_ffn_out{l}")
                stats(NORM[f"a_ffn_out{l}"])
                ple_unit(l, 0)
                spread(NORM[f"a_ffn_out{l}"])
                ple_unit(l, 4)
                from_x(f"a_gate{l}", NORM[f"a_gate{l}"])
                stats(NORM[f"a_ple{l}"])
                spread(NORM[f"a_ple{l}"])
            for l in range(LAYERS):
                from_x(f"b_pre_in{l}", NORM[f"b_pre_in{l}"])
                down(f"b_pre_out{l}")
                from_x(f"b_mix_in{l}", NORM[f"b_mix_in{l}"])
                pe.wait_ge(bank_free, lin[f"b_mix_in{l}"].e0 + lin[f"b_mix_in{l}"].n)
                pe.wait_ge(tables, 16 * (6 + 2 * l))
                if l == 0:
                    transpose_values("b0")
                    rotary()
                    pe.wait_ge(vt_copied, 20)
                    retention()
                    pe.wait_ge(gated_ready, 2 * LAYERS + TB)
                    attention(DIL_ATT)
                else:
                    transpose_values("b1")
                    pe.wait_ge(vt_copied, 28)
                    gla()
                L, body = from_cat(f"b_mix_out{l}")
                for i in range(8):
                    body(0, i)
                from_x(f"b_post_in{l}", NORM[f"b_post_in{l}"])
                down(f"b_post_out{l}")
            stats(NORM["final"])
            spread(NORM["final"])


def tiles_of(w):
    k, n = w.shape
    return w.reshape(k // P, P, n // P, P).transpose(2, 1, 0, 3).reshape(n // P, P, k)


def weight_units(i):
    out = []

    def ffn(gate, up, down):
        g, u = tiles_of(gate), tiles_of(up)
        out.append(np.stack([g, u], axis=1).reshape(-1, P, UNIT))
        out.append(down.reshape(FT, P, D))

    swa0 = 2304 - 256 - 384
    order = [h for t in range(3) for h in (t, 3 + t)]
    for l in range(LAYERS):
        w = i["w_in"][l]
        q = w[:, swa0:swa0 + 384].reshape(D, 6, 64)[:, order].reshape(D, 384)
        out.append(tiles_of(np.concatenate([w[:, :swa0], q, w[:, swa0 + 384:]], axis=1)))
        out.append(tiles_of(i["w_out"][l]))
        ffn(i["w_ffn_in"][l][:, :FT * P], i["w_ffn_in"][l][:, FT * P:], i["w_ffn_out"][l])
        up = tiles_of(i["w_ple_up"][l])
        out.append(up.reshape(2, 4, P, 256).transpose(0, 2, 1, 3).reshape(2, P, UNIT))
        out.append(tiles_of(i["w_ple_gate"][l]))
    for l in range(LAYERS):
        ffn(i["ffn_pre_w_gate_2"][l], i["ffn_pre_w_up_2"][l], i["ffn_pre_w_down_2"][l])
        if l == 0:
            out.append(tiles_of(i["ab_w_in_2"][0]))
            out.append(tiles_of(i["ab_w_out_2"][0]))
        else:
            w = i["gla_w_in_2"][0]
            out.append(tiles_of(np.concatenate([w, np.zeros((D, 25 * P - w.shape[1]), w.dtype)], axis=1)))
            out.append(tiles_of(i["gla_w_out_2"][0]))
        ffn(i["ffn_post_w_gate_2"][l], i["ffn_post_w_up_2"][l], i["ffn_post_w_down_2"][l])
    return np.ascontiguousarray(np.concatenate(out, axis=0))


def column_table(i):
    at, n = column_layout()
    t = np.zeros((P, n), np.float32)
    for l in range(LAYERS):
        for name, key in (("a_pre", "g_pre_mix"), ("a_post", "g_post_mix"), ("a_pre_ffn", "g_pre_ffn"),
                          ("a_post_ffn", "g_post_ffn"), ("a_gate", "g_ple_gate"), ("a_ple", "g_ple_post"),
                          ("b_pre", "ffn_pre_norm_2"), ("b_mix", "mix_norm_2"), ("b_post", "ffn_post_norm_2")):
            t[:, at[f"{name}{l}"]:at[f"{name}{l}"] + 8] = i[key][l].reshape(8, P).T
        t[:, at[f"g_sub{l}"]] = np.tile(i["g_diff_sub"][l], 2)
        t[:, at[f"sinks{l}"]:at[f"sinks{l}"] + 6] = i["swa_sinks"][l][None]
        lam = np.concatenate([i[k][l] for k in ("lam_q1", "lam_k1", "lam_q2", "lam_k2")])
        t[:, at[f"lam{l}"]:at[f"lam{l}"] + 128] = lam[None]
    diff_slopes, swa_slopes = slopes()
    for c in range(2 * DIFF_H):
        p0 = 32 * (c % 4)
        t[p0:p0 + 32, at["diff_rows"] + c] = np.float32(32 ** -0.5) / diff_slopes[c // 2]
    for h in range(SWA_H):
        p0 = 64 * (h // 3)
        t[p0:p0 + 64, at["swa_rows"] + h] = np.float32(0.125) / swa_slopes[h]
    for c in range(2):
        t[64 * c:64 * c + 64, at["dil_rows"] + c] = 1.0
    t[:, at["final"]:at["final"] + 8] = i["final_norm_2"].reshape(8, P).T
    return t


def gmlp_table(i):
    out = []
    for l in range(LAYERS):
        w = i["w_spatial"][l].transpose(2, 0, 1).reshape(P, 4 * P)
        bias = np.repeat(i["b_spatial"][l].reshape(2, 2, 1, P), 64, axis=2).reshape(2, P, P)
        out.append(np.concatenate([np.tile(i["gmlp_ln_g"][l], (P, 1)), np.tile(i["gmlp_ln_b"][l], (P, 1)), w,
                                   bias.transpose(1, 0, 2).reshape(P, 2 * P)], axis=1))
    return np.ascontiguousarray(np.stack(out))


def constants():
    p = np.arange(P)[:, None]
    diff = -np.abs(p - (np.arange(896)[None] - 384)).astype(np.float32)
    dist = np.abs(p - (np.arange(384)[None] - P)).astype(np.float32)
    swa = np.where(dist <= 128, -dist, NEG)
    rel = np.arange(S)[None] - p
    log_g = np.log(1.0 - 2.0 ** (-5.0 - np.arange(4, dtype=np.float32))).astype(np.float32)
    ret = np.concatenate([np.where(rel >= 0, np.exp(g * np.maximum(rel, 0)), 0.0) * 128 ** -0.5 for g in log_g],
                         axis=1)
    d = p - (np.arange(512)[None] - 384)
    count = ((d <= 128) * 1 + (d % 4 == 0) * 1 + (d % 16 == 0) * 1) * (d >= 0)
    dil = np.where(count > 0, np.log(np.maximum(count, 1)) * 8.0, NEG)
    pos = np.arange(S, dtype=np.float32)
    f_ret = np.float32(10000.0) ** (-np.linspace(0.0, 1.0, 64, dtype=np.float32))
    f_dil = np.float32(500000.0) ** (-np.arange(0, 16, 2, dtype=np.float32) / np.float32(16))
    a_ret = f_ret[np.arange(P) % 64][:, None] * pos[None]
    a_dil = np.zeros((P, S), np.float32)
    rot = np.zeros((P, 2, P), np.float32)
    for m in range(64):
        rot[m + 64, 0, m], rot[m, 0, m + 64] = -1.0, 1.0
    for h in range(2):
        for m in range(8):
            lo, hi = 64 * h + m, 64 * h + m + 8
            a_dil[lo] = a_dil[hi] = f_dil[m] * pos
            rot[hi, 1, lo], rot[lo, 1, hi] = -1.0, 1.0
    rotary = np.stack([np.cos(a_ret), np.sin(a_ret), np.cos(a_dil), np.sin(a_dil)], axis=1)
    c = np.arange(P)[None]
    causal = ((p <= c) & (p // 64 == c // 64)).astype(np.float32)
    gla = np.concatenate([causal / 16, causal], axis=1)
    f = lambda a: np.ascontiguousarray(a, dtype=np.float32)
    return {"dist": f(np.concatenate([diff, swa], axis=1)), "ident": f(np.eye(P)), "rot": f(rot), "rotary": f(rotary),
            "ret_dil": f(np.concatenate([ret, dil], axis=1)), "gla": f(gla)}


def kernel(**inputs):
    import concourse.bacc as bacc
    from concourse.bass_utils import run_bass_kernel_spmd

    i = {k: np.asarray(v) for k, v in inputs.items()}
    c = constants()
    wa2 = np.zeros((33, 512), np.float32)
    wa2[0:16], wa2[32] = i["gla_w_a2_2"][0], i["gla_b_a_2"][0]
    arrays = {
        "x": np.ascontiguousarray(i["x"][0].T.reshape(KT, P, S).transpose(1, 0, 2)),
        "p": np.ascontiguousarray(i["p"][:, 0].transpose(0, 2, 1).reshape(LAYERS, 2, P, S).transpose(0, 2, 1, 3)),
        "weights": weight_units(i), "cols": column_table(i), "gmlp": gmlp_table(i),
        "dist": c["dist"], "ident": c["ident"], "rot": c["rot"],
        "rotary": c["rotary"], "ret_dil": c["ret_dil"], "gla": c["gla"], "wa2": wa2,
    }
    nc = bacc.Bacc("TRN2", target_bir_lowering=False, num_devices=1)
    args = [nc.dram_tensor(f"in_{k}", a.shape, mybir.dt.from_np(a.dtype), kind="ExternalInput").ap()
            for k, a in arrays.items()]
    out = nc.dram_tensor("out_y", (P, KT, S), F32, kind="ExternalOutput").ap()
    program(nc, *args, out)
    r = run_bass_kernel_spmd(nc, [{f"in_{k}": a for k, a in arrays.items()}], core_ids=[0])
    y = r.results[0]["out_y"]
    return np.ascontiguousarray(y.transpose(1, 0, 2).reshape(D, S).T)[None]
```

```python
import math
from contextlib import ExitStack

import numpy as np

import concourse.bass as bass
from concourse import mybir

F32 = mybir.dt.float32
F32R = mybir.dt.float32r
I32 = mybir.dt.int32
ACT = mybir.ActivationFunctionType
ALU = mybir.AluOpType
AX = mybir.AxisListType

P = 128
D = 1024
S = 512
KT = D // P
TB = S // P
EPS = 1e-6
NEG = -1e30
FT = 2816 // P
LAYERS = 2
RING = 4
UNIT = 8 * P

DIFF_H, SWA_H, DIL_H, RET_H, GLA_H = 6, 6, 8, 4, 4
GLA_CHUNK = 64
GLA_DV = 256
AQ, AK, AV, BU, BV, CQ, CK, CV = 0, 3, 6, 9, 11, 13, 16, 17
RQ, RK, RV, RG, DQ, DK, DV = 0, 4, 8, 12, 16, 20, 24
GQ, GK, GA, GV, GR = 0, 4, 8, 9, 17
STAT, BCAST = 0, 1
LIN = (2, 3, 4, 5)
BACK = (2, 0, 3, 4, 5, 1, 6, 7)


def slopes():
    k = np.arange(1, 13, dtype=np.float32)
    s = np.exp2(-8.0 * k / 12)
    return s[6:], s[:6]


def linears():
    out = []
    for l in range(LAYERS):
        out += [(f"a_in{l}", 18, 18, 8), (f"a_out{l}", 8, 0, 10), (f"a_ffn_in{l}", 2 * FT, 2 * FT, 8),
                (f"a_ffn_out{l}", FT, 0, FT), (f"a_ple_up{l}", 2, 8, 0), (f"a_gate{l}", 8, 8, 8)]
    for l in range(LAYERS):
        n, cat = ((28, 8), (25, 4))[l]
        out += [(f"b_pre_in{l}", 2 * FT, 2 * FT, 8), (f"b_pre_out{l}", FT, 0, FT),
                (f"b_mix_in{l}", n, n, 8), (f"b_mix_out{l}", 8, 0, cat),
                (f"b_post_in{l}", 2 * FT, 2 * FT, 8), (f"b_post_out{l}", FT, 0, FT)]
    return out


class Linear:

    def __init__(self, n, u0, e0, m0, moving):
        self.n, self.u0, self.e0, self.m0, self.moving = n, u0, e0, m0, moving


def plan():
    u, e, m, out = 0, len(LIN), 0, {}
    for name, n, banks, moving in linears():
        out[name] = Linear(n, u, e, m, moving)
        u, e, m = u + n, e + banks, m + moving
    return out, u


def column_layout():
    at, n = {}, 0
    for name in ("a_pre", "a_post", "a_pre_ffn", "a_post_ffn", "a_gate", "a_ple", "b_pre", "b_mix", "b_post"):
        for l in range(LAYERS):
            at[f"{name}{l}"] = n
            n += 8
    at["final"] = n
    n += 8
    for name, w in (("diff_rows", 2 * DIFF_H), ("swa_rows", SWA_H), ("dil_rows", 2)):
        at[name] = n
        n += w
    for l in range(LAYERS):
        for name, w in (("g_sub", 1), ("sinks", SWA_H), ("lam", 4 * 32)):
            at[f"{name}{l}"] = n
            n += w
    return at, n


def program(nc, x_in, p_in, weights, cols_in, gmlp_in, dist_in, ident_in, rot_in, rotary_in,
            ret_dil_in, gla_in, wa2_in, y_out):
    lin, UNITS = plan()
    col_at, NCOL = column_layout()

    with ExitStack() as ctx:
        def sb(name, shape, dt=F32):
            return ctx.enter_context(nc.sbuf_tensor(name, shape, dt))

        def sem(name):
            return ctx.enter_context(nc.semaphore(name))

        x = sb("x", [P, KT, S])
        mvh = sb("mvh", [P, KT, S], F32R)
        mvl = sb("mvl", [P, KT, S], F32R)
        big = sb("big", [P, 28, S])
        y = sb("y", [P, KT, S])
        w_raw = sb("w_raw", [P, RING, UNIT])
        w_hi = sb("w_hi", [P, RING, UNIT], F32R)
        w_lo = sb("w_lo", [P, RING, UNIT], F32R)
        tab = sb("tab", [P, 2560])
        scr = sb("scr", [P, 10, S])
        cols = sb("cols", [P, NCOL])
        ident = sb("ident", [P, P])
        ones = sb("ones", [P, P])
        rot = sb("rot", [P, 2, P])
        rstd_b = sb("rstd_b", [P, S])
        diag = sb("diag", [P, TB, P])
        small = sb("small", [P, 256])

        g1, u1, s1 = scr[:, 0:2, :], scr[:, 2:4, :], scr[:, 4:6, :]
        sq = scr[:, 6:10, :]
        scaled, expo = y[:, 0:4, :], y[:, 4:8, :]
        comb, ptile, onorm, osq = scr[:, 0:2, :], scr[:, 2:4, :], scr[:, 4:6, :], scr[:, 6, :]
        gtmp = scr[:, 7:9, :]
        sm_x, sm_t, sm_y = small[:, 0:16], small[:, 16:32], small[:, 32:48]
        neg_max, row_sum = small[:, 48:64], small[:, 64:80]
        inv = small[:, 80:96]
        lam_s = small[:, 96:104]
        stats6 = small[:, 104:128]
        mean_var = small[:, 200:232]
        norm_stats = diag[:, 0, 0:96]
        neg_sinks = small[:, 144:144 + SWA_H]
        sink_c = small[:, 160:168]
        decay = small[:, 168:200]

        banks = [ctx.enter_context(nc.psum_tensor(f"bank{i}", [P, 512], F32)) for i in range(8)]

        x_loaded, p_loaded = [sem(f"x_loaded{i}") for i in range(4)], sem("p_loaded")
        cols_loaded = sem("cols_loaded")
        tables, consts = sem("tables"), sem("consts")
        out_stored = sem("out_stored")
        w_loaded = [sem(f"w_loaded{i}") for i in range(RING)]
        w_hi_ready, w_lo_ready = sem("w_hi_ready"), sem("w_lo_ready")
        unit_done = sem("unit_done")
        bank_free = sem("bank_free")
        mv_hi, mv_lo = sem("mv_hi"), sem("mv_lo")
        x_ready = sem("x_ready")
        y_ready = sem("y_ready")
        ones_set = sem("ones_set")
        dve_chain, act_chain = sem("dve_chain"), sem("act_chain")
        sq_ready, sq_used, sums_done = sem("sq_ready"), sem("sq_used"), sem("sums_done")
        diag_ready, bcast_done = sem("diag_ready"), sem("bcast_done")
        silu_done, hidden_ready = sem("silu_done"), sem("hidden_ready")
        p_hi, p_lo = sem("p_hi"), sem("p_lo")
        gate_sig, z_ready = sem("gate_sig"), sem("z_ready")
        vt_done, vt_copied = sem("vt_done"), sem("vt_copied")
        scores_done, scores_scaled, exp_done = sem("scores_done"), sem("scores_scaled"), sem("exp_done")
        probs_ready, pt_done, pt_copied = sem("probs_ready"), sem("pt_done"), sem("pt_copied")
        pv_done = sem("pv_done")
        osq_ready, onorm_ready, ot_done = sem("osq_ready"), sem("onorm_ready"), sem("ot_done")
        gated_ready, mixer_gates = sem("gated_ready"), sem("mixer_gates")
        lam_sum, lam_exp = sem("lam_sum"), sem("lam_exp")
        sink_sum, sink_exp = sem("sink_sum"), sem("sink_exp")
        keys_masked = sem("keys_masked")
        vn_ready, mixed_done = sem("vn_ready"), sem("mixed_done")
        rot_done, rotated = sem("rot_done"), sem("rotated")
        ret_scores, ret_decayed, ret_pv = sem("ret_scores"), sem("ret_decayed"), sem("ret_pv")
        alow_ready, z_done, z_soft, log_a = sem("alow_ready"), sem("z_done"), sem("z_soft"), sem("log_a")
        b_done, b_exp, b_used, kdec_ready = sem("b_done"), sem("b_exp"), sem("b_used"), sem("kdec_ready")
        kt_done, kt_copied = sem("kt_done"), sem("kt_copied")
        gsc_done, gsc_masked = sem("gsc_done"), sem("gsc_masked")
        kv_done, state_ready, gla_o = sem("kv_done"), sem("state_ready"), sem("gla_o")

        def ge(eng, s, v):
            if not isinstance(v, int) or v > 0:
                eng.wait_ge(s, v)

        def unit_loop(eng, n, body, tail=0):
            head = (n - tail) % RING
            for i in range(head):
                body(0, i)
            turns = (n - tail - head) // RING
            if turns:
                with eng.Fori(0, turns) as t:
                    for j in range(RING):
                        body(t, head + j)
            for i in range(n - tail, n):
                body(0, i)

        class Chain:

            def __init__(self, eng, s):
                self.eng, self.s, self.n = eng, s, 0

            def __call__(self, ins):
                ins.then_inc(self.s, 1)
                self.n += 1
                self.eng.wait_ge(self.s, self.n)

        def col(name, k=0, n=1):
            return cols[:, col_at[name] + k:col_at[name] + k + n]

        diff_slopes, swa_slopes = slopes()

        class Pair:
            pass

        def tok(tile, tb, c0, n):
            return big[:, tile, tb * P + c0:tb * P + c0 + n]

        def state(n, h):
            return y[:, 2 * (n % 2) + h // 2, (h % 2) * GLA_DV:(h % 2 + 1) * GLA_DV]

        diff_dist, swa_dist = tab[:, 1280:2176], tab[:, 2176:2560]
        logc = tab[:, 2048:2560]

        diff_keys = [big[:, 18 + i, :] for i in range(10)] + [scr[:, 7, :], scr[:, 8, :]]
        swa_keys = diff_keys[0:SWA_H]

        def diff_pairs():
            out = []
            for qb in range(TB):
                for h in range(DIFF_H):
                    q = Pair()
                    q.qb, q.h, q.kb0, q.nkb = qb, h, 0, TB
                    q.parts = []
                    for c in range(2):
                        q.parts.append((big[:, AQ + h // 2, qb * P:(qb + 1) * P], diff_keys[2 * h + c]))
                    q.masked = 2 * h + 2
                    q.bias, q.scale = diff_dist[:, 384 - qb * P:896 - qb * P], float(diff_slopes[h])
                    q.v = lambda kb, h=h: tok(AV + h // 2, kb, 64 * (h % 2), 64)
                    q.first = 3e38
                    out.append(q)
            return out

        def swa_pairs(l):
            out = []
            for qb in range(TB):
                for h in range(SWA_H):
                    q = Pair()
                    kv, t = h // 3, h % 3
                    kb1 = min(TB, qb + 2)
                    q.qb, q.h, q.kb0 = qb, h, max(0, qb - 1)
                    q.nkb = kb1 - q.kb0
                    q.parts = [(big[:, CQ + t, qb * P:(qb + 1) * P], swa_keys[h][:, q.kb0 * P:kb1 * P])]
                    q.masked = h + 1
                    c0 = (q.kb0 - qb + 1) * P
                    q.bias, q.scale = swa_dist[:, c0:c0 + q.nkb * P], float(swa_slopes[h])
                    q.v = lambda kb, kv=kv: tok(CV, kb, 64 * kv, 64)
                    q.first = neg_sinks[:, h:h + 1]
                    out.append(q)
            return out

        def dil_pairs():
            out = []
            for qb in range(TB):
                for h in range(DIL_H):
                    q = Pair()
                    q.qb, q.h, q.kb0, q.nkb = qb, h, 0, qb + 1
                    q.parts = [(big[:, DQ + h // 2, qb * P:(qb + 1) * P], big[:, RQ + h, 0:(qb + 1) * P])]
                    q.masked = h + 1
                    q.bias, q.scale = logc[:, 384 - qb * P:512], 0.125
                    q.v = lambda kb, h=h: tok(DV + h // 2, kb, 64 * (h % 2), 64)
                    q.first = 3e38
                    out.append(q)
            return out

        class Attention:

            def __init__(self, pairs, heads, comps, tile0, item0, pair0, block0):
                self.pairs, self.heads, self.comps, self.tile0 = pairs, heads, comps, tile0
                self.item0, self.pair0, self.block0 = item0, pair0, block0
                self.tiles = heads // 2

            def stat(self, t, c):
                q = self.pairs[t]
                return 2 * (t % 4) + c if self.comps == 2 else 8 * (q.qb % 2) + q.h

            def steps(self):
                return len(self.pairs) + 8

            def due(self, t, lag):
                q = t - lag
                if q >= 0 and (q + 1) % self.heads == 0 and q < len(self.pairs):
                    return q // self.heads
                return None

        atts, i0, p0, b0, probs0, keys0 = [], 0, 0, 0, 0, 0
        for kind, l in (("diff", 0), ("swa", 0), ("diff", 1), ("swa", 1), ("dil", 0)):
            pairs = {"diff": diff_pairs, "swa": lambda: swa_pairs(l), "dil": dil_pairs}[kind]()
            comps = 2 if kind == "diff" else 1
            heads, tile0 = {"diff": (6, 0), "swa": (6, 5), "dil": (8, 4)}[kind]
            if kind == "dil":
                RET_BLOCK0, b0 = b0, b0 + TB
            a = Attention(pairs, heads, comps, tile0, i0, p0, b0)
            a.kind, a.layer, a.probs0, a.keys0 = kind, l, probs0, keys0
            keys0 += {"diff": 2 * DIFF_H, "swa": SWA_H, "dil": DIL_H}[kind]
            a.m0 = {"diff": lin[f"a_out{l}"].m0, "swa": lin[f"a_out{l}"].m0 + TB + 2,
                    "dil": lin["b_mix_out0"].m0 + TB}[kind]
            probs0 += len(pairs) if comps == 2 else 0
            atts.append(a)
            i0, p0, b0 = i0 + comps * len(pairs), p0 + len(pairs), b0 + TB
        DIFF_ATT, SWA_ATT, DIL_ATT = (atts[0], atts[2]), (atts[1], atts[3]), atts[4]
        GLA_BLOCK0 = b0
        VT = {"a0": ([AV, AV + 1, AV + 2, BV, BV + 1, CV], 0), "a1": ([AV, AV + 1, AV + 2, BV, BV + 1, CV], 6),
              "b0": ([RV + i for i in range(4)] + [DV + i for i in range(4)], 12),
              "b1": ([GV + i for i in range(8)], 20)}
        NORM = {}
        for l in range(LAYERS):
            for n in ("a_in", "a_out", "a_ffn_in", "a_ffn_out", "a_gate", "a_ple"):
                NORM[f"{n}{l}"] = len(NORM)
        for l in range(LAYERS):
            for n in ("b_pre_in", "b_mix_in", "b_post_in"):
                NORM[f"{n}{l}"] = len(NORM)
        NORM["final"] = len(NORM)
        XR = {}
        for n in [f"a_{k}{l}" for l in range(LAYERS) for k in ("mix", "ffn", "ple")] + [
                f"b_{k}{l}" for l in range(LAYERS) for k in ("pre", "mix", "post")]:
            XR[n] = 8 * len(XR)
        XIN = {"a_in1": "a_ple0", "b_pre_in0": "a_ple1", "b_pre_in1": "b_post0"}
        for l in range(LAYERS):
            XIN.update({f"a_ffn_in{l}": f"a_mix{l}", f"a_gate{l}": f"a_ffn{l}", f"b_mix_in{l}": f"b_pre{l}",
                        f"b_post_in{l}": f"b_mix{l}"})
        XIN = {k: XR[v] for k, v in XIN.items()}
        FFN = {n: FT * i for i, n in enumerate(("a_ffn_in0", "a_ffn_in1", "b_pre_in0", "b_post_in0", "b_pre_in1",
                                                "b_post_in1"))}

        ROTARY = {8 + i: (RQ + i, 0) for i in range(8)}
        ROTARY.update({18 + i: (DQ + i, 1) for i in range(8)})
        ROT_N = {u: i for i, u in enumerate(sorted(ROTARY))}
        RET_VT, RET_SILU = {16 + i: i for i in range(4)}, 16
        GLA_Z, GLA_ABS, GLA_EXP, GLA_LN, GLA_SUM, GLA_VT = 9, 9, 10, 11, 13, 17
        GLA_B = {13: (0, 1), 14: (2, 3)}
        GLA_SC = {15: (0, 1), 16: (2, 3)}
        A_VT, A_LAM = {9: 0, 10: 1, 11: 2, 13: 3, 14: 4}, 15
        FREE = (0, 1, 6, 7)

        block = ctx.enter_context(nc.Block())

        @block.sync
        def _(sp):
            def load(u, slot):
                return sp.dma_start(w_raw[:, slot, :], weights[bass.ds(u, 1), :, :].rearrange("u p n -> p (u n)"))

            sp.dma_start(cols[:, :], cols_in).then_inc(cols_loaded, 16)
            for u in range(RING):
                load(u, u).then_inc(w_loaded[u], 16)
                sp.dma_start(x[:, 2 * u:2 * u + 2, :], x_in[:, 2 * u:2 * u + 2, :]).then_inc(x_loaded[u], 16)
            sp.dma_start(ident[:, :], ident_in).then_inc(consts, 16)
            sp.dma_start(rot[:, :, :], rot_in).then_inc(consts, 16)
            turns = (UNITS - RING) // RING
            with sp.Fori(0, turns) as t:
                for j in range(RING):
                    sp.wait_ge(w_lo_ready, t * RING + j + 1)
                    load(t * RING + RING + j, j).then_inc(w_loaded[j], 16)
            for u in range(RING + turns * RING, UNITS):
                sp.wait_ge(w_lo_ready, u - RING + 1)
                load(u, u % RING).then_inc(w_loaded[u % RING], 16)
            sp.wait_ge(y_ready, 8)
            sp.dma_start(y_out, y[:, :, :]).then_inc(out_stored, 16)
            sp.wait_ge(out_stored, 16)

        @block.gpsimd
        def _(pool):
            def split(u, slot):
                pool.wait_ge(w_hi_ready, u + 1)
                nc.gpsimd.tensor_tensor(w_lo[:, slot, :], w_raw[:, slot, :], w_hi[:, slot, :].bitcast(F32),
                                        ALU.subtract).then_inc(w_lo_ready, 1)

            done = [0]

            def splits(until):
                u0 = done[0]
                turns = (until - u0) // RING
                if turns:
                    with pool.Fori(0, turns) as t:
                        for j in range(RING):
                            split(t * RING + u0 + j, (u0 + j) % RING)
                for u in range(u0 + turns * RING, until):
                    split(u, u % RING)
                done[0] = until

            def mask(dst, src, factor):
                nc.gpsimd.tensor_scalar(dst, src, factor, None, ALU.mult).then_inc(keys_masked, 1)

            acc = diag[:, :, :].rearrange("p a b -> p (a b)")

            def add_squares(name, k0, k1):
                n = NORM[name]
                for k in range(max(k0, 1), k1):
                    pool.wait_ge(sq_ready, 8 * n + k + 1)
                    if k == 1:
                        ge(pool, bcast_done, n)
                        nc.gpsimd.tensor_tensor(acc, sq[:, 0, :], sq[:, 1, :], ALU.add).then_inc(sq_used, 2)
                    else:
                        pool.wait_ge(sq_used, 8 * n + k)
                        nc.gpsimd.tensor_tensor(acc, acc, sq[:, k % 4, :], ALU.add).then_inc(sq_used, 1)

            def up_to(name):
                splits(lin[name].u0 + RING)
                add_squares(name, 0, KT)

            for l in range(LAYERS):
                a, out = lin[f"a_in{l}"], lin[f"a_out{l}"]
                if l:
                    up_to("a_in1")
                else:
                    splits(3)
                    add_squares("a_in0", 0, 4)
                    splits(4)
                    add_squares("a_in0", 4, KT)
                for i in range(DIFF_H // 2):
                    splits(a.u0 + 8 + 3 * i)
                    pool.wait_ge(bank_free, a.e0 + AK + i + 1)
                    pool.wait_ge(sq_used, 8 * (NORM[f"a_in{l}"] + 1))
                    for c in range(4):
                        mask(diff_keys[4 * i + c], big[:, AK + i, :], col("diff_rows", 4 * i + c))
                splits(out.u0 + 4)
                pool.wait_ge(bank_free, a.e0 + CK + 1)
                pool.wait_ge(scores_done, DIFF_ATT[l].item0 + 48)
                for h in range(SWA_H):
                    mask(swa_keys[h], big[:, CK, :], col("swa_rows", h))
                up_to(f"a_ffn_in{l}")
                gate = f"a_gate{l}"
                splits(lin[gate].u0 + 2)
                add_squares(gate, 0, 2)
                splits(lin[gate].u0 + 3)
                add_squares(gate, 2, 4)
                splits(lin[gate].u0 + 4)
                add_squares(gate, 4, KT)
            up_to("b_pre_in0")
            up_to("b_mix_in0")
            splits(lin["b_mix_out0"].u0 + 4)
            pool.wait_ge(ret_scores, TB * RET_H)
            pool.wait_ge(rotated, 16)
            for h in range(DIL_H):
                mask(big[:, RQ + h, :], big[:, DK + h // 2, :], col("dil_rows", h % 2))
            for name in ("b_post_in0", "b_pre_in1", "b_mix_in1", "b_post_in1"):
                up_to(name)
            splits(UNITS)

        @block.scalar
        def _(act):
            chain = Chain(act, act_chain)

            def weight_hi(slot, loads):
                act.wait_ge(w_loaded[slot], loads)
                nc.scalar.activation(w_hi[:, slot, :], w_raw[:, slot, :], ACT.Copy).then_inc(w_hi_ready, 1)

            def after_unit(L, t, s):
                act.wait_ge(unit_done, t * RING + L.u0 + s + 1)
                loads = (L.u0 + s + RING) // RING + 1
                weight_hi((L.u0 + s) % RING, t * 16 + 16 * loads)

            def plain_units(L, beside=None):
                if beside is None:
                    unit_loop(act, L.n, lambda t, s: after_unit(L, t, s))
                    return
                unit_loop(act, 8, lambda t, s: after_unit(L, t, s))
                for s in range(8, L.n):
                    after_unit(L, 0, s)
                    beside(s)

            def square(norm, k, src):
                ge(act, sq_used, 8 * norm + k - 3)
                nc.scalar.activation(sq[:, k % 4, :], src, ACT.Square).then_inc(sq_ready, 1)

            def moving_from_x(name, gain):
                L = lin[name]
                gate = name.startswith("a_gate")
                ge(act, unit_done, L.u0 - 2 if gate else L.u0)
                for k in range(KT):
                    if gate and k in (1, 4):
                        after_unit(lin[f"a_ple_up{name[-1]}"], 0, k // 4)
                    if name in XIN:
                        act.wait_ge(x_ready, XIN[name] + k + 1)
                    else:
                        act.wait_ge(x_loaded[k // 2], 16)
                    nc.scalar.activation(mvh[:, k, :], x[:, k, :], ACT.Copy, scale=col(gain, k)).then_inc(mv_hi, 1)
                    square(NORM[name], k, x[:, k, :])
                    if name == "a_in0" and k in (0, 2, 4):
                        weight_hi(k // 2 + 1, 16)

            def ffn_in(name):
                L, f0 = lin[name], FFN[name]

                def body(t, s):
                    after_unit(L, t, s)
                    if s % 2 == 0:
                        act.wait_ge(bank_free, t * RING + L.e0 + s + 1)
                        ring = (s // 2) % 2
                        nc.scalar.activation(s1[:, ring, :], g1[:, ring, :], ACT.Silu).then_inc(silu_done, 1)

                unit_loop(act, L.n, body)

            def ffn_out(name, in_name, tail=0):
                L, f0 = lin[name], FFN[in_name]

                def cast(t, s):
                    act.wait_ge(hidden_ready, t * RING + f0 + s + 1)
                    src = big[:, bass.ds(t * RING + s, 1), :].rearrange("p a b -> p (a b)")
                    nc.scalar.activation(mvh[:, s % 4, :], src, ACT.Copy).then_inc(mv_hi, 1)

                act.wait_ge(unit_done, L.u0)
                for f in range(4):
                    cast(0, f)
                if name[0] == "a":
                    l = int(name[-1])
                    act.wait_ge(p_loaded, 16 * (l + 1))
                    nc.scalar.activation(mvh[:, 4:6, :], y[:, 0:2, :], ACT.Copy).then_inc(p_hi, 1)

                def body(t, s):
                    after_unit(L, t, s)
                    cast(t, s + 4)

                unit_loop(act, FT - 4, body)
                for f in range(FT - 4, FT - tail):
                    after_unit(L, 0, f)

            def emit(block_n, b, bank, tile0, tiles, scale):
                act.wait_ge(ot_done, block_n + 1)
                src = bank[:, 0:tiles * P].rearrange("p (a b) -> p a b", b=P)
                dst = mvh[:, tile0:tile0 + tiles, b * P:(b + 1) * P]
                if scale is None:
                    nc.scalar.activation(dst, src, ACT.Copy).then_inc(mv_hi, 1)
                else:
                    nc.scalar.activation(dst, src, ACT.Copy, scale=scale).then_inc(mv_hi, 1)

            def attention(a):
                n = len(a.pairs)
                for t in range(a.steps()):
                    if t < n:
                        q = a.pairs[t]
                        for c in range(a.comps):
                            slot, sc = 2 * (t % 2) + c, a.stat(t, c)
                            act.wait_ge(scores_scaled, a.item0 + a.comps * t + c + 1)
                            if a.comps == 1:
                                ge(act, pt_done, a.pair0 + t - 1)
                            else:
                                ge(act, probs_ready, a.probs0 + t - 1)
                            nc.scalar.activation(expo[:, slot, 0:q.nkb * P], scaled[:, slot, 0:q.nkb * P], ACT.Exp,
                                                 scale=-1.0, bias=neg_max[:, sc:sc + 1],
                                                 accum_out=row_sum[:, sc:sc + 1]).then_inc(exp_done, 1)
                    if 1 <= t <= n:
                        r = t - 1
                        act.wait_ge(pt_done, a.pair0 + r + 1)
                        ge(act, pv_done, a.pair0 + r - 1)
                        w = a.pairs[r].nkb * P
                        nc.scalar.activation(ptile[:, r % 2, 0:w], banks[4 + r % 2][:, 0:w],
                                             ACT.Copy).then_inc(pt_copied, 1)
                    b = a.due(t, 3)
                    if b is not None and a.kind == "diff":
                        act.wait_ge(pv_done, a.pair0 + (b + 1) * a.heads)
                        ge(act, onorm_ready, a.block0 + b)
                        nc.scalar.activation(osq[:, 0:384], banks[6 + b % 2][:, 0:384],
                                             ACT.Square).then_inc(osq_ready, 1)
                    if b is not None and a.kind == "swa":
                        act.wait_ge(sink_sum, a.layer * TB + b + 1)
                        nc.scalar.activation(sink_c[:, 0:a.heads], sink_c[:, 0:a.heads],
                                             ACT.Exp).then_inc(sink_exp, 1)
                    b = a.due(t, 7)
                    if b is not None:
                        emit(a.block0 + b, b, banks[6 + b % 2], a.tile0, a.tiles,
                             col(f"g_sub{a.layer}") if a.kind == "diff" else None)

            def transposed_value(key, i):
                tiles, n0 = VT[key]
                act.wait_ge(vt_done, n0 + i + 1)
                nc.scalar.activation(big[:, tiles[i], :], banks[6 + i % 2][:, :], ACT.Copy).then_inc(vt_copied, 1)

            def transposed_values(key, first=0):
                for i in range(first, len(VT[key][0])):
                    transposed_value(key, i)

            def silus(L, tiles):
                act.wait_ge(bank_free, L.e0 + tiles[-1] + 1)
                for m in tiles:
                    nc.scalar.activation(big[:, m, :], big[:, m, :], ACT.Silu).then_inc(mixer_gates, 1)

            def beside_a(l, s):
                if s in A_VT:
                    transposed_value(f"a{l}", A_VT[s])
                if s == A_LAM:
                    act.wait_ge(lam_sum, l + 1)
                    nc.scalar.activation(lam_s[:, 2:4], lam_s[:, 0:2], ACT.Exp).then_inc(lam_exp, 1)

            def beside_retention(s):
                if s == RET_SILU:
                    silus(lin["b_mix_in0"], range(RG, RG + RET_H))
                if s in RET_VT:
                    transposed_value("b0", RET_VT[s])

            def emit_gated(n, tile0, tiles, b):
                act.wait_ge(gated_ready, n + 1)
                src = (scr[:, 8:10, :] if tiles == 8 else gtmp[:, b % 2:b % 2 + 1, :]).rearrange(
                    "p a (b c) -> p (a b) c", c=P)
                nc.scalar.activation(mvh[:, tile0:tile0 + tiles, b * P:(b + 1) * P], src,
                                     ACT.Copy).then_inc(mv_hi, 1)

            def beside_gla(s):
                for b in range(TB):
                    if s == GLA_ABS:
                        act.wait_ge(z_done, b + 1)
                        chain(nc.scalar.activation(scr[:, 4 + b, :], banks[FREE[b]][:, :], ACT.Abs))
                    if s == GLA_EXP:
                        chain(nc.scalar.activation(scr[:, 4 + b, :], scr[:, 4 + b, :], ACT.Exp, scale=-1.0))
                    if s == GLA_LN:
                        nc.scalar.activation(scr[:, 4 + b, :], scr[:, 4 + b, :], ACT.Ln, bias=1.0).then_inc(z_soft, 1)
                for h in GLA_B.get(s, ()):
                    act.wait_ge(b_done, h + 1)
                    ge(act, b_used, h)
                    nc.scalar.activation(scr[:, 8, :], banks[FREE[h]][:, :], ACT.Exp)
                    nc.scalar.activation(scr[:, 9, :], banks[FREE[h]][:, :], ACT.Exp, scale=-1.0).then_inc(b_exp, 1)
                for h in GLA_SC.get(s, ()):
                    act.wait_ge(kt_done, h + 1)
                    nc.scalar.activation(y[:, 4 + h, :], banks[h % 2][:, :], ACT.Copy).then_inc(kt_copied, 1)
                if s >= GLA_VT:
                    transposed_value("b1", s - GLA_VT)
                if s == 22:
                    silus(lin["b_mix_in1"], range(GR, GR + 4))

            def gla():
                silus(lin["b_mix_in1"], range(GR + 4, GR + 8))
                for b in range(TB):
                    emit_gated(2 * LAYERS + TB + b, 0, 8, b)

            weight_hi(0, 16)
            act.wait_ge(cols_loaded, 16)
            for l in range(LAYERS):
                moving_from_x(f"a_in{l}", f"a_pre{l}")
                act.dma_start(tab[:, 1280:2560], dist_in).then_inc(tables, 16)
                act.dma_start(tab[:, 0:1280], gmlp_in[l]).then_inc(tables, 16)
                plain_units(lin[f"a_in{l}"], lambda s: beside_a(l, s))
                transposed_values(f"a{l}", len(A_VT))
                attention(DIFF_ATT[l])
                for g in range(2):
                    act.wait_ge(gated_ready, 2 * l + g + 1)
                    nc.scalar.activation(mvh[:, 3 + g, :], gtmp[:, g, :], ACT.Copy).then_inc(mv_hi, 1)
                attention(SWA_ATT[l])
                L = lin[f"a_out{l}"]
                for i in range(8):
                    after_unit(L, 0, i)
                    nc.scalar.activation(y[:, i, :], banks[BACK[i]][:, :], ACT.Copy)
                    square(NORM[f"a_out{l}"], i, banks[BACK[i]][:, :])
                moving_from_x(f"a_ffn_in{l}", f"a_pre_ffn{l}")
                act.dma_start(y[:, 0:2, :], p_in[l]).then_inc(p_loaded, 16)
                ffn_in(f"a_ffn_in{l}")
                ffn_out(f"a_ffn_out{l}", f"a_ffn_in{l}")
                act.wait_ge(p_lo, l + 1)
                for n in range(8):
                    nc.scalar.activation(y[:, n, :], banks[BACK[n]][:, :], ACT.Copy)
                    square(NORM[f"a_ffn_out{l}"], n, banks[BACK[n]][:, :])
                moving_from_x(f"a_gate{l}", f"a_gate{l}")
                L = lin[f"a_gate{l}"]
                for i in range(8):
                    after_unit(L, 0, i)
                    act.wait_ge(bank_free, L.e0 + i + 1)
                    nc.scalar.activation(s1[:, i % 2, :], g1[:, i % 2, :], ACT.Sigmoid).then_inc(gate_sig, 1)
                    if i:
                        act.wait_ge(z_ready, 8 * l + i)
                        square(NORM[f"a_ple{l}"], i - 1, y[:, i - 1, :])
                act.wait_ge(z_ready, 8 * l + 8)
                square(NORM[f"a_ple{l}"], 7, y[:, 7, :])

            for l in range(LAYERS):
                moving_from_x(f"b_pre_in{l}", f"b_pre{l}")
                if l == 0:
                    act.dma_start(tab[:, :], ret_dil_in).then_inc(tables, 16)
                    act.dma_start(y[:, 0:4, :], rotary_in).then_inc(tables, 16)
                else:
                    act.dma_start(tab[:, 0:256], gla_in).then_inc(tables, 16)
                    act.dma_start(tab[0:33, 256:768], wa2_in).then_inc(tables, 16)
                ffn_in(f"b_pre_in{l}")
                ffn_out(f"b_pre_out{l}", f"b_pre_in{l}")
                moving_from_x(f"b_mix_in{l}", f"b_mix{l}")
                plain_units(lin[f"b_mix_in{l}"], beside_gla if l else beside_retention)
                if l == 0:
                    transposed_values("b0", RET_H)
                    for b in range(TB):
                        emit_gated(2 * LAYERS + b, 0, 4, b)
                    attention(DIL_ATT)
                else:
                    gla()
                plain_units(lin[f"b_mix_out{l}"])
                moving_from_x(f"b_post_in{l}", f"b_post{l}")
                ffn_in(f"b_post_in{l}")
                ffn_out(f"b_post_out{l}", f"b_post_in{l}", tail=4 if l else 0)
            for k in range(KT):
                act.wait_ge(x_ready, XR["b_post1"] + k + 1)
                square(NORM["final"], k, x[:, k, :])

        @block.vector
        def _(dve):
            chain = Chain(dve, dve_chain)

            def rsqrt(out, src, scale, n):
                v, t = sm_x[:, 0:n], sm_t[:, 0:n]
                chain(nc.vector.tensor_scalar(v, src, scale, EPS, ALU.mult, ALU.add))
                chain(nc.vector.tensor_scalar(t.bitcast(I32), v.bitcast(I32), 1, None, ALU.logical_shift_right))
                chain(nc.vector.tensor_scalar(out.bitcast(I32), t.bitcast(I32), -1.0, float(0x5F3759DF),
                                              ALU.mult, ALU.add))
                for _ in range(3):
                    chain(nc.vector.scalar_tensor_tensor(out=t, in0=out, scalar=-0.5, in1=out,
                                                         op0=ALU.mult, op1=ALU.mult))
                    chain(nc.vector.tensor_tensor(t, t, v, ALU.mult))
                    chain(nc.vector.scalar_tensor_tensor(out=out, in0=t, scalar=1.5, in1=out,
                                                         op0=ALU.add, op1=ALU.mult))

            def rstd_diag(norm):
                dve.wait_ge(sums_done, norm + 1)
                rsqrt(sm_y[:, 0:TB], banks[STAT][:, 0:TB], 1.0 / D, TB)
                nc.vector.tensor_tensor(diag[:, :, :], ident[:, :].unsqueeze(1).broadcast_to([P, TB, P]),
                                        sm_y[:, 0:TB].unsqueeze(2).broadcast_to([P, TB, P]),
                                        ALU.mult).then_inc(diag_ready, 1)

            def rstd_spread(norm):
                dve.wait_ge(bcast_done, norm + 1)
                chain(nc.vector.tensor_copy(rstd_b[:, :], banks[BCAST][:, :]))

            def rstd(norm):
                rstd_diag(norm)
                rstd_spread(norm)

            def enter(name, gain, update=None):
                L = lin[name]
                for k in range(KT + 1):
                    if update is not None and k < KT:
                        update(k)
                    if k:
                        dve.wait_ge(mv_hi, L.m0 + k)
                        nc.vector.scalar_tensor_tensor(out=mvl[:, k - 1, :], in0=x[:, k - 1, :],
                                                       scalar=col(gain, k - 1), in1=mvh[:, k - 1, :].bitcast(F32),
                                                       op0=ALU.mult, op1=ALU.subtract).then_inc(mv_lo, 1)

            def post(gain):
                def update(k):
                    if k == 0:
                        nc.vector.scalar_tensor_tensor(out=y[:, 0, :], in0=y[:, 0, :], scalar=col(gain, 0),
                                                       in1=rstd_b[:, :], op0=ALU.mult, op1=ALU.mult
                                                       ).then_inc(dve_chain, 1)
                        chain.n += 1
                    own = chain.n
                    if k + 1 < KT:
                        nc.vector.scalar_tensor_tensor(out=y[:, k + 1, :], in0=y[:, k + 1, :],
                                                       scalar=col(gain, k + 1), in1=rstd_b[:, :],
                                                       op0=ALU.mult, op1=ALU.mult).then_inc(dve_chain, 1)
                        chain.n += 1
                    dve.wait_ge(dve_chain, own)
                    nc.vector.tensor_tensor(x[:, k, :], x[:, k, :], y[:, k, :], ALU.add).then_inc(x_ready, 1)
                return update

            def add_down(L):
                def update(k):
                    if k == 0:
                        dve.wait_ge(unit_done, L.u0 + FT)
                    nc.vector.scalar_tensor_tensor(out=x[:, k, :], in0=banks[BACK[k]][:, :], scalar=0.5,
                                                   in1=x[:, k, :], op0=ALU.mult, op1=ALU.add).then_inc(x_ready, 1)
                return update

            def add_mix(L):
                def update(k):
                    dve.wait_ge(unit_done, L.u0 + k + 1)
                    nc.vector.tensor_tensor(x[:, k, :], banks[BACK[k]][:, :], x[:, k, :],
                                            ALU.add).then_inc(x_ready, 1)
                return update

            def project(name, beside=None):
                L = lin[name]

                def body(t, s):
                    dve.wait_ge(unit_done, t * RING + L.u0 + s + 1)
                    dst = big[:, bass.ds(t * RING + s, 1), :].rearrange("p a b -> p (a b)")
                    nc.vector.tensor_tensor(dst, banks[LIN[s % 4]][:, :], rstd_b[:, :], ALU.mult).then_inc(bank_free, 1)

                if beside is None:
                    unit_loop(dve, L.n, body)
                    return
                unit_loop(dve, 8, body)
                for s in range(8, L.n):
                    body(0, s)
                    beside(s)

            def ffn_in(name):
                L, f0 = lin[name], FFN[name]

                def body(t, s):
                    ring = (s // 2) % 2
                    dve.wait_ge(unit_done, t * RING + L.u0 + s + 1)
                    dst = (g1 if s % 2 == 0 else u1)[:, ring, :]
                    nc.vector.tensor_tensor(dst, banks[LIN[s % 4]][:, :], rstd_b[:, :], ALU.mult).then_inc(bank_free, 1)
                    if s % 2:
                        dve.wait_ge(silu_done, t * 2 + f0 + s // 2 + 1)
                        dve.wait_ge(bank_free, t * RING + L.e0 + s + 1)
                        dst = big[:, bass.ds(t * 2 + s // 2, 1), :].rearrange("p a b -> p (a b)")
                        nc.vector.tensor_tensor(dst, s1[:, ring, :], u1[:, ring, :], ALU.mult).then_inc(hidden_ready, 1)

                unit_loop(dve, L.n, body)

            def ffn_out(name):
                L = lin[name]

                def body(t, s):
                    dve.wait_ge(mv_hi, t * RING + L.m0 + s + 1)
                    src = big[:, bass.ds(t * RING + s, 1), :].rearrange("p a b -> p (a b)")
                    nc.vector.tensor_tensor(mvl[:, s % 4, :], src, mvh[:, s % 4, :].bitcast(F32),
                                            ALU.subtract).then_inc(mv_lo, 1)

                for f in range(4):
                    body(0, f)
                if name[0] == "a":
                    dve.wait_ge(p_hi, int(name[-1]) + 1)
                    nc.vector.tensor_tensor(mvl[:, 4:6, :], y[:, 0:2, :], mvh[:, 4:6, :].bitcast(F32),
                                            ALU.subtract).then_inc(p_lo, 1)
                for f in range(4, 6):
                    body(0, f)
                with dve.Fori(0, (FT - 6) // RING) as t:
                    for j in range(RING):
                        body(t, 6 + j)

            def emit(m0, block_n, b, bank, tile0, tiles, scale):
                dve.wait_ge(mv_hi, m0 + 1)
                src = bank[:, 0:tiles * P].rearrange("p (a b) -> p a b", b=P)
                at = (slice(None), slice(tile0, tile0 + tiles), slice(b * P, (b + 1) * P))
                if scale is None:
                    nc.vector.tensor_tensor(mvl[at], src, mvh[at].bitcast(F32), ALU.subtract).then_inc(mv_lo, 1)
                else:
                    nc.vector.scalar_tensor_tensor(out=mvl[at], in0=src, scalar=scale, in1=mvh[at].bitcast(F32),
                                                   op0=ALU.mult, op1=ALU.subtract).then_inc(mv_lo, 1)

            def attention(a, m0):
                n, H = len(a.pairs), a.heads
                for t in range(a.steps()):
                    if a.kind == "diff" and t == 1:
                        dve.wait_ge(vt_copied, 6 * (a.layer + 1))
                    if a.kind == "diff" and 1 <= t < 14:
                        gmlp_norm(t - 1)
                    if a.kind == "diff" and t == n + 3:
                        gmlp_gate(a.layer)
                    if t < n:
                        q = a.pairs[t]
                        for c in range(a.comps):
                            i, slot, sc = a.item0 + a.comps * t + c, 2 * (t % 2) + c, a.stat(t, c)
                            w = q.nkb * P
                            dve.wait_ge(scores_done, i + 1)
                            ge(dve, exp_done, a.item0 + a.comps * (t - 1))
                            nc.vector.tensor_tensor_reduce(out=scaled[:, slot, 0:w], in0=banks[slot][:, 0:w],
                                                           in1=q.bias, scale=-q.scale, scalar=q.first,
                                                           op0=ALU.add, op1=ALU.min,
                                                           accum_out=neg_max[:, sc:sc + 1]).then_inc(scores_scaled, 1)
                    if a.comps == 2 and 1 <= t <= n:
                        r = t - 1
                        s0, sl, ring = 2 * (r % 2), a.stat(r, 0), r % 2
                        dve.wait_ge(exp_done, a.item0 + 2 * t)
                        ge(dve, pt_done, a.pair0 + r - 1)
                        chain(nc.vector.reciprocal(inv[:, 0:2], row_sum[:, sl:sl + 2]))
                        nc.vector.tensor_scalar(inv[:, 2:3], inv[:, 1:2], lam_s[:, 4:5], None, ALU.mult)
                        chain(nc.vector.tensor_scalar(comb[:, ring, :], expo[:, s0, :], inv[:, 0:1], None, ALU.mult))
                        nc.vector.scalar_tensor_tensor(out=comb[:, ring, :], in0=expo[:, s0 + 1, :],
                                                       scalar=inv[:, 2:3], in1=comb[:, ring, :],
                                                       op0=ALU.mult, op1=ALU.add).then_inc(probs_ready, 1)
                    b = a.due(t, 2)
                    if b is not None and a.kind == "swa":
                        dve.wait_ge(scores_scaled, a.item0 + (b + 1) * H)
                        chain(nc.vector.tensor_copy(sink_c[:, 0:8], neg_max[:, 8 * (b % 2):8 * (b % 2) + 8]))
                        nc.vector.tensor_tensor(sink_c[:, 0:H], sink_c[:, 0:H], col(f"sinks{a.layer}", 0, H),
                                                ALU.add).then_inc(sink_sum, 1)
                    b = a.due(t, 4)
                    if b is not None:
                        o = banks[6 + b % 2][:, 0:64 * H].rearrange("p (h d) -> p h d", d=64)
                        on = onorm[:, b % 2, 0:64 * H].rearrange("p (h d) -> p h d", d=64)
                        if a.kind == "diff":
                            dve.wait_ge(osq_ready, a.layer * TB + b + 1)
                            sums = sm_t[:, 8:8 + H]
                            chain(nc.vector.reduce_sum(sums, osq[:, 0:384].rearrange("p (h d) -> p h d", d=64),
                                                       AX.X))
                            rsqrt(sm_y[:, 0:H], sums, 1.0 / 64, H)
                        else:
                            dve.wait_ge(pv_done, a.pair0 + (b + 1) * H)
                            ls = row_sum[:, 8 * (b % 2):8 * (b % 2) + H]
                            dve.wait_ge(exp_done, a.item0 + (b + 1) * H)
                            if a.kind == "swa":
                                dve.wait_ge(sink_exp, a.layer * TB + b + 1)
                                chain(nc.vector.tensor_tensor(sink_c[:, 0:H], sink_c[:, 0:H], ls, ALU.add))
                                ls = sink_c[:, 0:H]
                            chain(nc.vector.reciprocal(sm_y[:, 0:H], ls))
                        ge(dve, ot_done, a.block0 + b - 1)
                        nc.vector.tensor_tensor(on, o, sm_y[:, 0:H].unsqueeze(2).broadcast_to([P, H, 64]),
                                                ALU.mult).then_inc(onorm_ready, 1)
                    b = a.due(t, 8)
                    if b is not None:
                        emit(m0 + b, a.block0 + b, b, banks[6 + b % 2], a.tile0, a.tiles,
                             col(f"g_sub{a.layer}") if a.kind == "diff" else None)

            def lam(l):
                init = 0.8 - 0.6 * math.exp(-0.3 * l)
                v = col(f"lam{l}", 0, 128).rearrange("p (a b c) -> p a b c", b=2, c=32)
                prod = onorm[:, 0, 0:64].rearrange("p (a c) -> p a c", c=32)
                chain(nc.vector.tensor_tensor(prod, v[:, :, 0, :], v[:, :, 1, :], ALU.mult))
                nc.vector.reduce_sum(lam_s[:, 0:2], prod, AX.X).then_inc(lam_sum, 1)
                dve.wait_ge(lam_exp, l + 1)
                chain(nc.vector.tensor_tensor(lam_s[:, 5:6], lam_s[:, 3:4], lam_s[:, 2:3], ALU.subtract))
                chain(nc.vector.tensor_scalar(lam_s[:, 4:5], lam_s[:, 5:6], -init, None, ALU.add))
                chain(nc.vector.tensor_scalar(neg_sinks, col(f"sinks{l}", 0, SWA_H), -1.0, None, ALU.mult))
                chain(nc.vector.tensor_scalar(col(f"g_sub{l}"), col(f"g_sub{l}"), 1.0 - init, None, ALU.mult))

            def gmlp_norm(i):
                if i < 4:
                    for m in range(2):
                        last = nc.vector.bn_stats(stats6[:, 6 * m:6 * m + 6], tok(BV + m, i, 0, P))
                    chain(last)
                    chain(nc.vector.bn_aggr(mean_var[:, 2 * i:2 * i + 2], stats6[:, 0:12]))
                elif i == 4:
                    rsqrt(sm_y[:, 8:8 + TB], mean_var[:, 1:8:2], 1.0, TB)
                elif i < 9:
                    b = i - 5
                    vn = big[:, BV:BV + 2, b * P:(b + 1) * P]
                    chain(nc.vector.tensor_scalar(vn, vn, mean_var[:, 2 * b:2 * b + 1], sm_y[:, 8 + b:9 + b],
                                                  ALU.subtract, ALU.mult))
                else:
                    m = (i - 9) % 2
                    row, op = (tab[:, 0:256], ALU.mult) if i < 11 else (tab[:, 256:512], ALU.add)
                    vn = big[:, BV + m, :].rearrange("p (b c) -> p b c", c=P)
                    last = nc.vector.tensor_tensor(vn, vn, row[:, m * P:(m + 1) * P].unsqueeze(1).broadcast_to(
                        [P, TB, P]), op)
                    if i == 12:
                        last.then_inc(vn_ready, 1)
                    else:
                        chain(last)

            def gmlp_gate(l):
                for g in range(2):
                    dve.wait_ge(mixed_done, 2 * l + g + 1)
                    t = gtmp[:, g, :].rearrange("p (b c) -> p b c", c=P)
                    chain(nc.vector.tensor_tensor(t, banks[1 + 2 * g][:, :].rearrange("p (b c) -> p b c", c=P),
                                                  tab[:, 1024 + g * P:1024 + (g + 1) * P].unsqueeze(1).broadcast_to(
                                                      [P, TB, P]), ALU.add))
                    nc.vector.tensor_tensor(gtmp[:, g, :], gtmp[:, g, :], big[:, BU + g, :],
                                            ALU.mult).then_inc(gated_ready, 1)

            def gmlp_low(m0):
                for g in range(2):
                    dve.wait_ge(mv_hi, m0 + g + 1)
                    nc.vector.tensor_tensor(mvl[:, 3 + g, :], gtmp[:, g, :], mvh[:, 3 + g, :].bitcast(F32),
                                            ALU.subtract).then_inc(mv_lo, 1)

            def centre(n, src):
                for h in range(n):
                    last = nc.vector.bn_stats(norm_stats[:, 6 * h:6 * h + 6], src(h))
                chain(last)
                for h in range(n):
                    last = nc.vector.bn_aggr(mean_var[:, 2 * h:2 * h + 2], norm_stats[:, 6 * h:6 * h + 6])
                chain(last)
                rsqrt(sm_y[:, 0:n], mean_var[:, 1:2 * n:2], 1.0, n)

            def normalise(heads, src, dst, h0=0):
                for h in range(heads):
                    last = nc.vector.tensor_scalar(dst(h), src(h), mean_var[:, 2 * (h0 + h):2 * (h0 + h) + 1],
                                                   sm_y[:, h0 + h:h0 + h + 1], ALU.subtract, ALU.mult)
                last.then_inc(onorm_ready, 1)

            def rotary(i, m, kind):
                dve.wait_ge(rot_done, i + 1)
                nc.vector.tensor_tensor(scr[:, i % 2, :], banks[i % 2][:, :], y[:, 2 * kind + 1, :], ALU.mult)
                chain(nc.vector.tensor_tensor(big[:, m, :], big[:, m, :], y[:, 2 * kind, :], ALU.mult))
                nc.vector.tensor_tensor(big[:, m, :], big[:, m, :], scr[:, i % 2, :], ALU.add).then_inc(rotated, 1)

            def beside_retention(s):
                if s == 8:
                    dve.wait_ge(tables, 16 * 6)
                if s in ROTARY:
                    rotary(ROT_N[s], *ROTARY[s])

            def retention(m0):
                i = 0
                for h in range(RET_H):
                    for jt in range(TB):
                        w = S - jt * P
                        dve.wait_ge(ret_scores, i + 1)
                        if h >= 2:
                            dve.wait_ge(ret_pv, h - 1)
                        nc.vector.tensor_tensor(y[:, 4 * (h % 2) + jt, 0:w], banks[i % 4][:, 0:w],
                                                tab[:, h * S:h * S + w], ALU.mult).then_inc(ret_decayed, 1)
                        i += 1
                dve.wait_ge(ret_pv, RET_H)
                centre(TB * RET_H, lambda h: banks[4 + h // 4][:, (h % 4) * P:(h % 4 + 1) * P])
                for b in range(TB + 1):
                    if b < TB:
                        ge(dve, ot_done, RET_BLOCK0 + b - 1 if b >= 2 else 0)
                        normalise(RET_H, lambda h: banks[4 + b][:, h * P:(h + 1) * P],
                                  lambda h: onorm[:, b % 2, h * P:(h + 1) * P], RET_H * b)
                    if b:
                        gated(b - 1, m0, [banks[4 + b - 1]], RG, gtmp[:, (b - 1) % 2:(b - 1) % 2 + 1, :], RET_BLOCK0,
                              2 * LAYERS)

            def gated(b, m0, src, gate, dst, block0, g0):
                n = 4 * len(src)
                dve.wait_ge(mixer_gates, RET_H if n == 4 else RET_H + n)
                dve.wait_ge(ot_done, block0 + b + 1)
                for i, bank in enumerate(src):
                    if i + 1 == len(src) and i:
                        chain(last)
                    last = nc.vector.tensor_tensor(dst[:, i, :].rearrange("p (a c) -> p a c", c=P),
                                                   bank[:, :].rearrange("p (a c) -> p a c", c=P),
                                                   big[:, gate + 4 * i:gate + 4 * i + 4, b * P:(b + 1) * P], ALU.mult)
                last.then_inc(gated_ready, 1)
                dve.wait_ge(mv_hi, m0 + b + 1)
                at = (slice(None), slice(0, n), slice(b * P, (b + 1) * P))
                nc.vector.tensor_tensor(mvl[at], dst.rearrange("p a (b c) -> p (a b) c", c=P),
                                        mvh[at].bitcast(F32), ALU.subtract).then_inc(mv_lo, 1)

            def beside_gla(s):
                if s == GA:
                    dve.wait_ge(bank_free, lin["b_mix_in1"].e0 + GA + 1)
                    nc.vector.memset(big[32:33, GA, :], 1.0).then_inc(alow_ready, 1)
                if s == GLA_LN:
                    for b in range(TB):
                        dve.wait_ge(z_soft, b + 1)
                        nc.vector.scalar_tensor_tensor(out=scr[:, b, :], in0=banks[FREE[b]][:, :], scalar=0.0,
                                                       in1=scr[:, 4 + b, :], op0=ALU.min,
                                                       op1=ALU.subtract).then_inc(log_a, 1)
                for h in GLA_B.get(s, ()):
                    q, k, dec = big[:, GQ + h, :], big[:, GK + h, :], decay[:, 8 * h:8 * h + 8]
                    dve.wait_ge(b_exp, h + 1)
                    nc.vector.tensor_copy(dec, scr[:, 8, GLA_CHUNK - 1:S:GLA_CHUNK])
                    nc.vector.scalar_tensor_tensor(out=q, in0=q, scalar=128 ** -0.5, in1=scr[:, 8, :],
                                                   op0=ALU.mult, op1=ALU.mult)
                    nc.vector.tensor_tensor(k, k, scr[:, 9, :], ALU.mult).then_inc(b_used, 1)
                    dve.wait_ge(b_used, h + 1)
                    nc.vector.tensor_tensor(y[:, h, :].rearrange("p (n c) -> p n c", c=GLA_CHUNK),
                                            k.rearrange("p (n c) -> p n c", c=GLA_CHUNK),
                                            dec.unsqueeze(2).broadcast_to([P, 8, GLA_CHUNK]),
                                            ALU.mult).then_inc(kdec_ready, 1)
                if s == min(GLA_SC):
                    dve.wait_ge(tables, 16 * 8)
                for h in GLA_SC.get(s, ()):
                    dve.wait_ge(gsc_done, h + 1)
                    nc.vector.tensor_tensor(scr[:, h, :].rearrange("p (b c) -> p b c", c=P),
                                            banks[6 + h % 2][:, :].rearrange("p (b c) -> p b c", c=P),
                                            tab[:, 128:256].unsqueeze(1).broadcast_to([P, TB, P]),
                                            ALU.mult).then_inc(gsc_masked, 1)

            def gla(m0):
                for b in range(TB):
                    for n in (2 * b, 2 * b + 1):
                        if n == 7:
                            break
                        for h in range(GLA_H):
                            dve.wait_ge(kv_done, 4 * n + 2 * (h // 2) + 2)
                            kv = banks[2 * (n % 2) + h // 2][:, (h % 2) * GLA_DV:(h % 2 + 1) * GLA_DV]
                            if n == 0:
                                nc.vector.tensor_copy(state(1, h), kv).then_inc(state_ready, 1)
                                continue
                            dve.wait_ge(state_ready, 4 * (n - 1) + h + 1)
                            if n >= 2 or n == 1:
                                ge(dve, gla_o, 4 * ((n - 1) // 2) + h + 1 if n >= 2 else 0)
                            nc.vector.scalar_tensor_tensor(out=state(n + 1, h), in0=state(n, h),
                                                           scalar=decay[:, 8 * h + n:8 * h + n + 1], in1=kv,
                                                           op0=ALU.mult, op1=ALU.add).then_inc(state_ready, 1)
                    dve.wait_ge(gla_o, 4 * (b + 1))
                    ob = [banks[4 + 2 * (b % 2)], banks[5 + 2 * (b % 2)]]
                    src = lambda h: ob[h // 2][:, (h % 2) * GLA_DV:(h % 2 + 1) * GLA_DV]
                    centre(GLA_H, src)
                    normalise(GLA_H, src, lambda h: scr[:, 4 + 2 * (b % 2) + h // 2,
                                                        (h % 2) * GLA_DV:(h % 2 + 1) * GLA_DV])
                    if b:
                        gated(b - 1, m0, [banks[4 + 2 * ((b - 1) % 2)], banks[5 + 2 * ((b - 1) % 2)]], GR,
                              scr[:, 8:10, :], GLA_BLOCK0, 2 * LAYERS + TB)
                dve.wait_ge(mv_lo, m0 + TB - 1)
                gated(TB - 1, m0, [banks[6], banks[7]], GR, scr[:, 8:10, :], GLA_BLOCK0, 2 * LAYERS + TB)

            nc.vector.memset(ones[:, :], 1.0).then_inc(ones_set, 1)
            nc.vector.memset(small[:, :], 0.0).then_inc(bank_free, len(LIN))
            update = None
            n_tables = 0
            for l in range(LAYERS):
                enter(f"a_in{l}", f"a_pre{l}", update)
                dve.wait_ge(consts, 32)
                rstd(NORM[f"a_in{l}"])
                project(f"a_in{l}", lambda s: lam(l) if s == A_LAM else None)
                m0 = lin[f"a_out{l}"].m0
                dve.wait_ge(tables, 16 * (2 * l + 2))
                attention(DIFF_ATT[l], m0)
                gmlp_low(m0 + TB)
                attention(SWA_ATT[l], m0 + TB + 2)
                rstd(NORM[f"a_out{l}"])
                enter(f"a_ffn_in{l}", f"a_pre_ffn{l}", post(f"a_post{l}"))
                rstd(NORM[f"a_ffn_in{l}"])
                ffn_in(f"a_ffn_in{l}")
                ffn_out(f"a_ffn_out{l}")
                rstd_diag(NORM[f"a_ffn_out{l}"])
                up = lin[f"a_ple_up{l}"]
                for n in range(4):
                    if n == 0:
                        dve.wait_ge(unit_done, up.u0 + 1)
                    nc.vector.tensor_copy(big[:, n, :], banks[LIN[n]][:, :]).then_inc(bank_free, 1)
                rstd_spread(NORM[f"a_ffn_out{l}"])
                add = post(f"a_post_ffn{l}")

                def update(k):
                    add(k)
                    if k == 1:
                        dve.wait_ge(unit_done, up.u0 + 2)
                        for n in range(4):
                            nc.vector.tensor_copy(big[:, 4 + n, :], banks[LIN[n]][:, :]).then_inc(bank_free, 1)

                enter(f"a_gate{l}", f"a_gate{l}", update)
                rstd(NORM[f"a_gate{l}"])
                L = lin[f"a_gate{l}"]
                for i in range(9):
                    if i < 8:
                        dve.wait_ge(unit_done, L.u0 + i + 1)
                        nc.vector.tensor_tensor(g1[:, i % 2, :], banks[LIN[i % 4]][:, :], rstd_b[:, :],
                                                ALU.mult).then_inc(bank_free, 1)
                    if i:
                        dve.wait_ge(gate_sig, 8 * l + i)
                        nc.vector.tensor_tensor(y[:, i - 1, :], s1[:, (i - 1) % 2, :], big[:, i - 1, :],
                                                ALU.mult).then_inc(z_ready, 1)
                rstd(NORM[f"a_ple{l}"])
                update = post(f"a_ple{l}")

            for l in range(LAYERS):
                enter(f"b_pre_in{l}", f"b_pre{l}", update)
                rstd(NORM[f"b_pre_in{l}"])
                ffn_in(f"b_pre_in{l}")
                ffn_out(f"b_pre_out{l}")
                enter(f"b_mix_in{l}", f"b_mix{l}", add_down(lin[f"b_pre_out{l}"]))
                rstd(NORM[f"b_mix_in{l}"])
                project(f"b_mix_in{l}", beside_gla if l else beside_retention)
                m0 = lin[f"b_mix_out{l}"].m0
                if l == 0:
                    retention(m0)
                    dve.wait_ge(vt_copied, 20)
                    attention(DIL_ATT, m0 + TB)
                else:
                    gla(m0)
                L = lin[f"b_mix_out{l}"]
                enter(f"b_post_in{l}", f"b_post{l}", add_mix(L))
                rstd(NORM[f"b_post_in{l}"])
                ffn_in(f"b_post_in{l}")
                ffn_out(f"b_post_out{l}")
                update = add_down(lin[f"b_post_out{l}"])
            for k in range(KT):
                update(k)
            rstd(NORM["final"])
            for k in range(KT):
                nc.vector.scalar_tensor_tensor(out=y[:, k, :], in0=x[:, k, :], scalar=col("final", k),
                                               in1=rstd_b[:, :], op0=ALU.mult, op1=ALU.mult).then_inc(y_ready, 1)

        @block.tensor
        def _(pe):
            def three(bank, slot, tile, k, first, last):
                hi, lo = w_hi[:, slot, tile * P:(tile + 1) * P], w_lo[:, slot, tile * P:(tile + 1) * P]
                nc.tensor.matmul(bank[:, :], hi, mvh[:, k, :], start=first, stop=False)
                nc.tensor.matmul(bank[:, :], hi, mvl[:, k, :], start=False, stop=False)
                return nc.tensor.matmul(bank[:, :], lo, mvh[:, k, :], start=False, stop=last)

            def wide(name):
                L = lin[name]
                back = [f"a_out{l}" for l in range(LAYERS)] + [f"b_mix_out{l}" for l in range(LAYERS)]

                def body(t, s):
                    slot = (L.u0 + s) % RING
                    pe.wait_ge(w_lo_ready, t * RING + L.u0 + s + 1)
                    bank = banks[BACK[s] if name in back else LIN[s % 4]]
                    if name not in back:
                        pe.wait_ge(bank_free, t * RING + L.e0 + s - 3)
                    for k in range(8):
                        last = three(bank, slot, k, k, k == 0, k == 7)
                    last.then_inc(unit_done, 1)

                return L, body

            def sum_squares(norm, k):
                pe.wait_ge(sq_ready, 8 * norm + k + 1)
                if k == 0:
                    pe.wait_ge(sq_ready, 8 * norm + 2)
                for b in range(TB):
                    last = nc.tensor.matmul(banks[STAT][:, b:b + 1], sq[:, k % 4, b * P:(b + 1) * P],
                                            ones[:, 0:1], start=(k == 0 and b == 0), stop=(k == 7),
                                            skip_group_check=True)
                    if k == KT - 1 and b == TB - 2:
                        last.then_inc(sq_used, 1)
                last.then_inc(sums_done if k == KT - 1 else sq_used, 1)

            def stats(norm, first=0):
                for k in range(first, KT):
                    sum_squares(norm, k)

            def sum_added(norm):
                pe.wait_ge(sq_used, 8 * (norm + 1))
                for b in range(TB):
                    last = nc.tensor.matmul(banks[STAT][:, b:b + 1], diag[:, b, :], ones[:, 0:1], start=True, stop=True)
                last.then_inc(sums_done, 1)

            def spread(norm):
                pe.wait_ge(diag_ready, norm + 1)
                nc.tensor.matmul(banks[BCAST][:, :], ones[:, :], diag[:, :, :].rearrange("p a b -> p (a b)"),
                                 start=True, stop=True).then_inc(bcast_done, 1)

            def from_x(name, norm, beside=None):
                L, body = wide(name)

                def product(j, k):
                    last = three(banks[LIN[j]], (L.u0 + j) % RING, k, k, k == 0, k == KT - 1)
                    if k == KT - 1:
                        last.then_inc(unit_done, 1)

                for k in range(KT - 3):
                    pe.wait_ge(mv_lo, L.m0 + k + 1)
                    for j in range(min(k, RING)):
                        product(j, k)
                    if k < RING:
                        pe.wait_ge(w_lo_ready, L.u0 + k + 1)
                        pe.wait_ge(bank_free, L.e0 + k - 3)
                        for i in range(k + 1):
                            product(k, i)
                for j in range(RING):
                    for k in range(KT - 3, KT):
                        if j == 0:
                            pe.wait_ge(mv_lo, L.m0 + k + 1)
                        product(j, k)
                    if j == 0:
                        sum_added(norm)
                    if j == 2:
                        spread(norm)
                if beside is None:
                    rest(L, body, RING)
                    return
                for s in range(RING, L.n):
                    body(0, s)
                    beside(s)

            def rest(L, body, done):
                head = (L.n - done) % RING
                for i in range(done, done + head):
                    body(0, i)
                turns = (L.n - done - head) // RING
                if turns:
                    with pe.Fori(0, turns) as t:
                        for j in range(RING):
                            body(t, done + head + j)

            def from_cat(name):
                L, body = wide(name)
                pe.wait_ge(mv_lo, L.m0 + L.moving)
                return L, body

            def down(name):
                L = lin[name]

                def body(t, s, first=False):
                    slot = (L.u0 + s) % RING
                    pe.wait_ge(w_lo_ready, t * RING + L.u0 + s + 1)
                    pe.wait_ge(mv_lo, t * RING + L.m0 + s + 1)
                    for n in range(8):
                        if first and BACK[n] in LIN:
                            pe.wait_ge(bank_free, L.e0 - 3 + LIN.index(BACK[n]))
                        last = three(banks[BACK[n]], slot, n, s % 4, first, s == FT - 1)
                    last.then_inc(unit_done, 1)

                body(0, 0, True)
                body(0, 1)
                with pe.Fori(0, (FT - 6) // RING) as t:
                    for j in range(RING):
                        body(t, 2 + j)
                for f in range(FT - 4, FT):
                    body(0, f)

            def ple_unit(l, n0):
                L = lin[f"a_ple_up{l}"]
                i = n0 // 4
                pe.wait_ge(w_lo_ready, L.u0 + i + 1)
                pe.wait_ge(p_lo, l + 1)
                for n in range(4):
                    pe.wait_ge(bank_free, L.e0 + n0 + n - 3)
                    for k in range(2):
                        last = three(banks[LIN[n]], (L.u0 + i) % RING, 2 * n + k, 4 + k, k == 0, k == 1)
                last.then_inc(unit_done, 1)

            def transpose_value(key, i):
                tiles, n0 = VT[key]
                ge(pe, vt_copied, n0 + i - 1)
                for b in range(TB):
                    last = nc.tensor.transpose(banks[6 + i % 2][:, b * P:(b + 1) * P],
                                               big[:, tiles[i], b * P:(b + 1) * P], ident[:, :])
                last.then_inc(vt_done, 1)

            def transpose_values(key, first=0):
                for i in range(first, len(VT[key][0])):
                    transpose_value(key, i)

            def attention(a):
                n, H = len(a.pairs), a.heads

                def scores(t):
                    q = a.pairs[t]
                    ge(pe, scores_scaled, a.item0 + a.comps * (t - 1))
                    if q.qb == 0:
                        pe.wait_ge(keys_masked, a.keys0 + q.masked)
                    for c, (lhs, rhs) in enumerate(q.parts):
                        nc.tensor.matmul(banks[2 * (t % 2) + c][:, 0:q.nkb * P], lhs, rhs, start=True,
                                         stop=True).then_inc(scores_done, 1)

                scores(0)
                for t in range(a.steps()):
                    if t + 1 < n:
                        scores(t + 1)
                    if 1 <= t <= n:
                        r = t - 1
                        q = a.pairs[r]
                        if a.comps == 2:
                            pe.wait_ge(probs_ready, a.probs0 + r + 1)
                            src = comb[:, r % 2, :]
                        else:
                            pe.wait_ge(exp_done, a.item0 + r + 1)
                            src = expo[:, 2 * (r % 2), :]
                        ge(pe, pt_copied, a.pair0 + r - 1)
                        for kb in range(q.nkb):
                            last = nc.tensor.transpose(banks[4 + r % 2][:, kb * P:(kb + 1) * P],
                                                       src[:, kb * P:(kb + 1) * P], ident[:, :])
                        last.then_inc(pt_done, 1)
                    if 2 <= t <= n + 1:
                        r = t - 2
                        q = a.pairs[r]
                        pe.wait_ge(pt_copied, a.pair0 + r + 1)
                        if r == 0 and a.kind == "diff":
                            pe.wait_ge(vt_copied, 6 * (a.layer + 1))
                        if q.h == 0 and q.qb >= 2:
                            pe.wait_ge(mv_lo, a.m0 + q.qb - 1)
                        elif q.h == 0 and a.kind == "swa":
                            pe.wait_ge(mv_lo, a.m0 - 2 - TB + q.qb + 3)
                        for kb in range(q.nkb):
                            last = nc.tensor.matmul(banks[6 + q.qb % 2][:, q.h * 64:(q.h + 1) * 64],
                                                    ptile[:, r % 2, kb * P:(kb + 1) * P], q.v(q.kb0 + kb),
                                                    start=(kb == 0), stop=(kb == q.nkb - 1))
                        last.then_inc(pv_done, 1)
                    if a.kind == "diff" and t == n + 1:
                        gmlp(a.layer)
                    b = a.due(t, 6)
                    if b is not None:
                        transpose_out(a.block0 + b, [banks[6 + b % 2]], a.tiles, onorm[:, b % 2:b % 2 + 1, :])

            def transpose_out(block_n, dst, tiles, src):
                pe.wait_ge(onorm_ready, block_n + 1)
                for m in range(tiles):
                    last = nc.tensor.transpose(dst[m // 4][:, (m % 4) * P:(m % 4 + 1) * P],
                                               src[:, m // 4, (m % 4) * P:(m % 4 + 1) * P], ident[:, :])
                last.then_inc(ot_done, 1)

            def gmlp(l):
                pe.wait_ge(tables, 16 * (2 * l + 2))
                pe.wait_ge(vn_ready, l + 1)
                for g in range(4):
                    p0 = 64 * (g % 2)
                    for b in range(TB):
                        last = nc.tensor.matmul(banks[1 + 2 * (g // 2)][p0:p0 + 64, b * P:(b + 1) * P],
                                                tok(BV + g // 2, b, p0, 64), tab[:, 512 + g * P:512 + (g + 1) * P],
                                                start=True, stop=True)
                    if g % 2:
                        last.then_inc(mixed_done, 1)

            def beside_a(l, s):
                if s == min(A_VT):
                    pe.wait_ge(consts, 32)
                if s in A_VT:
                    i = A_VT[s]
                    pe.wait_ge(bank_free, lin[f"a_in{l}"].e0 + VT[f"a{l}"][0][i] + 1)
                    transpose_value(f"a{l}", i)

            def beside_retention(s):
                L = lin["b_mix_in0"]
                if s in ROTARY:
                    (m, kind), i = ROTARY[s], ROT_N[s]
                    pe.wait_ge(bank_free, L.e0 + m + 1)
                    ge(pe, rotated, i - 1)
                    nc.tensor.matmul(banks[i % 2][:, :], rot[:, kind, :], big[:, m, :], start=True,
                                     stop=True).then_inc(rot_done, 1)
                if s in RET_VT:
                    pe.wait_ge(bank_free, L.e0 + RV + RET_VT[s] + 1)
                    transpose_value("b0", RET_VT[s])

            def retention():
                pe.wait_ge(rotated, 16)
                for h in range(RET_H + 1):
                    if h < RET_H:
                        for jt in range(TB):
                            i = TB * h + jt
                            ge(pe, ret_decayed, i - 3)
                            nc.tensor.matmul(banks[i % 4][:, 0:S - jt * P], big[:, RK + h, jt * P:(jt + 1) * P],
                                             big[:, RQ + h, jt * P:S], start=True, stop=True).then_inc(ret_scores, 1)
                    if h == 1:
                        pe.wait_ge(vt_copied, 20)
                    if h:
                        r = h - 1
                        pe.wait_ge(ret_decayed, TB * (r + 1))
                        for b in range(TB):
                            for jt in range(b + 1):
                                last = nc.tensor.matmul(banks[4 + b][:, r * P:(r + 1) * P],
                                                        y[:, 4 * (r % 2) + jt, (b - jt) * P:(b - jt + 1) * P],
                                                        tok(RV + r, jt, 0, P), start=(jt == 0), stop=(jt == b))
                        last.then_inc(ret_pv, 1)
                for b in range(TB):
                    transpose_out(RET_BLOCK0 + b, [banks[4 + b]], 4, onorm[:, b % 2:b % 2 + 1, :])

            def beside_gla(s):
                L = lin["b_mix_in1"]
                if s == GLA_Z:
                    pe.wait_ge(tables, 16 * 8)
                    pe.wait_ge(alow_ready, 1)
                    for b in range(TB):
                        nc.tensor.matmul(banks[FREE[b]][:, :], big[0:33, GA, b * P:(b + 1) * P],
                                         tab[0:33, 256:768], start=True, stop=True).then_inc(z_done, 1)
                if s == GLA_SUM:
                    pe.wait_ge(log_a, TB)
                    for h in range(GLA_H):
                        for b in range(TB):
                            last = nc.tensor.matmul(banks[FREE[h]][:, b * P:(b + 1) * P],
                                                    scr[:, b, h * P:(h + 1) * P], tab[:, 0:128], start=True, stop=True)
                        last.then_inc(b_done, 1)
                for h in GLA_SC.get(s, ()):
                    pe.wait_ge(b_exp, GLA_H)
                    pe.wait_ge(kdec_ready, h + 1)
                    ge(pe, kt_copied, h - 1)
                    for b in range(TB):
                        last = nc.tensor.transpose(banks[h % 2][:, b * P:(b + 1) * P], y[:, h, b * P:(b + 1) * P],
                                                   ident[:, :])
                    last.then_inc(kt_done, 1)
                    ge(pe, gsc_masked, h - 1)
                    for b in range(TB):
                        last = nc.tensor.matmul(banks[6 + h % 2][:, b * P:(b + 1) * P],
                                                big[:, GK + h, b * P:(b + 1) * P], big[:, GQ + h, b * P:(b + 1) * P],
                                                start=True, stop=True)
                    last.then_inc(gsc_done, 1)
                if s >= GLA_VT:
                    i = s - GLA_VT
                    pe.wait_ge(bank_free, L.e0 + GV + i + 1)
                    ge(pe, gsc_masked, min(GLA_H, i + 3))
                    transpose_value("b1", i)

            def gla():
                pe.wait_ge(kt_copied, GLA_H)
                pe.wait_ge(gsc_masked, GLA_H)
                for b in range(TB + 1):
                    if b < TB:
                        for n in (2 * b, 2 * b + 1):
                            if n == 7:
                                break
                            p0 = 64 * (n % 2)
                            ge(pe, state_ready, 4 * (n - 1))
                            for h in range(GLA_H):
                                nc.tensor.matmul(banks[2 * (n % 2) + h // 2][:, (h % 2) * GLA_DV:(h % 2 + 1) * GLA_DV],
                                                 y[p0:p0 + 64, 4 + h, b * P:(b + 1) * P],
                                                 big[p0:p0 + 64, GV + 2 * h:GV + 2 * h + 2, b * P:(b + 1) * P],
                                                 start=True, stop=True).then_inc(kv_done, 1)
                        if b >= 2:
                            pe.wait_ge(gated_ready, 2 * LAYERS + TB + b - 1)
                        for h in range(GLA_H):
                            bank = banks[4 + 2 * (b % 2) + h // 2]
                            c0 = (h % 2) * GLA_DV
                            last = nc.tensor.matmul(bank[:, c0:c0 + GLA_DV], scr[:, h, b * P:(b + 1) * P],
                                                    big[:, GV + 2 * h:GV + 2 * h + 2, b * P:(b + 1) * P],
                                                    start=True, stop=False, skip_group_check=True)
                            for n in (2 * b, 2 * b + 1):
                                if n == 0:
                                    continue
                                pe.wait_ge(state_ready, 4 * (n - 1) + h + 1)
                                p0 = 64 * (n % 2)
                                last = nc.tensor.matmul(bank[p0:p0 + 64, c0:c0 + GLA_DV],
                                                        big[:, GQ + h, n * 64:(n + 1) * 64], state(n, h),
                                                        start=False, stop=True, skip_group_check=True)
                            last.then_inc(gla_o, 1)
                    if b:
                        r = b - 1
                        transpose_out(GLA_BLOCK0 + r, [banks[4 + 2 * (r % 2)], banks[5 + 2 * (r % 2)]], 8,
                                      scr[:, 4 + 2 * (r % 2):6 + 2 * (r % 2), :])

            pe.wait_ge(ones_set, 1)
            for l in range(LAYERS):
                from_x(f"a_in{l}", NORM[f"a_in{l}"], lambda s: beside_a(l, s))
                pe.wait_ge(bank_free, lin[f"a_in{l}"].e0 + 18)
                transpose_values(f"a{l}", len(A_VT))
                attention(DIFF_ATT[l])
                attention(SWA_ATT[l])
                L, body = from_cat(f"a_out{l}")
                for i in range(8):
                    body(0, i)
                    if i >= 2:
                        sum_squares(NORM[f"a_out{l}"], i - 2)
                stats(NORM[f"a_out{l}"], 6)
                spread(NORM[f"a_out{l}"])
                from_x(f"a_ffn_in{l}", NORM[f"a_ffn_in{l}"])
                down(f"a_ffn_out{l}")
                stats(NORM[f"a_ffn_out{l}"])
                ple_unit(l, 0)
                spread(NORM[f"a_ffn_out{l}"])
                ple_unit(l, 4)
                from_x(f"a_gate{l}", NORM[f"a_gate{l}"])
                stats(NORM[f"a_ple{l}"])
                spread(NORM[f"a_ple{l}"])
            for l in range(LAYERS):
                from_x(f"b_pre_in{l}", NORM[f"b_pre_in{l}"])
                down(f"b_pre_out{l}")
                from_x(f"b_mix_in{l}", NORM[f"b_mix_in{l}"], beside_gla if l else beside_retention)
                pe.wait_ge(bank_free, lin[f"b_mix_in{l}"].e0 + lin[f"b_mix_in{l}"].n)
                if l == 0:
                    transpose_values("b0", RET_H)
                    retention()
                    pe.wait_ge(gated_ready, 2 * LAYERS + TB)
                    attention(DIL_ATT)
                else:
                    pe.wait_ge(vt_copied, 28)
                    gla()
                L, body = from_cat(f"b_mix_out{l}")
                for i in range(8):
                    body(0, i)
                from_x(f"b_post_in{l}", NORM[f"b_post_in{l}"])
                down(f"b_post_out{l}")
            stats(NORM["final"])
            spread(NORM["final"])


def tiles_of(w):
    k, n = w.shape
    return w.reshape(k // P, P, n // P, P).transpose(2, 1, 0, 3).reshape(n // P, P, k)


def weight_units(i):
    out = []

    def ffn(gate, up, down):
        g, u = tiles_of(gate), tiles_of(up)
        out.append(np.stack([g, u], axis=1).reshape(-1, P, UNIT))
        out.append(down.reshape(FT, P, D))

    swa0 = 2304 - 256 - 384
    order = [h for t in range(3) for h in (t, 3 + t)]
    for l in range(LAYERS):
        w = i["w_in"][l]
        q = w[:, swa0:swa0 + 384].reshape(D, 6, 64)[:, order].reshape(D, 384)
        out.append(tiles_of(np.concatenate([w[:, :swa0], q, w[:, swa0 + 384:]], axis=1)))
        out.append(tiles_of(i["w_out"][l]))
        ffn(i["w_ffn_in"][l][:, :FT * P], i["w_ffn_in"][l][:, FT * P:], i["w_ffn_out"][l])
        up = tiles_of(i["w_ple_up"][l])
        out.append(up.reshape(2, 4, P, 256).transpose(0, 2, 1, 3).reshape(2, P, UNIT))
        out.append(tiles_of(i["w_ple_gate"][l]))
    for l in range(LAYERS):
        ffn(i["ffn_pre_w_gate_2"][l], i["ffn_pre_w_up_2"][l], i["ffn_pre_w_down_2"][l])
        if l == 0:
            out.append(tiles_of(i["ab_w_in_2"][0]))
            out.append(tiles_of(i["ab_w_out_2"][0]))
        else:
            w = i["gla_w_in_2"][0]
            a = 2 * 512 + 2 * 1024
            pad = np.zeros((D, 25 * P - w.shape[1]), w.dtype)
            out.append(tiles_of(np.concatenate([w[:, :1024], w[:, a:], pad, w[:, 1024:a]], axis=1)))
            out.append(tiles_of(i["gla_w_out_2"][0]))
        ffn(i["ffn_post_w_gate_2"][l], i["ffn_post_w_up_2"][l], i["ffn_post_w_down_2"][l])
    return np.ascontiguousarray(np.concatenate(out, axis=0))


def column_table(i):
    at, n = column_layout()
    t = np.zeros((P, n), np.float32)
    for l in range(LAYERS):
        for name, key in (("a_pre", "g_pre_mix"), ("a_post", "g_post_mix"), ("a_pre_ffn", "g_pre_ffn"),
                          ("a_post_ffn", "g_post_ffn"), ("a_gate", "g_ple_gate"), ("a_ple", "g_ple_post"),
                          ("b_pre", "ffn_pre_norm_2"), ("b_mix", "mix_norm_2"), ("b_post", "ffn_post_norm_2")):
            t[:, at[f"{name}{l}"]:at[f"{name}{l}"] + 8] = i[key][l].reshape(8, P).T
        t[:, at[f"g_sub{l}"]] = np.tile(i["g_diff_sub"][l], 2)
        t[:, at[f"sinks{l}"]:at[f"sinks{l}"] + 6] = i["swa_sinks"][l][None]
        lam = np.concatenate([i[k][l] for k in ("lam_q1", "lam_k1", "lam_q2", "lam_k2")])
        t[:, at[f"lam{l}"]:at[f"lam{l}"] + 128] = lam[None]
    diff_slopes, swa_slopes = slopes()
    for c in range(2 * DIFF_H):
        p0 = 32 * (c % 4)
        t[p0:p0 + 32, at["diff_rows"] + c] = np.float32(32 ** -0.5) / diff_slopes[c // 2]
    for h in range(SWA_H):
        p0 = 64 * (h // 3)
        t[p0:p0 + 64, at["swa_rows"] + h] = np.float32(0.125) / swa_slopes[h]
    for c in range(2):
        t[64 * c:64 * c + 64, at["dil_rows"] + c] = 1.0
    t[:, at["final"]:at["final"] + 8] = i["final_norm_2"].reshape(8, P).T
    return t


def gmlp_table(i):
    out = []
    for l in range(LAYERS):
        w = i["w_spatial"][l].transpose(2, 0, 1).reshape(P, 4 * P)
        bias = np.repeat(i["b_spatial"][l].reshape(2, 2, 1, P), 64, axis=2).reshape(2, P, P)
        out.append(np.concatenate([np.tile(i["gmlp_ln_g"][l], (P, 1)), np.tile(i["gmlp_ln_b"][l], (P, 1)), w,
                                   bias.transpose(1, 0, 2).reshape(P, 2 * P)], axis=1))
    return np.ascontiguousarray(np.stack(out))


def constants():
    p = np.arange(P)[:, None]
    diff = -np.abs(p - (np.arange(896)[None] - 384)).astype(np.float32)
    dist = np.abs(p - (np.arange(384)[None] - P)).astype(np.float32)
    swa = np.where(dist <= 128, -dist, NEG)
    rel = np.arange(S)[None] - p
    log_g = np.log(1.0 - 2.0 ** (-5.0 - np.arange(4, dtype=np.float32))).astype(np.float32)
    ret = np.concatenate([np.where(rel >= 0, np.exp(g * np.maximum(rel, 0)), 0.0) * 128 ** -0.5 for g in log_g],
                         axis=1)
    d = p - (np.arange(512)[None] - 384)
    count = ((d <= 128) * 1 + (d % 4 == 0) * 1 + (d % 16 == 0) * 1) * (d >= 0)
    dil = np.where(count > 0, np.log(np.maximum(count, 1)) * 8.0, NEG)
    pos = np.arange(S, dtype=np.float32)
    f_ret = np.float32(10000.0) ** (-np.linspace(0.0, 1.0, 64, dtype=np.float32))
    f_dil = np.float32(500000.0) ** (-np.arange(0, 16, 2, dtype=np.float32) / np.float32(16))
    a_ret = f_ret[np.arange(P) % 64][:, None] * pos[None]
    a_dil = np.zeros((P, S), np.float32)
    rot = np.zeros((P, 2, P), np.float32)
    for m in range(64):
        rot[m + 64, 0, m], rot[m, 0, m + 64] = -1.0, 1.0
    for h in range(2):
        for m in range(8):
            lo, hi = 64 * h + m, 64 * h + m + 8
            a_dil[lo] = a_dil[hi] = f_dil[m] * pos
            rot[hi, 1, lo], rot[lo, 1, hi] = -1.0, 1.0
    rotary = np.stack([np.cos(a_ret), np.sin(a_ret), np.cos(a_dil), np.sin(a_dil)], axis=1)
    c = np.arange(P)[None]
    causal = ((p <= c) & (p // 64 == c // 64)).astype(np.float32)
    gla = np.concatenate([causal / 16, causal], axis=1)
    f = lambda a: np.ascontiguousarray(a, dtype=np.float32)
    return {"dist": f(np.concatenate([diff, swa], axis=1)), "ident": f(np.eye(P)), "rot": f(rot), "rotary": f(rotary),
            "ret_dil": f(np.concatenate([ret, dil], axis=1)), "gla": f(gla)}


def kernel(**inputs):
    import concourse.bacc as bacc
    from concourse.bass_utils import run_bass_kernel_spmd

    i = {k: np.asarray(v) for k, v in inputs.items()}
    c = constants()
    wa2 = np.zeros((33, 512), np.float32)
    wa2[0:16], wa2[32] = i["gla_w_a2_2"][0], i["gla_b_a_2"][0]
    arrays = {
        "x": np.ascontiguousarray(i["x"][0].T.reshape(KT, P, S).transpose(1, 0, 2)),
        "p": np.ascontiguousarray(i["p"][:, 0].transpose(0, 2, 1).reshape(LAYERS, 2, P, S).transpose(0, 2, 1, 3)),
        "weights": weight_units(i), "cols": column_table(i), "gmlp": gmlp_table(i),
        "dist": c["dist"], "ident": c["ident"], "rot": c["rot"],
        "rotary": c["rotary"], "ret_dil": c["ret_dil"], "gla": c["gla"], "wa2": wa2,
    }
    nc = bacc.Bacc("TRN2", target_bir_lowering=False, num_devices=1)
    args = [nc.dram_tensor(f"in_{k}", a.shape, mybir.dt.from_np(a.dtype), kind="ExternalInput").ap()
            for k, a in arrays.items()]
    out = nc.dram_tensor("out_y", (P, KT, S), F32, kind="ExternalOutput").ap()
    program(nc, *args, out)
    r = run_bass_kernel_spmd(nc, [{f"in_{k}": a for k, a in arrays.items()}], core_ids=[0])
    y = r.results[0]["out_y"]
    return np.ascontiguousarray(y.transpose(1, 0, 2).reshape(D, S).T)[None]
```

```python
import math
from contextlib import ExitStack

import numpy as np

import concourse.bass as bass
from concourse import mybir

F32 = mybir.dt.float32
F32R = mybir.dt.float32r
I32 = mybir.dt.int32
ACT = mybir.ActivationFunctionType
ALU = mybir.AluOpType
AX = mybir.AxisListType

P = 128
D = 1024
S = 512
KT = D // P
TB = S // P
EPS = 1e-6
NEG = -1e30
FT = 2816 // P
LAYERS = 2
RING = 4
UNIT = 8 * P

DIFF_H, SWA_H, DIL_H, RET_H, GLA_H = 6, 6, 8, 4, 4
GLA_CHUNK = 64
GLA_DV = 256
AQ, AK, AV, BU, BV, CQ, CK, CV = 0, 3, 6, 9, 11, 13, 16, 17
RQ, RK, RV, RG, DQ, DK, DV = 0, 4, 8, 12, 16, 20, 24
GQ, GK, GA, GV, GR = 0, 4, 8, 9, 17
STAT, BCAST = 0, 1
LIN = (2, 3, 4, 5)
BACK = (2, 0, 3, 4, 5, 1, 6, 7)


def slopes():
    k = np.arange(1, 13, dtype=np.float32)
    s = np.exp2(-8.0 * k / 12)
    return s[6:], s[:6]


def linears():
    out = []
    for l in range(LAYERS):
        out += [(f"a_in{l}", 18, 18, 8), (f"a_out{l}", 8, 0, 10), (f"a_ffn_in{l}", 2 * FT, 2 * FT, 8),
                (f"a_ffn_out{l}", FT, 0, FT), (f"a_ple_up{l}", 2, 8, 0), (f"a_gate{l}", 8, 8, 8)]
    for l in range(LAYERS):
        n, cat = ((28, 8), (25, 4))[l]
        out += [(f"b_pre_in{l}", 2 * FT, 2 * FT, 8), (f"b_pre_out{l}", FT, 0, FT),
                (f"b_mix_in{l}", n, n, 8), (f"b_mix_out{l}", 8, 0, cat),
                (f"b_post_in{l}", 2 * FT, 2 * FT, 8), (f"b_post_out{l}", FT, 0, FT)]
    return out


class Linear:

    def __init__(self, n, u0, e0, m0, moving):
        self.n, self.u0, self.e0, self.m0, self.moving = n, u0, e0, m0, moving


def plan():
    u, e, m, out = 0, len(LIN), 0, {}
    for name, n, banks, moving in linears():
        out[name] = Linear(n, u, e, m, moving)
        u, e, m = u + n, e + banks, m + moving
    return out, u


def column_layout():
    at, n = {}, 0
    for name in ("a_pre", "a_post", "a_pre_ffn", "a_post_ffn", "a_gate", "a_ple", "b_pre", "b_mix", "b_post"):
        for l in range(LAYERS):
            at[f"{name}{l}"] = n
            n += 8
    at["final"] = n
    n += 8
    for name, w in (("diff_rows", 2 * DIFF_H), ("swa_rows", SWA_H), ("dil_rows", 2)):
        at[name] = n
        n += w
    for l in range(LAYERS):
        for name, w in (("g_sub", 1), ("sinks", SWA_H), ("lam", 4 * 32)):
            at[f"{name}{l}"] = n
            n += w
    return at, n


def program(nc, x_in, p_in, weights, cols_in, gmlp_in, dist_in, ident_in, rot_in, rotary_in,
            ret_dil_in, gla_in, wa2_in, y_out):
    lin, UNITS = plan()
    col_at, NCOL = column_layout()

    with ExitStack() as ctx:
        def sb(name, shape, dt=F32):
            return ctx.enter_context(nc.sbuf_tensor(name, shape, dt))

        def sem(name):
            return ctx.enter_context(nc.semaphore(name))

        x = sb("x", [P, KT, S])
        mvh = sb("mvh", [P, KT, S], F32R)
        mvl = sb("mvl", [P, KT, S], F32R)
        big = sb("big", [P, 28, S])
        y = sb("y", [P, KT, S])
        w_raw = sb("w_raw", [P, RING, UNIT])
        w_hi = sb("w_hi", [P, RING, UNIT], F32R)
        w_lo = sb("w_lo", [P, RING, UNIT], F32R)
        tab = sb("tab", [P, 2560])
        scr = sb("scr", [P, 10, S])
        cols = sb("cols", [P, NCOL])
        ident = sb("ident", [P, P])
        ones = sb("ones", [P, P])
        rot = sb("rot", [P, 2, P])
        rstd_b = sb("rstd_b", [P, S])
        diag = sb("diag", [P, TB, P])
        small = sb("small", [P, 256])

        g1, u1, s1 = scr[:, 0:2, :], scr[:, 2:4, :], scr[:, 4:6, :]
        sq = scr[:, 6:10, :]
        scaled, expo = y[:, 0:4, :], y[:, 4:8, :]
        comb, ptile, onorm, osq = scr[:, 0:2, :], scr[:, 2:4, :], scr[:, 4:6, :], scr[:, 6, :]
        gtmp = scr[:, 7:9, :]
        sm_x, sm_t, sm_y = small[:, 0:16], small[:, 16:32], small[:, 32:48]
        neg_max, row_sum = small[:, 48:64], small[:, 64:80]
        inv = small[:, 80:96]
        lam_s = small[:, 96:104]
        stats6 = small[:, 104:128]
        mean_var = small[:, 200:232]
        shift = diag[:, 1, 0:16]
        osum, orstd, o_v, o_t = (small[:, 232 + 6 * i:238 + 6 * i] for i in range(4))
        norm_stats = diag[:, 0, 0:96]
        neg_sinks = small[:, 144:144 + SWA_H]
        sink_c = small[:, 160:168]
        decay = small[:, 168:200]

        banks = [ctx.enter_context(nc.psum_tensor(f"bank{i}", [P, 512], F32)) for i in range(8)]

        x_loaded, p_loaded = [sem(f"x_loaded{i}") for i in range(4)], sem("p_loaded")
        cols_loaded = sem("cols_loaded")
        tables, consts = sem("tables"), sem("consts")
        out_stored = sem("out_stored")
        w_loaded = [sem(f"w_loaded{i}") for i in range(RING)]
        w_hi_ready, w_lo_ready = sem("w_hi_ready"), sem("w_lo_ready")
        unit_done = sem("unit_done")
        mv_free = sem("mv_free")
        out_done = sem("out_done")
        bank_free = sem("bank_free")
        mv_hi, mv_lo = sem("mv_hi"), sem("mv_lo")
        x_ready = sem("x_ready")
        y_ready = sem("y_ready")
        ones_set = sem("ones_set")
        dve_chain, act_chain = sem("dve_chain"), sem("act_chain")
        sq_ready, sq_used, sums_done = sem("sq_ready"), sem("sq_used"), sem("sums_done")
        diag_ready, bcast_done = sem("diag_ready"), sem("bcast_done")
        silu_done, hidden_ready = sem("silu_done"), sem("hidden_ready")
        p_hi, p_lo = sem("p_hi"), sem("p_lo")
        gate_sig, z_ready = sem("gate_sig"), sem("z_ready")
        vt_done, vt_copied = sem("vt_done"), sem("vt_copied")
        scores_done, scores_scaled, exp_done = sem("scores_done"), sem("scores_scaled"), sem("exp_done")
        probs_ready, pt_done, pt_copied = sem("probs_ready"), sem("pt_done"), sem("pt_copied")
        pv_done = sem("pv_done")
        osq_sums, osq_rstd = sem("osq_sums"), sem("osq_rstd")
        pool_chain = sem("pool_chain")
        osq_ready, onorm_ready, ot_done = sem("osq_ready"), sem("onorm_ready"), sem("ot_done")
        centred = sem("centred")
        gated_ready, mixer_gates = sem("gated_ready"), sem("mixer_gates")
        lam_sum, lam_exp = sem("lam_sum"), sem("lam_exp")
        sink_sum, sink_exp = sem("sink_sum"), sem("sink_exp")
        keys_masked = sem("keys_masked")
        vn_ready, mixed_done = sem("vn_ready"), sem("mixed_done")
        rot_done, rotated = sem("rot_done"), sem("rotated")
        ret_scores, ret_decayed, ret_pv = sem("ret_scores"), sem("ret_decayed"), sem("ret_pv")
        alow_ready, z_done, z_soft, log_a = sem("alow_ready"), sem("z_done"), sem("z_soft"), sem("log_a")
        b_done, b_exp, b_used, kdec_ready = sem("b_done"), sem("b_exp"), sem("b_used"), sem("kdec_ready")
        kt_done, kt_copied = sem("kt_done"), sem("kt_copied")
        gsc_done, gsc_masked = sem("gsc_done"), sem("gsc_masked")
        kv_done, state_ready, gla_o = sem("kv_done"), sem("state_ready"), sem("gla_o")

        def ge(eng, s, v):
            if not isinstance(v, int) or v > 0:
                eng.wait_ge(s, v)

        def unit_loop(eng, n, body, tail=0):
            head = (n - tail) % RING
            for i in range(head):
                body(0, i)
            turns = (n - tail - head) // RING
            if turns:
                with eng.Fori(0, turns) as t:
                    for j in range(RING):
                        body(t, head + j)
            for i in range(n - tail, n):
                body(0, i)

        class Chain:

            def __init__(self, eng, s):
                self.eng, self.s, self.n = eng, s, 0

            def __call__(self, ins):
                ins.then_inc(self.s, 1)
                self.n += 1
                self.eng.wait_ge(self.s, self.n)

        def inverse_root(eng, chain, out, src, scale, v, t):
            chain(eng.tensor_scalar(v, src, scale, EPS, ALU.mult, ALU.add))
            chain(eng.tensor_scalar(out.bitcast(I32), v.bitcast(I32), -0.5, float(0x5F3759DF), ALU.mult, ALU.add))
            for _ in range(3):
                if eng is nc.vector:
                    chain(eng.scalar_tensor_tensor(out=t, in0=out, scalar=-0.5, in1=out, op0=ALU.mult, op1=ALU.mult))
                    chain(eng.tensor_tensor(t, t, v, ALU.mult))
                    chain(eng.scalar_tensor_tensor(out=out, in0=t, scalar=1.5, in1=out, op0=ALU.add, op1=ALU.mult))
                else:
                    chain(eng.tensor_tensor(t, out, out, ALU.mult))
                    chain(eng.tensor_tensor(t, t, v, ALU.mult))
                    chain(eng.tensor_scalar(t, t, -0.5, 1.5, ALU.mult, ALU.add))
                    chain(eng.tensor_tensor(out, out, t, ALU.mult))

        def col(name, k=0, n=1):
            return cols[:, col_at[name] + k:col_at[name] + k + n]

        diff_slopes, swa_slopes = slopes()

        class Pair:
            pass

        def tok(tile, tb, c0, n):
            return big[:, tile, tb * P + c0:tb * P + c0 + n]

        def state(n, h):
            return y[:, 2 * (n % 2) + h // 2, (h % 2) * GLA_DV:(h % 2 + 1) * GLA_DV]

        diff_dist, swa_dist = tab[:, 1280:2176], tab[:, 2176:2560]
        logc = tab[:, 2048:2560]

        diff_keys = [big[:, 18 + i, :] for i in range(10)] + [scr[:, 7, :], scr[:, 8, :]]
        swa_keys = [scr[:, 9, :]] + [big[:, AK + i, :] for i in range(3)] + diff_keys[0:2]

        def diff_pairs():
            out = []
            for qb in range(TB):
                for h in range(DIFF_H):
                    q = Pair()
                    q.qb, q.h, q.kb0, q.nkb = qb, h, 0, TB
                    q.parts = []
                    for c in range(2):
                        q.parts.append((big[:, AQ + h // 2, qb * P:(qb + 1) * P], diff_keys[2 * h + c]))
                    q.masked = 2 * h + 2
                    q.bias, q.scale = diff_dist[:, 384 - qb * P:896 - qb * P], float(diff_slopes[h])
                    q.v = lambda kb, h=h: tok(AV + h // 2, kb, 64 * (h % 2), 64)
                    q.first = 3e38
                    out.append(q)
            return out

        def swa_pairs(l):
            out = []
            for qb in range(TB):
                for h in range(SWA_H):
                    q = Pair()
                    kv, t = h // 3, h % 3
                    kb1 = min(TB, qb + 2)
                    q.qb, q.h, q.kb0 = qb, h, max(0, qb - 1)
                    q.nkb = kb1 - q.kb0
                    q.parts = [(big[:, CQ + t, qb * P:(qb + 1) * P], swa_keys[h][:, q.kb0 * P:kb1 * P])]
                    q.masked = h + 1
                    c0 = (q.kb0 - qb + 1) * P
                    q.bias, q.scale = swa_dist[:, c0:c0 + q.nkb * P], float(swa_slopes[h])
                    q.v = lambda kb, kv=kv: tok(CV, kb, 64 * kv, 64)
                    q.first = neg_sinks[:, h:h + 1]
                    out.append(q)
            return out

        def dil_pairs():
            out = []
            for qb in range(TB):
                for h in range(DIL_H):
                    q = Pair()
                    q.qb, q.h, q.kb0, q.nkb = qb, h, 0, qb + 1
                    q.parts = [(big[:, DQ + h // 2, qb * P:(qb + 1) * P], big[:, RQ + h, 0:(qb + 1) * P])]
                    q.masked = h + 1
                    q.bias, q.scale = logc[:, 384 - qb * P:512], 0.125
                    q.v = lambda kb, h=h: tok(DV + h // 2, kb, 64 * (h % 2), 64)
                    q.first = 3e38
                    out.append(q)
            return out

        class Attention:

            def __init__(self, pairs, heads, comps, tile0, item0, pair0, block0):
                self.pairs, self.heads, self.comps, self.tile0 = pairs, heads, comps, tile0
                self.item0, self.pair0, self.block0 = item0, pair0, block0
                self.tiles = heads // 2

            def stat(self, t, c):
                q = self.pairs[t]
                return 2 * (t % 4) + c if self.comps == 2 else 8 * (q.qb % 2) + q.h

            def steps(self):
                return len(self.pairs) + 9

            def due(self, t, lag):
                q = t - lag
                if q >= 0 and (q + 1) % self.heads == 0 and q < len(self.pairs):
                    return q // self.heads
                return None

        atts, i0, p0, b0, probs0, keys0 = [], 0, 0, 0, 0, 0
        for kind, l in (("diff", 0), ("swa", 0), ("diff", 1), ("swa", 1), ("dil", 0)):
            pairs = {"diff": diff_pairs, "swa": lambda: swa_pairs(l), "dil": dil_pairs}[kind]()
            comps = 2 if kind == "diff" else 1
            heads, tile0 = {"diff": (6, 0), "swa": (6, 5), "dil": (8, 4)}[kind]
            if kind == "dil":
                RET_BLOCK0, b0 = b0, b0 + TB
            a = Attention(pairs, heads, comps, tile0, i0, p0, b0)
            a.kind, a.layer, a.probs0, a.keys0 = kind, l, probs0, keys0
            keys0 += {"diff": 2 * DIFF_H, "swa": SWA_H, "dil": DIL_H}[kind]
            a.m0 = {"diff": lin[f"a_out{l}"].m0, "swa": lin[f"a_out{l}"].m0 + TB + 2,
                    "dil": lin["b_mix_out0"].m0 + TB}[kind]
            probs0 += len(pairs) if comps == 2 else 0
            atts.append(a)
            i0, p0, b0 = i0 + comps * len(pairs), p0 + len(pairs), b0 + TB

        def diff_and_window(l, turn, gmlp_out):
            d, w = DIFF_ATT[l], SWA_ATT[l]
            n = len(d.pairs)
            for t in range(n + w.steps()):
                if t < d.steps():
                    turn(d, t)
                if t == d.steps():
                    gmlp_out(l)
                if t >= n:
                    turn(w, t - n)

        def dilated(turn):
            for t in range(DIL_ATT.steps()):
                turn(DIL_ATT, t)

        DIFF_ATT, SWA_ATT, DIL_ATT = (atts[0], atts[2]), (atts[1], atts[3]), atts[4]
        GLA_BLOCK0 = b0
        VT = {"a0": ([AV, AV + 1, AV + 2, BV, BV + 1, CV], 0), "a1": ([AV, AV + 1, AV + 2, BV, BV + 1, CV], 6),
              "b0": ([RV + i for i in range(4)] + [DV + i for i in range(4)], 12),
              "b1": ([GV + i for i in range(8)], 20)}
        NORM = {}
        for l in range(LAYERS):
            for n in ("a_in", "a_out", "a_ffn_in", "a_ffn_out", "a_gate", "a_ple"):
                NORM[f"{n}{l}"] = len(NORM)
        for l in range(LAYERS):
            for n in ("b_pre_in", "b_mix_in", "b_post_in"):
                NORM[f"{n}{l}"] = len(NORM)
        NORM["final"] = len(NORM)
        XR = {}
        for n in [f"a_{k}{l}" for l in range(LAYERS) for k in ("mix", "ffn", "ple")] + [
                f"b_{k}{l}" for l in range(LAYERS) for k in ("pre", "mix", "post")]:
            XR[n] = 8 * len(XR)
        XIN = {"a_in1": "a_ple0", "b_pre_in0": "a_ple1", "b_pre_in1": "b_post0"}
        for l in range(LAYERS):
            XIN.update({f"a_ffn_in{l}": f"a_mix{l}", f"a_gate{l}": f"a_ffn{l}", f"b_mix_in{l}": f"b_pre{l}",
                        f"b_post_in{l}": f"b_mix{l}"})
        XIN = {k: XR[v] for k, v in XIN.items()}
        FFN = {n: FT * i for i, n in enumerate(("a_ffn_in0", "a_ffn_in1", "b_pre_in0", "b_post_in0", "b_pre_in1",
                                                "b_post_in1"))}

        def ffn_no(name):
            return FFN[name.replace("out", "in")] // FT

        DOWN_BEFORE = {"b_mix_in0": "b_pre_out0", "b_mix_in1": "b_pre_out1", "b_pre_in1": "b_post_out0"}

        def hidden_slot(name):
            return 0 if name[0] == "a" else 4

        ROTARY = {8 + i: (RQ + i, 0) for i in range(8)}
        ROTARY.update({18 + i: (DQ + i, 1) for i in range(8)})
        ROT_N = {u: i for i, u in enumerate(sorted(ROTARY))}
        RET_VT, RET_SILU = {16 + i: i for i in range(4)}, 16
        GLA_Z, GLA_ABS, GLA_EXP, GLA_LN, GLA_SUM, GLA_VT = 9, 9, 10, 11, 13, 17
        GLA_B = {13: (0, 1), 14: (2, 3)}
        GLA_SC = {15: (0, 1), 16: (2, 3)}
        A_VT, A_LAM = {9: 0, 10: 1, 11: 2, 13: 3, 14: 4}, 15
        FREE = (0, 1, 6, 7)

        block = ctx.enter_context(nc.Block())

        @block.sync
        def _(sp):
            def load(u, slot):
                return sp.dma_start(w_raw[:, slot, :], weights[bass.ds(u, 1), :, :].rearrange("u p n -> p (u n)"))

            sp.dma_start(cols[:, :], cols_in).then_inc(cols_loaded, 16)
            for u in range(RING):
                load(u, u).then_inc(w_loaded[u], 16)
                sp.dma_start(x[:, 2 * u:2 * u + 2, :], x_in[:, 2 * u:2 * u + 2, :]).then_inc(x_loaded[u], 16)
            sp.dma_start(ident[:, :], ident_in).then_inc(consts, 16)
            sp.dma_start(rot[:, :, :], rot_in).then_inc(consts, 16)
            turns = (UNITS - RING) // RING
            with sp.Fori(0, turns) as t:
                for j in range(RING):
                    sp.wait_ge(w_lo_ready, t * RING + j + 1)
                    load(t * RING + RING + j, j).then_inc(w_loaded[j], 16)
            for u in range(RING + turns * RING, UNITS):
                sp.wait_ge(w_lo_ready, u - RING + 1)
                load(u, u % RING).then_inc(w_loaded[u % RING], 16)
            for k in range(0, KT, 2):
                sp.wait_ge(y_ready, k + 2)
                sp.dma_start(y_out[:, k:k + 2, :], y[:, k:k + 2, :]).then_inc(out_stored, 16)
            sp.wait_ge(out_stored, 16 * (KT // 2))

        @block.gpsimd
        def _(pool):
            def split(u, slot):
                pool.wait_ge(w_hi_ready, u + 1)
                nc.gpsimd.tensor_tensor(w_lo[:, slot, :], w_raw[:, slot, :], w_hi[:, slot, :].bitcast(F32),
                                        ALU.subtract).then_inc(w_lo_ready, 1)

            done = [0]

            def splits(until):
                u0 = done[0]
                turns = (until - u0) // RING
                if turns:
                    with pool.Fori(0, turns) as t:
                        for j in range(RING):
                            split(t * RING + u0 + j, (u0 + j) % RING)
                for u in range(u0 + turns * RING, until):
                    split(u, u % RING)
                done[0] = until

            def mask(dst, src, factor):
                nc.gpsimd.tensor_scalar(dst, src, factor, None, ALU.mult).then_inc(keys_masked, 1)

            chain = Chain(pool, pool_chain)

            def sub_norm(l, b):
                n = TB * l + b
                pool.wait_ge(osq_sums, n + 1)
                ge(pool, onorm_ready, DIFF_ATT[l].block0 + b if n else 0)
                inverse_root(nc.gpsimd, chain, orstd, osum, 1.0 / 64, o_v, o_t)
                nc.gpsimd.tensor_copy(o_v, orstd).then_inc(osq_rstd, 1)

            acc = diag[:, :, :].rearrange("p a b -> p (a b)")

            def add_squares(name, k0, k1):
                n = NORM[name]
                for k in range(max(k0, 1), k1):
                    pool.wait_ge(sq_ready, 8 * n + k + 1)
                    if k == 1:
                        ge(pool, bcast_done, n)
                        nc.gpsimd.tensor_tensor(acc, sq[:, 0, :], sq[:, 1, :], ALU.add).then_inc(sq_used, 2)
                    else:
                        pool.wait_ge(sq_used, 8 * n + k)
                        nc.gpsimd.tensor_tensor(acc, acc, sq[:, k % 4, :], ALU.add).then_inc(sq_used, 1)

            def up_to(name):
                splits(lin[name].u0 + RING)
                add_squares(name, 0, KT)

            for l in range(LAYERS):
                a, out = lin[f"a_in{l}"], lin[f"a_out{l}"]
                if l:
                    up_to("a_in1")
                else:
                    splits(2)
                    add_squares("a_in0", 0, 2)
                    splits(3)
                    add_squares("a_in0", 2, 4)
                    splits(4)
                    add_squares("a_in0", 4, KT)
                for i in range(DIFF_H // 2):
                    splits(a.u0 + 8 + 3 * i)
                    pool.wait_ge(bank_free, a.e0 + AK + i + 1)
                    pool.wait_ge(sq_used, 8 * (NORM[f"a_in{l}"] + 1))
                    for c in range(4):
                        mask(diff_keys[4 * i + c], big[:, AK + i, :], col("diff_rows", 4 * i + c))
                splits(out.u0 + 4)
                pool.wait_ge(bank_free, a.e0 + CK + 1)
                for h in range(SWA_H):
                    if h == 4:
                        for b in range(TB - 1):
                            sub_norm(l, b)
                        pool.wait_ge(scores_done, DIFF_ATT[l].item0 + 48)
                    if h == 1:
                        pool.wait_ge(keys_masked, DIFF_ATT[l].keys0 + 2 * DIFF_H)
                    mask(swa_keys[h], big[:, CK, :], col("swa_rows", h))
                sub_norm(l, TB - 1)
                for k in range(KT):
                    splits(out.u0 + RING + k + 1)
                    add_squares(f"a_out{l}", k, k + 1)
                up_to(f"a_ffn_in{l}")
                gate = f"a_gate{l}"
                u0 = lin[gate].u0
                splits(u0 + 1)
                add_squares(f"a_ffn_out{l}", 0, 7)
                splits(u0 + 2)
                add_squares(f"a_ffn_out{l}", 7, 8)
                add_squares(gate, 0, 2)
                splits(u0 + 3)
                add_squares(gate, 2, 4)
                splits(u0 + 4)
                add_squares(gate, 4, KT)
                for k in range(KT):
                    splits(u0 + RING + k + 1)
                    add_squares(f"a_ple{l}", k - 1, k)
                add_squares(f"a_ple{l}", 7, 8)
            up_to("b_pre_in0")
            up_to("b_mix_in0")
            splits(lin["b_mix_out0"].u0 + 4)
            pool.wait_ge(ret_scores, TB * RET_H)
            pool.wait_ge(rotated, 16)
            for h in range(DIL_H):
                mask(big[:, RQ + h, :], big[:, DK + h // 2, :], col("dil_rows", h % 2))
            for name in ("b_post_in0", "b_pre_in1", "b_mix_in1", "b_post_in1"):
                up_to(name)
            splits(UNITS)
            add_squares("final", 0, KT)

        @block.scalar
        def _(act):
            chain = Chain(act, act_chain)

            def weight_hi(slot, loads):
                act.wait_ge(w_loaded[slot], loads)
                nc.scalar.activation(w_hi[:, slot, :], w_raw[:, slot, :], ACT.Copy).then_inc(w_hi_ready, 1)

            def after_unit(L, t, s):
                act.wait_ge(unit_done, t * RING + L.u0 + s + 1)
                loads = (L.u0 + s + RING) // RING + 1
                weight_hi((L.u0 + s) % RING, t * 16 + 16 * loads)

            def plain_units(L, beside=None):
                if beside is None:
                    unit_loop(act, L.n, lambda t, s: after_unit(L, t, s))
                    return
                unit_loop(act, 8, lambda t, s: after_unit(L, t, s))
                for s in range(8, L.n):
                    after_unit(L, 0, s)
                    beside(s)

            def square(norm, k, src):
                ge(act, sq_used, 8 * norm + k - 3)
                nc.scalar.activation(sq[:, k % 4, :], src, ACT.Square).then_inc(sq_ready, 1)

            def moving_from_x(name, gain):
                L = lin[name]
                gate = name.startswith("a_gate")
                after_ffn = DOWN_BEFORE.get(name)
                if after_ffn is None:
                    ge(act, unit_done, L.u0 - 2 if gate else L.u0)
                for k in range(KT):
                    if gate and k in (1, 4):
                        after_unit(lin[f"a_ple_up{name[-1]}"], 0, k // 4)
                    if after_ffn and k == 3:
                        after_unit(lin[after_ffn], 0, FT - 1)
                    if name in XIN:
                        act.wait_ge(x_ready, XIN[name] + k + 1)
                    else:
                        act.wait_ge(x_loaded[k // 2], 16)
                    nc.scalar.activation(mvh[:, k, :], x[:, k, :], ACT.Copy, scale=col(gain, k)).then_inc(mv_hi, 1)
                    square(NORM[name], k, x[:, k, :])
                    if name == "a_in0" and k in (0, 2, 4):
                        weight_hi(k // 2 + 1, 16)

            def ffn_in(name):
                L, f0 = lin[name], FFN[name]

                def body(t, s):
                    after_unit(L, t, s)
                    if s % 2 == 0:
                        act.wait_ge(bank_free, t * RING + L.e0 + s + 1)
                        ring = (s // 2) % 2
                        nc.scalar.activation(s1[:, ring, :], g1[:, ring, :], ACT.Silu).then_inc(silu_done, 1)

                unit_loop(act, L.n - 1, body)

            def ffn_out(name, in_name, tail=0):
                L, f0, slot0 = lin[name], FFN[in_name], hidden_slot(name)

                def cast(t, s):
                    act.wait_ge(hidden_ready, t * RING + f0 + s + 1)
                    src = big[:, bass.ds(t * RING + s, 1), :].rearrange("p a b -> p (a b)")
                    nc.scalar.activation(mvh[:, slot0 + s % 4, :], src, ACT.Copy).then_inc(mv_hi, 1)

                act.wait_ge(mv_free, ffn_no(name) + 1)
                for f in range(4):
                    cast(0, f)
                after_unit(lin[in_name], 0, 2 * FT - 1)
                if name[0] == "a":
                    l = int(name[-1])
                    act.wait_ge(p_loaded, 16 * (l + 1))
                    nc.scalar.activation(mvh[:, 4:6, :], y[:, 0:2, :], ACT.Copy).then_inc(p_hi, 1)

                def body(t, s):
                    after_unit(L, t, s)
                    cast(t, s + 4)

                unit_loop(act, FT - 4, body)
                for f in range(FT - 4, FT - max(tail, 1)):
                    after_unit(L, 0, f)

            def emit(block_n, b, bank, tile0, tiles, scale):
                act.wait_ge(ot_done, block_n + 1)
                src = bank[:, 0:tiles * P].rearrange("p (a b) -> p a b", b=P)
                dst = mvh[:, tile0:tile0 + tiles, b * P:(b + 1) * P]
                if scale is None:
                    nc.scalar.activation(dst, src, ACT.Copy).then_inc(mv_hi, 1)
                else:
                    nc.scalar.activation(dst, src, ACT.Copy, scale=scale).then_inc(mv_hi, 1)

            def turn(a, t):
                n = len(a.pairs)
                b = a.due(t, 8)
                if b is not None:
                    emit(a.block0 + b, b, banks[6 + b % 2], a.tile0, a.tiles,
                         col(f"g_sub{a.layer}") if a.kind == "diff" else None)
                if t < n:
                    q = a.pairs[t]
                    for c in range(a.comps):
                        slot, sc = 2 * (t % 2) + c, a.stat(t, c)
                        act.wait_ge(scores_scaled, a.item0 + a.comps * t + c + 1)
                        if a.comps == 1:
                            ge(act, pt_done, a.pair0 + t - 1)
                        else:
                            ge(act, probs_ready, a.probs0 + t - 1)
                        nc.scalar.activation(expo[:, slot, 0:q.nkb * P], scaled[:, slot, 0:q.nkb * P], ACT.Exp,
                                             scale=-1.0, bias=neg_max[:, sc:sc + 1],
                                             accum_out=row_sum[:, sc:sc + 1]).then_inc(exp_done, 1)
                if 1 <= t <= n:
                    r = t - 1
                    act.wait_ge(pt_done, a.pair0 + r + 1)
                    ge(act, pv_done, a.pair0 + r - 1)
                    w = a.pairs[r].nkb * P
                    nc.scalar.activation(ptile[:, r % 2, 0:w], banks[4 + r % 2][:, 0:w],
                                         ACT.Copy).then_inc(pt_copied, 1)
                b = a.due(t, 3)
                if b is not None and a.kind == "diff":
                    act.wait_ge(pv_done, a.pair0 + (b + 1) * a.heads)
                    ge(act, onorm_ready, a.block0 + b)
                    nc.scalar.activation(osq[:, 0:384], banks[6 + b % 2][:, 0:384],
                                         ACT.Square).then_inc(osq_ready, 1)
                if b is not None and a.kind == "swa":
                    act.wait_ge(sink_sum, a.layer * TB + b + 1)
                    nc.scalar.activation(sink_c[:, 0:a.heads], sink_c[:, 0:a.heads],
                                         ACT.Exp).then_inc(sink_exp, 1)

            def gmlp_high(l):
                for g in range(2):
                    act.wait_ge(gated_ready, 2 * l + g + 1)
                    nc.scalar.activation(mvh[:, 3 + g, :], gtmp[:, g, :], ACT.Copy).then_inc(mv_hi, 1)

            def transposed_value(key, i):
                tiles, n0 = VT[key]
                act.wait_ge(vt_done, n0 + i + 1)
                nc.scalar.activation(big[:, tiles[i], :], banks[6 + i % 2][:, :], ACT.Copy).then_inc(vt_copied, 1)

            def transposed_values(key, first=0):
                for i in range(first, len(VT[key][0])):
                    transposed_value(key, i)

            def silus(L, tiles):
                act.wait_ge(bank_free, L.e0 + tiles[-1] + 1)
                for m in tiles:
                    nc.scalar.activation(big[:, m, :], big[:, m, :], ACT.Silu).then_inc(mixer_gates, 1)

            def beside_a(l, s):
                if s in A_VT:
                    transposed_value(f"a{l}", A_VT[s])
                if s == A_LAM:
                    act.wait_ge(lam_sum, l + 1)
                    nc.scalar.activation(lam_s[:, 2:4], lam_s[:, 0:2], ACT.Exp).then_inc(lam_exp, 1)

            def beside_retention(s):
                if s == RET_SILU:
                    silus(lin["b_mix_in0"], range(RG, RG + RET_H))
                if s in RET_VT:
                    transposed_value("b0", RET_VT[s])

            def emit_gated(n, tile0, tiles, b):
                act.wait_ge(gated_ready, n + 1)
                src = (scr[:, 8:10, :] if tiles == 8 else gtmp[:, b % 2:b % 2 + 1, :]).rearrange(
                    "p a (b c) -> p (a b) c", c=P)
                nc.scalar.activation(mvh[:, tile0:tile0 + tiles, b * P:(b + 1) * P], src,
                                     ACT.Copy).then_inc(mv_hi, 1)

            def beside_gla(s):
                for b in range(TB):
                    if s == GLA_ABS:
                        act.wait_ge(z_done, b + 1)
                        chain(nc.scalar.activation(scr[:, 4 + b, :], banks[FREE[b]][:, :], ACT.Abs))
                    if s == GLA_EXP:
                        chain(nc.scalar.activation(scr[:, 4 + b, :], scr[:, 4 + b, :], ACT.Exp, scale=-1.0))
                    if s == GLA_LN:
                        nc.scalar.activation(scr[:, 4 + b, :], scr[:, 4 + b, :], ACT.Ln, bias=1.0).then_inc(z_soft, 1)
                for h in GLA_B.get(s, ()):
                    act.wait_ge(b_done, h + 1)
                    ge(act, b_used, h)
                    nc.scalar.activation(scr[:, 8, :], banks[FREE[h]][:, :], ACT.Exp)
                    nc.scalar.activation(scr[:, 9, :], banks[FREE[h]][:, :], ACT.Exp, scale=-1.0).then_inc(b_exp, 1)
                for h in GLA_SC.get(s, ()):
                    act.wait_ge(kt_done, h + 1)
                    nc.scalar.activation(y[:, 4 + h, :], banks[h % 2][:, :], ACT.Copy).then_inc(kt_copied, 1)
                if s >= GLA_VT:
                    transposed_value("b1", s - GLA_VT)
                if s == 22:
                    silus(lin["b_mix_in1"], range(GR, GR + 4))

            def normalise(heads, count, block_n, src, dst, h0=0):
                act.wait_ge(centred, count)
                if block_n not in (RET_BLOCK0, RET_BLOCK0 + 1, GLA_BLOCK0, GLA_BLOCK0 + 1):
                    act.wait_ge(ot_done, block_n - 1)
                for h in range(heads):
                    last = nc.scalar.activation(dst(h), src(h), ACT.Identity, scale=sm_y[:, h0 + h:h0 + h + 1],
                                                bias=shift[:, h0 + h:h0 + h + 1])
                last.then_inc(onorm_ready, 1)

            def retention():
                for b in range(TB):
                    normalise(RET_H, 1, RET_BLOCK0 + b, lambda h: banks[4 + b][:, h * P:(h + 1) * P],
                              lambda h: onorm[:, b % 2, h * P:(h + 1) * P], RET_H * b)
                    if b:
                        emit_gated(2 * LAYERS + b - 1, 0, 4, b - 1)
                emit_gated(2 * LAYERS + TB - 1, 0, 4, TB - 1)

            def gla():
                silus(lin["b_mix_in1"], range(GR + 4, GR + 8))
                for b in range(TB):
                    normalise(GLA_H, 2 + b, GLA_BLOCK0 + b,
                              lambda h: banks[4 + 2 * (b % 2) + h // 2][:, (h % 2) * GLA_DV:(h % 2 + 1) * GLA_DV],
                              lambda h: scr[:, 4 + 2 * (b % 2) + h // 2, (h % 2) * GLA_DV:(h % 2 + 1) * GLA_DV])
                    if b:
                        emit_gated(2 * LAYERS + TB + b - 1, 0, 8, b - 1)
                emit_gated(2 * LAYERS + TB + TB - 1, 0, 8, TB - 1)

            weight_hi(0, 16)
            act.wait_ge(cols_loaded, 16)
            for l in range(LAYERS):
                moving_from_x(f"a_in{l}", f"a_pre{l}")
                act.dma_start(tab[:, 1280:2560], dist_in).then_inc(tables, 16)
                act.dma_start(tab[:, 0:1280], gmlp_in[l]).then_inc(tables, 16)
                plain_units(lin[f"a_in{l}"], lambda s: beside_a(l, s))
                transposed_values(f"a{l}", len(A_VT))
                diff_and_window(l, turn, gmlp_high)
                L = lin[f"a_out{l}"]
                for i in range(8):
                    after_unit(L, 0, i)
                    nc.scalar.activation(y[:, i, :], banks[BACK[i]][:, :], ACT.Copy)
                    square(NORM[f"a_out{l}"], i, banks[BACK[i]][:, :])
                moving_from_x(f"a_ffn_in{l}", f"a_pre_ffn{l}")
                act.dma_start(y[:, 0:2, :], p_in[l]).then_inc(p_loaded, 16)
                ffn_in(f"a_ffn_in{l}")
                ffn_out(f"a_ffn_out{l}", f"a_ffn_in{l}")
                act.wait_ge(p_lo, l + 1)
                for n in range(8):
                    if n < 7:
                        act.wait_ge(out_done, 7 * ffn_no(f"a_ffn_out{l}") + n + 1)
                    else:
                        after_unit(lin[f"a_ffn_out{l}"], 0, FT - 1)
                    nc.scalar.activation(y[:, n, :], banks[BACK[n]][:, :], ACT.Copy)
                    square(NORM[f"a_ffn_out{l}"], n, banks[BACK[n]][:, :])
                moving_from_x(f"a_gate{l}", f"a_gate{l}")
                L = lin[f"a_gate{l}"]
                for i in range(8):
                    after_unit(L, 0, i)
                    act.wait_ge(bank_free, L.e0 + i + 1)
                    nc.scalar.activation(s1[:, i % 2, :], g1[:, i % 2, :], ACT.Sigmoid).then_inc(gate_sig, 1)
                    if i:
                        act.wait_ge(z_ready, 8 * l + i)
                        square(NORM[f"a_ple{l}"], i - 1, y[:, i - 1, :])
                act.wait_ge(z_ready, 8 * l + 8)
                square(NORM[f"a_ple{l}"], 7, y[:, 7, :])

            for l in range(LAYERS):
                moving_from_x(f"b_pre_in{l}", f"b_pre{l}")
                if l == 0:
                    act.dma_start(tab[:, :], ret_dil_in).then_inc(tables, 16)
                    act.dma_start(y[:, 0:4, :], rotary_in).then_inc(tables, 16)
                else:
                    act.dma_start(tab[:, 0:256], gla_in).then_inc(tables, 16)
                    act.dma_start(tab[0:33, 256:768], wa2_in).then_inc(tables, 16)
                ffn_in(f"b_pre_in{l}")
                ffn_out(f"b_pre_out{l}", f"b_pre_in{l}")
                moving_from_x(f"b_mix_in{l}", f"b_mix{l}")
                plain_units(lin[f"b_mix_in{l}"], beside_gla if l else beside_retention)
                if l == 0:
                    transposed_values("b0", RET_H)
                    retention()
                    dilated(turn)
                else:
                    gla()
                plain_units(lin[f"b_mix_out{l}"])
                moving_from_x(f"b_post_in{l}", f"b_post{l}")
                ffn_in(f"b_post_in{l}")
                ffn_out(f"b_post_out{l}", f"b_post_in{l}", tail=4 if l else 0)
            for k in range(KT):
                act.wait_ge(x_ready, XR["b_post1"] + k + 1)
                square(NORM["final"], k, x[:, k, :])

        @block.vector
        def _(dve):
            chain = Chain(dve, dve_chain)

            def rsqrt(out, src, scale, n):
                inverse_root(nc.vector, chain, out, src, scale, sm_x[:, 0:n], sm_t[:, 0:n])

            def rstd_diag(norm):
                dve.wait_ge(sums_done, norm + 1)
                rsqrt(sm_y[:, 0:TB], banks[STAT][:, 0:TB], 1.0 / D, TB)
                nc.vector.tensor_tensor(diag[:, :, :], ident[:, :].unsqueeze(1).broadcast_to([P, TB, P]),
                                        sm_y[:, 0:TB].unsqueeze(2).broadcast_to([P, TB, P]),
                                        ALU.mult).then_inc(diag_ready, 1)

            def rstd_spread(norm):
                dve.wait_ge(bcast_done, norm + 1)
                chain(nc.vector.tensor_copy(rstd_b[:, :], banks[BCAST][:, :]))

            def rstd_ready(norm):
                rstd_diag(norm)
                dve.wait_ge(bcast_done, norm + 1)

            def rstd(norm):
                rstd_diag(norm)
                rstd_spread(norm)

            def enter(name, gain, update=None):
                L = lin[name]
                for k in range(KT + 1):
                    if update is not None and k < KT:
                        update(k)
                    if k:
                        dve.wait_ge(mv_hi, L.m0 + k)
                        nc.vector.scalar_tensor_tensor(out=mvl[:, k - 1, :], in0=x[:, k - 1, :],
                                                       scalar=col(gain, k - 1), in1=mvh[:, k - 1, :].bitcast(F32),
                                                       op0=ALU.mult, op1=ALU.subtract).then_inc(mv_lo, 1)

            def post(gain):
                def update(k):
                    if k == 0:
                        nc.vector.scalar_tensor_tensor(out=y[:, 0, :], in0=y[:, 0, :], scalar=col(gain, 0),
                                                       in1=banks[BCAST][:, :], op0=ALU.mult, op1=ALU.mult
                                                       ).then_inc(dve_chain, 1)
                        chain.n += 1
                    own = chain.n
                    if k + 1 < KT:
                        nc.vector.scalar_tensor_tensor(out=y[:, k + 1, :], in0=y[:, k + 1, :],
                                                       scalar=col(gain, k + 1), in1=banks[BCAST][:, :],
                                                       op0=ALU.mult, op1=ALU.mult).then_inc(dve_chain, 1)
                        chain.n += 1
                    dve.wait_ge(dve_chain, own)
                    nc.vector.tensor_tensor(x[:, k, :], x[:, k, :], y[:, k, :], ALU.add).then_inc(x_ready, 1)
                return update

            def add_down(name):
                def update(k):
                    if k < 7:
                        dve.wait_ge(out_done, 7 * ffn_no(name) + k + 1)
                    else:
                        dve.wait_ge(unit_done, lin[name].u0 + FT)
                    nc.vector.scalar_tensor_tensor(out=x[:, k, :], in0=banks[BACK[k]][:, :], scalar=0.5,
                                                   in1=x[:, k, :], op0=ALU.mult, op1=ALU.add).then_inc(x_ready, 1)
                return update

            def add_mix(L):
                def update(k):
                    dve.wait_ge(unit_done, L.u0 + k + 1)
                    nc.vector.tensor_tensor(x[:, k, :], banks[BACK[k]][:, :], x[:, k, :],
                                            ALU.add).then_inc(x_ready, 1)
                return update

            def project(name, beside=None):
                L = lin[name]

                def body(t, s):
                    dve.wait_ge(unit_done, t * RING + L.u0 + s + 1)
                    dst = big[:, bass.ds(t * RING + s, 1), :].rearrange("p a b -> p (a b)")
                    nc.vector.tensor_tensor(dst, banks[LIN[s % 4]][:, :], rstd_b[:, :], ALU.mult).then_inc(bank_free, 1)

                if beside is None:
                    unit_loop(dve, L.n, body)
                    return
                unit_loop(dve, 8, body)
                for s in range(8, L.n):
                    body(0, s)
                    beside(s)

            def ffn_in(name):
                L, f0 = lin[name], FFN[name]

                def body(t, s):
                    ring = (s // 2) % 2
                    dve.wait_ge(unit_done, t * RING + L.u0 + s + 1)
                    dst = (g1 if s % 2 == 0 else u1)[:, ring, :]
                    nc.vector.tensor_tensor(dst, banks[LIN[s % 4]][:, :], rstd_b[:, :], ALU.mult).then_inc(bank_free, 1)
                    if s % 2:
                        dve.wait_ge(silu_done, t * 2 + f0 + s // 2 + 1)
                        dve.wait_ge(bank_free, t * RING + L.e0 + s + 1)
                        dst = big[:, bass.ds(t * 2 + s // 2, 1), :].rearrange("p a b -> p (a b)")
                        nc.vector.tensor_tensor(dst, s1[:, ring, :], u1[:, ring, :], ALU.mult).then_inc(hidden_ready, 1)

                unit_loop(dve, L.n - 1, body)
                return lambda: body(0, L.n - 1)

            def ffn_out(name, last_up):
                L, slot0 = lin[name], hidden_slot(name)

                def body(t, s):
                    dve.wait_ge(mv_hi, t * RING + L.m0 + s + 1)
                    src = big[:, bass.ds(t * RING + s, 1), :].rearrange("p a b -> p (a b)")
                    nc.vector.tensor_tensor(mvl[:, slot0 + s % 4, :], src, mvh[:, slot0 + s % 4, :].bitcast(F32),
                                            ALU.subtract).then_inc(mv_lo, 1)

                for f in range(4):
                    body(0, f)
                last_up()
                if name[0] == "a":
                    dve.wait_ge(p_hi, int(name[-1]) + 1)
                    nc.vector.tensor_tensor(mvl[:, 4:6, :], y[:, 0:2, :], mvh[:, 4:6, :].bitcast(F32),
                                            ALU.subtract).then_inc(p_lo, 1)
                for f in range(4, 6):
                    body(0, f)
                with dve.Fori(0, (FT - 6) // RING) as t:
                    for j in range(RING):
                        body(t, 6 + j)

            def emit(m0, block_n, b, bank, tile0, tiles, scale):
                dve.wait_ge(mv_hi, m0 + 1)
                src = bank[:, 0:tiles * P].rearrange("p (a b) -> p a b", b=P)
                at = (slice(None), slice(tile0, tile0 + tiles), slice(b * P, (b + 1) * P))
                if scale is None:
                    nc.vector.tensor_tensor(mvl[at], src, mvh[at].bitcast(F32), ALU.subtract).then_inc(mv_lo, 1)
                else:
                    nc.vector.scalar_tensor_tensor(out=mvl[at], in0=src, scalar=scale, in1=mvh[at].bitcast(F32),
                                                   op0=ALU.mult, op1=ALU.subtract).then_inc(mv_lo, 1)

            def turn(a, t):
                n, H = len(a.pairs), a.heads
                b = a.due(t, 9)
                if b is not None:
                    emit(a.m0 + b, a.block0 + b, b, banks[6 + b % 2], a.tile0, a.tiles,
                         col(f"g_sub{a.layer}") if a.kind == "diff" else None)
                if a.kind == "diff" and t == n + 3:
                    gmlp_gate(a.layer)
                if t < n:
                    q = a.pairs[t]
                    for c in range(a.comps):
                        i, slot, sc = a.item0 + a.comps * t + c, 2 * (t % 2) + c, a.stat(t, c)
                        w = q.nkb * P
                        dve.wait_ge(scores_done, i + 1)
                        ge(dve, exp_done, a.item0 + a.comps * (t - 1))
                        nc.vector.tensor_tensor_reduce(out=scaled[:, slot, 0:w], in0=banks[slot][:, 0:w],
                                                       in1=q.bias, scale=-q.scale, scalar=q.first,
                                                       op0=ALU.add, op1=ALU.min,
                                                       accum_out=neg_max[:, sc:sc + 1]).then_inc(scores_scaled, 1)
                if a.comps == 2 and 1 <= t <= n:
                    r = t - 1
                    s0, sl, ring = 2 * (r % 2), a.stat(r, 0), r % 2
                    dve.wait_ge(exp_done, a.item0 + 2 * t)
                    ge(dve, pt_done, a.pair0 + r - 1)
                    chain(nc.vector.reciprocal(inv[:, 0:2], row_sum[:, sl:sl + 2]))
                    nc.vector.tensor_scalar(inv[:, 2:3], inv[:, 1:2], lam_s[:, 4:5], None, ALU.mult)
                    chain(nc.vector.tensor_scalar(comb[:, ring, :], expo[:, s0, :], inv[:, 0:1], None, ALU.mult))
                    nc.vector.scalar_tensor_tensor(out=comb[:, ring, :], in0=expo[:, s0 + 1, :],
                                                   scalar=inv[:, 2:3], in1=comb[:, ring, :],
                                                   op0=ALU.mult, op1=ALU.add).then_inc(probs_ready, 1)
                b = a.due(t, 2)
                if b is not None and a.kind == "swa":
                    dve.wait_ge(scores_scaled, a.item0 + (b + 1) * H)
                    chain(nc.vector.tensor_copy(sink_c[:, 0:8], neg_max[:, 8 * (b % 2):8 * (b % 2) + 8]))
                    nc.vector.tensor_tensor(sink_c[:, 0:H], sink_c[:, 0:H], col(f"sinks{a.layer}", 0, H),
                                            ALU.add).then_inc(sink_sum, 1)
                b = a.due(t, 4)
                if b is not None and a.kind == "diff":
                    dve.wait_ge(osq_ready, a.layer * TB + b + 1)
                    nc.vector.reduce_sum(osum, osq[:, 0:384].rearrange("p (h d) -> p h d", d=64),
                                         AX.X).then_inc(osq_sums, 1)
                b = a.due(t, 6)
                if b is not None:
                    scale = orstd if a.kind == "diff" else sm_y[:, 0:H]
                    o = banks[6 + b % 2][:, 0:64 * H].rearrange("p (h d) -> p h d", d=64)
                    on = onorm[:, b % 2, 0:64 * H].rearrange("p (h d) -> p h d", d=64)
                    if a.kind == "diff":
                        dve.wait_ge(osq_rstd, a.layer * TB + b + 1)
                    else:
                        dve.wait_ge(pv_done, a.pair0 + (b + 1) * H)
                        ls = row_sum[:, 8 * (b % 2):8 * (b % 2) + H]
                        dve.wait_ge(exp_done, a.item0 + (b + 1) * H)
                        if a.kind == "swa":
                            dve.wait_ge(sink_exp, a.layer * TB + b + 1)
                            chain(nc.vector.tensor_tensor(sink_c[:, 0:H], sink_c[:, 0:H], ls, ALU.add))
                            ls = sink_c[:, 0:H]
                        chain(nc.vector.reciprocal(sm_y[:, 0:H], ls))
                    ge(dve, ot_done, a.block0 + b - 1)
                    nc.vector.tensor_tensor(on, o, scale.unsqueeze(2).broadcast_to([P, H, 64]),
                                            ALU.mult).then_inc(onorm_ready, 1)

            def lam(l):
                init = 0.8 - 0.6 * math.exp(-0.3 * l)
                v = col(f"lam{l}", 0, 128).rearrange("p (a b c) -> p a b c", b=2, c=32)
                prod = onorm[:, 0, 0:64].rearrange("p (a c) -> p a c", c=32)
                chain(nc.vector.tensor_tensor(prod, v[:, :, 0, :], v[:, :, 1, :], ALU.mult))
                nc.vector.reduce_sum(lam_s[:, 0:2], prod, AX.X).then_inc(lam_sum, 1)
                dve.wait_ge(lam_exp, l + 1)
                chain(nc.vector.tensor_tensor(lam_s[:, 5:6], lam_s[:, 3:4], lam_s[:, 2:3], ALU.subtract))
                chain(nc.vector.tensor_scalar(lam_s[:, 4:5], lam_s[:, 5:6], -init, None, ALU.add))
                chain(nc.vector.tensor_scalar(neg_sinks, col(f"sinks{l}", 0, SWA_H), -1.0, None, ALU.mult))
                chain(nc.vector.tensor_scalar(col(f"g_sub{l}"), col(f"g_sub{l}"), 1.0 - init, None, ALU.mult))

            def gmlp_norm(i):
                if i < 4:
                    for m in range(2):
                        last = nc.vector.bn_stats(stats6[:, 6 * m:6 * m + 6], tok(BV + m, i, 0, P))
                    chain(last)
                    chain(nc.vector.bn_aggr(mean_var[:, 2 * i:2 * i + 2], stats6[:, 0:12]))
                elif i == 4:
                    rsqrt(sm_y[:, 8:8 + TB], mean_var[:, 1:8:2], 1.0, TB)
                elif i < 9:
                    b = i - 5
                    vn = big[:, BV:BV + 2, b * P:(b + 1) * P]
                    chain(nc.vector.tensor_scalar(vn, vn, mean_var[:, 2 * b:2 * b + 1], sm_y[:, 8 + b:9 + b],
                                                  ALU.subtract, ALU.mult))
                else:
                    m = (i - 9) % 2
                    row, op = (tab[:, 0:256], ALU.mult) if i < 11 else (tab[:, 256:512], ALU.add)
                    vn = big[:, BV + m, :].rearrange("p (b c) -> p b c", c=P)
                    last = nc.vector.tensor_tensor(vn, vn, row[:, m * P:(m + 1) * P].unsqueeze(1).broadcast_to(
                        [P, TB, P]), op)
                    if i == 12:
                        last.then_inc(vn_ready, 1)
                    else:
                        chain(last)

            def beside_a(l, s):
                if s == A_LAM:
                    lam(l)
                    dve.wait_ge(vt_copied, 6 * l + 5)
                    dve.wait_ge(tables, 16 * (2 * l + 2))
                for i in {A_LAM: range(5), A_LAM + 1: range(5, 13)}.get(s, ()):
                    gmlp_norm(i)

            def gmlp_gate(l):
                for g in range(2):
                    dve.wait_ge(mixed_done, 2 * l + g + 1)
                    t = gtmp[:, g, :].rearrange("p (b c) -> p b c", c=P)
                    chain(nc.vector.tensor_tensor(t, banks[1 + 2 * g][:, :].rearrange("p (b c) -> p b c", c=P),
                                                  tab[:, 1024 + g * P:1024 + (g + 1) * P].unsqueeze(1).broadcast_to(
                                                      [P, TB, P]), ALU.add))
                    nc.vector.tensor_tensor(gtmp[:, g, :], gtmp[:, g, :], big[:, BU + g, :],
                                            ALU.mult).then_inc(gated_ready, 1)

            def gmlp_low(l):
                m0 = lin[f"a_out{l}"].m0 + TB
                for g in range(2):
                    dve.wait_ge(mv_hi, m0 + g + 1)
                    nc.vector.tensor_tensor(mvl[:, 3 + g, :], gtmp[:, g, :], mvh[:, 3 + g, :].bitcast(F32),
                                            ALU.subtract).then_inc(mv_lo, 1)

            def centre(n, src):
                for h in range(n):
                    last = nc.vector.bn_stats(norm_stats[:, 6 * h:6 * h + 6], src(h))
                chain(last)
                for h in range(n):
                    last = nc.vector.bn_aggr(mean_var[:, 2 * h:2 * h + 2], norm_stats[:, 6 * h:6 * h + 6])
                chain(last)
                rsqrt(sm_y[:, 0:n], mean_var[:, 1:2 * n:2], 1.0, n)
                nc.vector.scalar_tensor_tensor(out=shift[:, 0:n], in0=mean_var[:, 0:2 * n:2], scalar=-1.0,
                                               in1=sm_y[:, 0:n], op0=ALU.mult, op1=ALU.mult).then_inc(centred, 1)

            def rotary(i, m, kind):
                dve.wait_ge(rot_done, i + 1)
                nc.vector.tensor_tensor(scr[:, i % 2, :], banks[i % 2][:, :], y[:, 2 * kind + 1, :], ALU.mult)
                chain(nc.vector.tensor_tensor(big[:, m, :], big[:, m, :], y[:, 2 * kind, :], ALU.mult))
                nc.vector.tensor_tensor(big[:, m, :], big[:, m, :], scr[:, i % 2, :], ALU.add).then_inc(rotated, 1)

            def beside_retention(s):
                if s == 8:
                    dve.wait_ge(tables, 16 * 6)
                if s in ROTARY:
                    rotary(ROT_N[s], *ROTARY[s])

            def retention(m0):
                i = 0
                for h in range(RET_H):
                    for jt in range(TB):
                        w = S - jt * P
                        dve.wait_ge(ret_scores, i + 1)
                        if h >= 2:
                            dve.wait_ge(ret_pv, h - 1)
                        nc.vector.tensor_tensor(y[:, 4 * (h % 2) + jt, 0:w], banks[i % 4][:, 0:w],
                                                tab[:, h * S:h * S + w], ALU.mult).then_inc(ret_decayed, 1)
                        i += 1
                dve.wait_ge(ret_pv, RET_H)
                centre(TB * RET_H, lambda h: banks[4 + h // 4][:, (h % 4) * P:(h % 4 + 1) * P])
                for b in range(TB):
                    gate(b, m0, [banks[4 + b]], RG, gtmp[:, b % 2:b % 2 + 1, :], RET_BLOCK0, 2 * LAYERS)
                    if b:
                        gated_low(b - 1, m0, gtmp[:, (b - 1) % 2:(b - 1) % 2 + 1, :])
                gated_low(TB - 1, m0, gtmp[:, 1:2, :])

            def gate(b, m0, src, gate, dst, block0, g0):
                left = b - 1 if len(src) == 1 else b
                ge(dve, mv_lo, m0 + left if left > 0 else 0)
                n = 4 * len(src)
                dve.wait_ge(mixer_gates, RET_H if n == 4 else RET_H + n)
                dve.wait_ge(ot_done, block0 + b + 1)
                for i, bank in enumerate(src):
                    if i + 1 == len(src) and i:
                        chain(last)
                    last = nc.vector.tensor_tensor(dst[:, i, :].rearrange("p (a c) -> p a c", c=P),
                                                   bank[:, :].rearrange("p (a c) -> p a c", c=P),
                                                   big[:, gate + 4 * i:gate + 4 * i + 4, b * P:(b + 1) * P], ALU.mult)
                last.then_inc(gated_ready, 1)

            def gated_low(b, m0, dst):
                n = 4 * dst.shape[1]
                dve.wait_ge(mv_hi, m0 + b + 1)
                at = (slice(None), slice(0, n), slice(b * P, (b + 1) * P))
                nc.vector.tensor_tensor(mvl[at], dst.rearrange("p a (b c) -> p (a b) c", c=P),
                                        mvh[at].bitcast(F32), ALU.subtract).then_inc(mv_lo, 1)

            def beside_gla(s):
                if s == GA:
                    dve.wait_ge(bank_free, lin["b_mix_in1"].e0 + GA + 1)
                    nc.vector.memset(big[32:33, GA, :], 1.0).then_inc(alow_ready, 1)
                if s == GLA_LN:
                    for b in range(TB):
                        dve.wait_ge(z_soft, b + 1)
                        nc.vector.scalar_tensor_tensor(out=scr[:, b, :], in0=banks[FREE[b]][:, :], scalar=0.0,
                                                       in1=scr[:, 4 + b, :], op0=ALU.min,
                                                       op1=ALU.subtract).then_inc(log_a, 1)
                for h in GLA_B.get(s, ()):
                    q, k, dec = big[:, GQ + h, :], big[:, GK + h, :], decay[:, 8 * h:8 * h + 8]
                    dve.wait_ge(b_exp, h + 1)
                    nc.vector.tensor_copy(dec, scr[:, 8, GLA_CHUNK - 1:S:GLA_CHUNK])
                    nc.vector.scalar_tensor_tensor(out=q, in0=q, scalar=128 ** -0.5, in1=scr[:, 8, :],
                                                   op0=ALU.mult, op1=ALU.mult)
                    nc.vector.tensor_tensor(k, k, scr[:, 9, :], ALU.mult).then_inc(b_used, 1)
                    dve.wait_ge(b_used, h + 1)
                    nc.vector.tensor_tensor(y[:, h, :].rearrange("p (n c) -> p n c", c=GLA_CHUNK),
                                            k.rearrange("p (n c) -> p n c", c=GLA_CHUNK),
                                            dec.unsqueeze(2).broadcast_to([P, 8, GLA_CHUNK]),
                                            ALU.mult).then_inc(kdec_ready, 1)
                if s == min(GLA_SC):
                    dve.wait_ge(tables, 16 * 8)
                for h in GLA_SC.get(s, ()):
                    dve.wait_ge(gsc_done, h + 1)
                    nc.vector.tensor_tensor(scr[:, h, :].rearrange("p (b c) -> p b c", c=P),
                                            banks[6 + h % 2][:, :].rearrange("p (b c) -> p b c", c=P),
                                            tab[:, 128:256].unsqueeze(1).broadcast_to([P, TB, P]),
                                            ALU.mult).then_inc(gsc_masked, 1)

            def gla(m0):
                for b in range(TB):
                    for n in (2 * b, 2 * b + 1):
                        if n == 7:
                            break
                        for h in range(GLA_H):
                            dve.wait_ge(kv_done, 4 * n + 2 * (h // 2) + 2)
                            kv = banks[2 * (n % 2) + h // 2][:, (h % 2) * GLA_DV:(h % 2 + 1) * GLA_DV]
                            if n == 0:
                                nc.vector.tensor_copy(state(1, h), kv).then_inc(state_ready, 1)
                                continue
                            dve.wait_ge(state_ready, 4 * (n - 1) + h + 1)
                            if n >= 2:
                                dve.wait_ge(gla_o, 4 * ((n - 1) // 2) + h + 1)
                            nc.vector.scalar_tensor_tensor(out=state(n + 1, h), in0=state(n, h),
                                                           scalar=decay[:, 8 * h + n:8 * h + n + 1], in1=kv,
                                                           op0=ALU.mult, op1=ALU.add).then_inc(state_ready, 1)
                    if b >= 2:
                        gated_low(b - 2, m0, scr[:, 8:10, :])
                    dve.wait_ge(gla_o, 4 * (b + 1))
                    ge(dve, onorm_ready, GLA_BLOCK0 + b if b else 0)
                    centre(GLA_H, lambda h: banks[4 + 2 * (b % 2) + h // 2][:, (h % 2) * GLA_DV:(h % 2 + 1) * GLA_DV])
                    if b:
                        g0 = 4 + 2 * ((b - 1) % 2)
                        gate(b - 1, m0, [banks[g0], banks[g0 + 1]], GR, scr[:, 8:10, :], GLA_BLOCK0, 2 * LAYERS + TB)
                gated_low(TB - 2, m0, scr[:, 8:10, :])
                gate(TB - 1, m0, [banks[6], banks[7]], GR, scr[:, 8:10, :], GLA_BLOCK0, 2 * LAYERS + TB)
                gated_low(TB - 1, m0, scr[:, 8:10, :])

            nc.vector.memset(ones[:, :], 1.0).then_inc(ones_set, 1)
            nc.vector.memset(small[:, :], 0.0).then_inc(bank_free, len(LIN))
            update = None
            for l in range(LAYERS):
                enter(f"a_in{l}", f"a_pre{l}", update)
                dve.wait_ge(consts, 32)
                rstd(NORM[f"a_in{l}"])
                project(f"a_in{l}", lambda s: beside_a(l, s))
                diff_and_window(l, turn, gmlp_low)
                rstd_ready(NORM[f"a_out{l}"])
                enter(f"a_ffn_in{l}", f"a_pre_ffn{l}", post(f"a_post{l}"))
                rstd(NORM[f"a_ffn_in{l}"])
                ffn_out(f"a_ffn_out{l}", ffn_in(f"a_ffn_in{l}"))
                up = lin[f"a_ple_up{l}"]
                for n in range(4):
                    if n == 0:
                        dve.wait_ge(unit_done, up.u0 + 1)
                    if n == 2:
                        rstd_diag(NORM[f"a_ffn_out{l}"])
                    nc.vector.tensor_copy(big[:, n, :], banks[LIN[n]][:, :]).then_inc(bank_free, 1)
                dve.wait_ge(bcast_done, NORM[f"a_ffn_out{l}"] + 1)
                add = post(f"a_post_ffn{l}")

                def update(k):
                    add(k)
                    if k == 1:
                        dve.wait_ge(unit_done, up.u0 + 2)
                        for n in range(4):
                            nc.vector.tensor_copy(big[:, 4 + n, :], banks[LIN[n]][:, :]).then_inc(bank_free, 1)

                enter(f"a_gate{l}", f"a_gate{l}", update)
                rstd(NORM[f"a_gate{l}"])
                L = lin[f"a_gate{l}"]
                for i in range(9):
                    if i < 8:
                        dve.wait_ge(unit_done, L.u0 + i + 1)
                        nc.vector.tensor_tensor(g1[:, i % 2, :], banks[LIN[i % 4]][:, :], rstd_b[:, :],
                                                ALU.mult).then_inc(bank_free, 1)
                    if i:
                        dve.wait_ge(gate_sig, 8 * l + i)
                        nc.vector.tensor_tensor(y[:, i - 1, :], s1[:, (i - 1) % 2, :], big[:, i - 1, :],
                                                ALU.mult).then_inc(z_ready, 1)
                rstd_ready(NORM[f"a_ple{l}"])
                update = post(f"a_ple{l}")

            for l in range(LAYERS):
                enter(f"b_pre_in{l}", f"b_pre{l}", update)
                rstd(NORM[f"b_pre_in{l}"])
                ffn_out(f"b_pre_out{l}", ffn_in(f"b_pre_in{l}"))
                enter(f"b_mix_in{l}", f"b_mix{l}", add_down(f"b_pre_out{l}"))
                rstd(NORM[f"b_mix_in{l}"])
                project(f"b_mix_in{l}", beside_gla if l else beside_retention)
                m0 = lin[f"b_mix_out{l}"].m0
                if l == 0:
                    retention(m0)
                    dve.wait_ge(vt_copied, 20)
                    dilated(turn)
                else:
                    gla(m0)
                L = lin[f"b_mix_out{l}"]
                enter(f"b_post_in{l}", f"b_post{l}", add_mix(L))
                rstd(NORM[f"b_post_in{l}"])
                ffn_out(f"b_post_out{l}", ffn_in(f"b_post_in{l}"))
                update = add_down(f"b_post_out{l}")
            for k in range(KT):
                update(k)
            rstd_ready(NORM["final"])
            for k in range(KT):
                nc.vector.scalar_tensor_tensor(out=y[:, k, :], in0=x[:, k, :], scalar=col("final", k),
                                               in1=banks[BCAST][:, :], op0=ALU.mult,
                                               op1=ALU.mult).then_inc(y_ready, 1)

        @block.tensor
        def _(pe):
            def three(bank, slot, tile, k, first, last):
                hi, lo = w_hi[:, slot, tile * P:(tile + 1) * P], w_lo[:, slot, tile * P:(tile + 1) * P]
                nc.tensor.matmul(bank[:, :], hi, mvh[:, k, :], start=first, stop=False)
                nc.tensor.matmul(bank[:, :], hi, mvl[:, k, :], start=False, stop=False)
                return nc.tensor.matmul(bank[:, :], lo, mvh[:, k, :], start=False, stop=last)

            def wide(name):
                L = lin[name]
                back = [f"a_out{l}" for l in range(LAYERS)] + [f"b_mix_out{l}" for l in range(LAYERS)]

                def body(t, s):
                    slot = (L.u0 + s) % RING
                    pe.wait_ge(w_lo_ready, t * RING + L.u0 + s + 1)
                    bank = banks[BACK[s] if name in back else LIN[s % 4]]
                    if name not in back:
                        pe.wait_ge(bank_free, t * RING + L.e0 + s - 3)
                    for k in range(8):
                        last = three(bank, slot, k, k, k == 0, k == 7)
                    last.then_inc(unit_done, 1)

                return L, body

            def sum_squares(norm):
                pe.wait_ge(sq_used, 8 * (norm + 1))
                for b in range(TB):
                    last = nc.tensor.matmul(banks[STAT][:, b:b + 1], diag[:, b, :], ones[:, 0:1], start=True, stop=True)
                last.then_inc(sums_done, 1)

            def spread(norm):
                pe.wait_ge(diag_ready, norm + 1)
                nc.tensor.matmul(banks[BCAST][:, :], ones[:, :], diag[:, :, :].rearrange("p a b -> p (a b)"),
                                 start=True, stop=True).then_inc(bcast_done, 1)

            def from_x(name, norm, beside=None):
                L, body = wide(name)

                def product(j, k):
                    last = three(banks[LIN[j]], (L.u0 + j) % RING, k, k, k == 0, k == KT - 1)
                    if k == KT - 1:
                        last.then_inc(unit_done, 1)

                for k in range(KT - 3):
                    pe.wait_ge(mv_lo, L.m0 + k + 1)
                    for j in range(min(k, RING)):
                        product(j, k)
                    if k < RING:
                        pe.wait_ge(w_lo_ready, L.u0 + k + 1)
                        pe.wait_ge(bank_free, L.e0 + k - 3)
                        for i in range(k + 1):
                            product(k, i)
                for j in range(RING):
                    for k in range(KT - 3, KT):
                        if j == 0:
                            pe.wait_ge(mv_lo, L.m0 + k + 1)
                        product(j, k)
                    if j == 0:
                        sum_squares(norm)
                    if j == 2:
                        spread(norm)
                if L.n == 2 * FT:
                    rest(L, body, RING, 1)
                    s = L.n - 1
                    pe.wait_ge(w_lo_ready, L.u0 + s + 1)
                    pe.wait_ge(bank_free, L.e0 + s - 3)
                    for i in range(KT):
                        k = (hidden_slot(name) + i) % KT
                        last = three(banks[LIN[s % 4]], (L.u0 + s) % RING, k, k, i == 0, i == KT - 1)
                        if i == 3:
                            last.then_inc(mv_free, 1)
                    last.then_inc(unit_done, 1)
                    return
                if beside is None:
                    rest(L, body, RING)
                    return
                for s in range(RING, L.n):
                    body(0, s)
                    beside(s)

            def rest(L, body, done, tail=0):
                head = (L.n - tail - done) % RING
                for i in range(done, done + head):
                    body(0, i)
                turns = (L.n - tail - done - head) // RING
                if turns:
                    with pe.Fori(0, turns) as t:
                        for j in range(RING):
                            body(t, done + head + j)

            def from_cat(name):
                L, body = wide(name)
                pe.wait_ge(mv_lo, L.m0 + L.moving)
                return L, body

            def down(name):
                L = lin[name]

                def body(t, s, first=False):
                    slot = (L.u0 + s) % RING
                    pe.wait_ge(w_lo_ready, t * RING + L.u0 + s + 1)
                    pe.wait_ge(mv_lo, t * RING + L.m0 + s + 1)
                    for n in range(8):
                        if first and BACK[n] in LIN:
                            pe.wait_ge(bank_free, L.e0 - 3 + LIN.index(BACK[n]))
                        last = three(banks[BACK[n]], slot, n, hidden_slot(name) + s % 4, first, s == FT - 1)
                        if s == FT - 1 and n < 7:
                            last.then_inc(out_done, 1)
                    last.then_inc(unit_done, 1)

                body(0, 0, True)
                body(0, 1)
                with pe.Fori(0, (FT - 6) // RING) as t:
                    for j in range(RING):
                        body(t, 2 + j)
                for f in range(FT - 4, FT):
                    body(0, f)

            def ple_tile(l, n):
                L = lin[f"a_ple_up{l}"]
                i, n4 = n // 4, n % 4
                if n4 == 0:
                    pe.wait_ge(w_lo_ready, L.u0 + i + 1)
                    pe.wait_ge(p_lo, l + 1)
                pe.wait_ge(bank_free, L.e0 + n - 3)
                for k in range(2):
                    last = three(banks[LIN[n4]], (L.u0 + i) % RING, 2 * n4 + k, 4 + k, k == 0, k == 1)
                if n4 == 3:
                    last.then_inc(unit_done, 1)

            def transpose_value(key, i):
                tiles, n0 = VT[key]
                ge(pe, vt_copied, n0 + i - 1)
                for b in range(TB):
                    last = nc.tensor.transpose(banks[6 + i % 2][:, b * P:(b + 1) * P],
                                               big[:, tiles[i], b * P:(b + 1) * P], ident[:, :])
                last.then_inc(vt_done, 1)

            def transpose_values(key, first=0):
                for i in range(first, len(VT[key][0])):
                    transpose_value(key, i)

            def turn(a, t):
                n, H = len(a.pairs), a.heads

                def scores(t):
                    q = a.pairs[t]
                    ge(pe, scores_scaled, a.item0 + a.comps * (t - 1))
                    if q.qb == 0:
                        pe.wait_ge(keys_masked, a.keys0 + q.masked)
                    for c, (lhs, rhs) in enumerate(q.parts):
                        nc.tensor.matmul(banks[2 * (t % 2) + c][:, 0:q.nkb * P], lhs, rhs, start=True,
                                         stop=True).then_inc(scores_done, 1)

                if t == 0:
                    scores(0)
                if t + 1 < n:
                    scores(t + 1)
                if 1 <= t <= n:
                    r = t - 1
                    q = a.pairs[r]
                    if a.comps == 2:
                        pe.wait_ge(probs_ready, a.probs0 + r + 1)
                        src = comb[:, r % 2, :]
                    else:
                        pe.wait_ge(exp_done, a.item0 + r + 1)
                        src = expo[:, 2 * (r % 2), :]
                    ge(pe, pt_copied, a.pair0 + r - 1)
                    for kb in range(q.nkb):
                        last = nc.tensor.transpose(banks[4 + r % 2][:, kb * P:(kb + 1) * P],
                                                   src[:, kb * P:(kb + 1) * P], ident[:, :])
                    last.then_inc(pt_done, 1)
                if 2 <= t <= n + 1:
                    r = t - 2
                    q = a.pairs[r]
                    pe.wait_ge(pt_copied, a.pair0 + r + 1)
                    if r == 0 and a.kind == "diff":
                        pe.wait_ge(vt_copied, 6 * (a.layer + 1))
                    if q.h == 0 and q.qb >= 2:
                        pe.wait_ge(mv_lo, a.m0 + q.qb - 1)
                    elif q.h == 0 and a.kind == "swa":
                        pe.wait_ge(mv_lo, a.m0 - 2 - TB + q.qb + 3)
                    for kb in range(q.nkb):
                        last = nc.tensor.matmul(banks[6 + q.qb % 2][:, q.h * 64:(q.h + 1) * 64],
                                                ptile[:, r % 2, kb * P:(kb + 1) * P], q.v(q.kb0 + kb),
                                                start=(kb == 0), stop=(kb == q.nkb - 1))
                    last.then_inc(pv_done, 1)
                if a.kind == "diff" and t == n + 1:
                    gmlp(a.layer)
                b = a.due(t, 7)
                if b is not None:
                    transpose_out(a.block0 + b, [banks[6 + b % 2]], a.tiles, onorm[:, b % 2:b % 2 + 1, :])

            def transpose_out(block_n, dst, tiles, src):
                pe.wait_ge(onorm_ready, block_n + 1)
                for m in range(tiles):
                    last = nc.tensor.transpose(dst[m // 4][:, (m % 4) * P:(m % 4 + 1) * P],
                                               src[:, m // 4, (m % 4) * P:(m % 4 + 1) * P], ident[:, :])
                last.then_inc(ot_done, 1)

            def gmlp(l):
                pe.wait_ge(tables, 16 * (2 * l + 2))
                pe.wait_ge(vn_ready, l + 1)
                for g in range(4):
                    p0 = 64 * (g % 2)
                    for b in range(TB):
                        last = nc.tensor.matmul(banks[1 + 2 * (g // 2)][p0:p0 + 64, b * P:(b + 1) * P],
                                                tok(BV + g // 2, b, p0, 64), tab[:, 512 + g * P:512 + (g + 1) * P],
                                                start=True, stop=True)
                    if g % 2:
                        last.then_inc(mixed_done, 1)

            def beside_a(l, s):
                if s == min(A_VT):
                    pe.wait_ge(consts, 32)
                if s in A_VT:
                    i = A_VT[s]
                    pe.wait_ge(bank_free, lin[f"a_in{l}"].e0 + VT[f"a{l}"][0][i] + 1)
                    transpose_value(f"a{l}", i)

            def beside_retention(s):
                L = lin["b_mix_in0"]
                if s in ROTARY:
                    (m, kind), i = ROTARY[s], ROT_N[s]
                    pe.wait_ge(bank_free, L.e0 + m + 1)
                    ge(pe, rotated, i - 1)
                    nc.tensor.matmul(banks[i % 2][:, :], rot[:, kind, :], big[:, m, :], start=True,
                                     stop=True).then_inc(rot_done, 1)
                if s in RET_VT:
                    pe.wait_ge(bank_free, L.e0 + RV + RET_VT[s] + 1)
                    transpose_value("b0", RET_VT[s])

            def retention():
                pe.wait_ge(rotated, 16)
                for h in range(RET_H + 1):
                    if h < RET_H:
                        for jt in range(TB):
                            i = TB * h + jt
                            ge(pe, ret_decayed, i - 3)
                            nc.tensor.matmul(banks[i % 4][:, 0:S - jt * P], big[:, RK + h, jt * P:(jt + 1) * P],
                                             big[:, RQ + h, jt * P:S], start=True, stop=True).then_inc(ret_scores, 1)
                    if h == 1:
                        pe.wait_ge(vt_copied, 20)
                    if h:
                        r = h - 1
                        pe.wait_ge(ret_decayed, TB * (r + 1))
                        for b in range(TB):
                            for jt in range(b + 1):
                                last = nc.tensor.matmul(banks[4 + b][:, r * P:(r + 1) * P],
                                                        y[:, 4 * (r % 2) + jt, (b - jt) * P:(b - jt + 1) * P],
                                                        tok(RV + r, jt, 0, P), start=(jt == 0), stop=(jt == b))
                        last.then_inc(ret_pv, 1)
                for b in range(TB):
                    transpose_out(RET_BLOCK0 + b, [banks[4 + b]], 4, onorm[:, b % 2:b % 2 + 1, :])

            def beside_gla(s):
                L = lin["b_mix_in1"]
                if s == GLA_Z:
                    pe.wait_ge(tables, 16 * 8)
                    pe.wait_ge(alow_ready, 1)
                    for b in range(TB):
                        nc.tensor.matmul(banks[FREE[b]][:, :], big[0:33, GA, b * P:(b + 1) * P],
                                         tab[0:33, 256:768], start=True, stop=True).then_inc(z_done, 1)
                if s == GLA_SUM:
                    pe.wait_ge(log_a, TB)
                    for h in range(GLA_H):
                        for b in range(TB):
                            last = nc.tensor.matmul(banks[FREE[h]][:, b * P:(b + 1) * P],
                                                    scr[:, b, h * P:(h + 1) * P], tab[:, 0:128], start=True, stop=True)
                        last.then_inc(b_done, 1)
                for h in GLA_SC.get(s, ()):
                    pe.wait_ge(b_exp, GLA_H)
                    pe.wait_ge(kdec_ready, h + 1)
                    ge(pe, kt_copied, h - 1)
                    for b in range(TB):
                        last = nc.tensor.transpose(banks[h % 2][:, b * P:(b + 1) * P], y[:, h, b * P:(b + 1) * P],
                                                   ident[:, :])
                    last.then_inc(kt_done, 1)
                    ge(pe, gsc_masked, h - 1)
                    for b in range(TB):
                        last = nc.tensor.matmul(banks[6 + h % 2][:, b * P:(b + 1) * P],
                                                big[:, GK + h, b * P:(b + 1) * P], big[:, GQ + h, b * P:(b + 1) * P],
                                                start=True, stop=True)
                    last.then_inc(gsc_done, 1)
                if s >= GLA_VT:
                    i = s - GLA_VT
                    pe.wait_ge(bank_free, L.e0 + GV + i + 1)
                    ge(pe, gsc_masked, min(GLA_H, i + 3))
                    transpose_value("b1", i)

            def gla():
                pe.wait_ge(kt_copied, GLA_H)
                pe.wait_ge(gsc_masked, GLA_H)
                for b in range(TB + 1):
                    if b < TB:
                        for n in (2 * b, 2 * b + 1):
                            if n == 7:
                                break
                            p0 = 64 * (n % 2)
                            ge(pe, state_ready, 4 * (n - 1))
                            for h in range(GLA_H):
                                nc.tensor.matmul(banks[2 * (n % 2) + h // 2][:, (h % 2) * GLA_DV:(h % 2 + 1) * GLA_DV],
                                                 y[p0:p0 + 64, 4 + h, b * P:(b + 1) * P],
                                                 big[p0:p0 + 64, GV + 2 * h:GV + 2 * h + 2, b * P:(b + 1) * P],
                                                 start=True, stop=True).then_inc(kv_done, 1)
                        if b >= 2:
                            pe.wait_ge(gated_ready, 2 * LAYERS + TB + b - 1)
                        for h in range(GLA_H):
                            bank = banks[4 + 2 * (b % 2) + h // 2]
                            c0 = (h % 2) * GLA_DV
                            last = nc.tensor.matmul(bank[:, c0:c0 + GLA_DV], scr[:, h, b * P:(b + 1) * P],
                                                    big[:, GV + 2 * h:GV + 2 * h + 2, b * P:(b + 1) * P],
                                                    start=True, stop=False, skip_group_check=True)
                            for n in (2 * b, 2 * b + 1):
                                if n == 0:
                                    continue
                                pe.wait_ge(state_ready, 4 * (n - 1) + h + 1)
                                p0 = 64 * (n % 2)
                                last = nc.tensor.matmul(bank[p0:p0 + 64, c0:c0 + GLA_DV],
                                                        big[:, GQ + h, n * 64:(n + 1) * 64], state(n, h),
                                                        start=False, stop=True, skip_group_check=True)
                            last.then_inc(gla_o, 1)
                    if b:
                        r = b - 1
                        transpose_out(GLA_BLOCK0 + r, [banks[4 + 2 * (r % 2)], banks[5 + 2 * (r % 2)]], 8,
                                      scr[:, 4 + 2 * (r % 2):6 + 2 * (r % 2), :])

            pe.wait_ge(ones_set, 1)
            for l in range(LAYERS):
                from_x(f"a_in{l}", NORM[f"a_in{l}"], lambda s: beside_a(l, s))
                pe.wait_ge(bank_free, lin[f"a_in{l}"].e0 + 18)
                transpose_values(f"a{l}", len(A_VT))
                diff_and_window(l, turn, lambda l: None)
                L, body = from_cat(f"a_out{l}")
                for i in range(8):
                    body(0, i)
                sum_squares(NORM[f"a_out{l}"])
                spread(NORM[f"a_out{l}"])
                from_x(f"a_ffn_in{l}", NORM[f"a_ffn_in{l}"])
                down(f"a_ffn_out{l}")
                norm = NORM[f"a_ffn_out{l}"]
                for n in range(4):
                    pe.wait_ge(sq_ready, 8 * norm + BACK.index(LIN[n]) + 1)
                    ple_tile(l, n)
                sum_squares(norm)
                ple_tile(l, 4)
                ple_tile(l, 5)
                spread(norm)
                ple_tile(l, 6)
                ple_tile(l, 7)
                from_x(f"a_gate{l}", NORM[f"a_gate{l}"])
                sum_squares(NORM[f"a_ple{l}"])
                spread(NORM[f"a_ple{l}"])
            for l in range(LAYERS):
                from_x(f"b_pre_in{l}", NORM[f"b_pre_in{l}"])
                down(f"b_pre_out{l}")
                from_x(f"b_mix_in{l}", NORM[f"b_mix_in{l}"], beside_gla if l else beside_retention)
                pe.wait_ge(bank_free, lin[f"b_mix_in{l}"].e0 + lin[f"b_mix_in{l}"].n)
                if l == 0:
                    transpose_values("b0", RET_H)
                    retention()
                    pe.wait_ge(gated_ready, 2 * LAYERS + TB)
                    dilated(turn)
                else:
                    pe.wait_ge(vt_copied, 28)
                    gla()
                L, body = from_cat(f"b_mix_out{l}")
                for i in range(8):
                    body(0, i)
                from_x(f"b_post_in{l}", NORM[f"b_post_in{l}"])
                down(f"b_post_out{l}")
            sum_squares(NORM["final"])
            spread(NORM["final"])


def tiles_of(w):
    k, n = w.shape
    return w.reshape(k // P, P, n // P, P).transpose(2, 1, 0, 3).reshape(n // P, P, k)


def weight_units(i):
    out = []

    def ffn(gate, up, down):
        g, u = tiles_of(gate), tiles_of(up)
        out.append(np.stack([g, u], axis=1).reshape(-1, P, UNIT))
        out.append(down.reshape(FT, P, D))

    swa0 = 2304 - 256 - 384
    order = [h for t in range(3) for h in (t, 3 + t)]
    for l in range(LAYERS):
        w = i["w_in"][l]
        q = w[:, swa0:swa0 + 384].reshape(D, 6, 64)[:, order].reshape(D, 384)
        out.append(tiles_of(np.concatenate([w[:, :swa0], q, w[:, swa0 + 384:]], axis=1)))
        out.append(tiles_of(i["w_out"][l]))
        ffn(i["w_ffn_in"][l][:, :FT * P], i["w_ffn_in"][l][:, FT * P:], i["w_ffn_out"][l])
        up = tiles_of(i["w_ple_up"][l])
        out.append(up.reshape(2, 4, P, 256).transpose(0, 2, 1, 3).reshape(2, P, UNIT))
        out.append(tiles_of(i["w_ple_gate"][l]))
    for l in range(LAYERS):
        ffn(i["ffn_pre_w_gate_2"][l], i["ffn_pre_w_up_2"][l], i["ffn_pre_w_down_2"][l])
        if l == 0:
            out.append(tiles_of(i["ab_w_in_2"][0]))
            out.append(tiles_of(i["ab_w_out_2"][0]))
        else:
            w = i["gla_w_in_2"][0]
            a = 2 * 512 + 2 * 1024
            pad = np.zeros((D, 25 * P - w.shape[1]), w.dtype)
            out.append(tiles_of(np.concatenate([w[:, :1024], w[:, a:], pad, w[:, 1024:a]], axis=1)))
            out.append(tiles_of(i["gla_w_out_2"][0]))
        ffn(i["ffn_post_w_gate_2"][l], i["ffn_post_w_up_2"][l], i["ffn_post_w_down_2"][l])
    return np.ascontiguousarray(np.concatenate(out, axis=0))


def column_table(i):
    at, n = column_layout()
    t = np.zeros((P, n), np.float32)
    for l in range(LAYERS):
        for name, key in (("a_pre", "g_pre_mix"), ("a_post", "g_post_mix"), ("a_pre_ffn", "g_pre_ffn"),
                          ("a_post_ffn", "g_post_ffn"), ("a_gate", "g_ple_gate"), ("a_ple", "g_ple_post"),
                          ("b_pre", "ffn_pre_norm_2"), ("b_mix", "mix_norm_2"), ("b_post", "ffn_post_norm_2")):
            t[:, at[f"{name}{l}"]:at[f"{name}{l}"] + 8] = i[key][l].reshape(8, P).T
        t[:, at[f"g_sub{l}"]] = np.tile(i["g_diff_sub"][l], 2)
        t[:, at[f"sinks{l}"]:at[f"sinks{l}"] + 6] = i["swa_sinks"][l][None]
        lam = np.concatenate([i[k][l] for k in ("lam_q1", "lam_k1", "lam_q2", "lam_k2")])
        t[:, at[f"lam{l}"]:at[f"lam{l}"] + 128] = lam[None]
    diff_slopes, swa_slopes = slopes()
    for c in range(2 * DIFF_H):
        p0 = 32 * (c % 4)
        t[p0:p0 + 32, at["diff_rows"] + c] = np.float32(32 ** -0.5) / diff_slopes[c // 2]
    for h in range(SWA_H):
        p0 = 64 * (h // 3)
        t[p0:p0 + 64, at["swa_rows"] + h] = np.float32(0.125) / swa_slopes[h]
    for c in range(2):
        t[64 * c:64 * c + 64, at["dil_rows"] + c] = 1.0
    t[:, at["final"]:at["final"] + 8] = i["final_norm_2"].reshape(8, P).T
    return t


def gmlp_table(i):
    out = []
    for l in range(LAYERS):
        w = i["w_spatial"][l].transpose(2, 0, 1).reshape(P, 4 * P)
        bias = np.repeat(i["b_spatial"][l].reshape(2, 2, 1, P), 64, axis=2).reshape(2, P, P)
        out.append(np.concatenate([np.tile(i["gmlp_ln_g"][l], (P, 1)), np.tile(i["gmlp_ln_b"][l], (P, 1)), w,
                                   bias.transpose(1, 0, 2).reshape(P, 2 * P)], axis=1))
    return np.ascontiguousarray(np.stack(out))


def constants():
    p = np.arange(P)[:, None]
    diff = -np.abs(p - (np.arange(896)[None] - 384)).astype(np.float32)
    dist = np.abs(p - (np.arange(384)[None] - P)).astype(np.float32)
    swa = np.where(dist <= 128, -dist, NEG)
    rel = np.arange(S)[None] - p
    log_g = np.log(1.0 - 2.0 ** (-5.0 - np.arange(4, dtype=np.float32))).astype(np.float32)
    ret = np.concatenate([np.where(rel >= 0, np.exp(g * np.maximum(rel, 0)), 0.0) * 128 ** -0.5 for g in log_g],
                         axis=1)
    d = p - (np.arange(512)[None] - 384)
    count = ((d <= 128) * 1 + (d % 4 == 0) * 1 + (d % 16 == 0) * 1) * (d >= 0)
    dil = np.where(count > 0, np.log(np.maximum(count, 1)) * 8.0, NEG)
    pos = np.arange(S, dtype=np.float32)
    f_ret = np.float32(10000.0) ** (-np.linspace(0.0, 1.0, 64, dtype=np.float32))
    f_dil = np.float32(500000.0) ** (-np.arange(0, 16, 2, dtype=np.float32) / np.float32(16))
    a_ret = f_ret[np.arange(P) % 64][:, None] * pos[None]
    a_dil = np.zeros((P, S), np.float32)
    rot = np.zeros((P, 2, P), np.float32)
    for m in range(64):
        rot[m + 64, 0, m], rot[m, 0, m + 64] = -1.0, 1.0
    for h in range(2):
        for m in range(8):
            lo, hi = 64 * h + m, 64 * h + m + 8
            a_dil[lo] = a_dil[hi] = f_dil[m] * pos
            rot[hi, 1, lo], rot[lo, 1, hi] = -1.0, 1.0
    rotary = np.stack([np.cos(a_ret), np.sin(a_ret), np.cos(a_dil), np.sin(a_dil)], axis=1)
    c = np.arange(P)[None]
    causal = ((p <= c) & (p // 64 == c // 64)).astype(np.float32)
    gla = np.concatenate([causal / 16, causal], axis=1)
    f = lambda a: np.ascontiguousarray(a, dtype=np.float32)
    return {"dist": f(np.concatenate([diff, swa], axis=1)), "ident": f(np.eye(P)), "rot": f(rot), "rotary": f(rotary),
            "ret_dil": f(np.concatenate([ret, dil], axis=1)), "gla": f(gla)}


def kernel(**inputs):
    import concourse.bacc as bacc
    from concourse.bass_utils import run_bass_kernel_spmd

    i = {k: np.asarray(v) for k, v in inputs.items()}
    c = constants()
    wa2 = np.zeros((33, 512), np.float32)
    wa2[0:16], wa2[32] = i["gla_w_a2_2"][0], i["gla_b_a_2"][0]
    arrays = {
        "x": np.ascontiguousarray(i["x"][0].T.reshape(KT, P, S).transpose(1, 0, 2)),
        "p": np.ascontiguousarray(i["p"][:, 0].transpose(0, 2, 1).reshape(LAYERS, 2, P, S).transpose(0, 2, 1, 3)),
        "weights": weight_units(i), "cols": column_table(i), "gmlp": gmlp_table(i),
        "dist": c["dist"], "ident": c["ident"], "rot": c["rot"],
        "rotary": c["rotary"], "ret_dil": c["ret_dil"], "gla": c["gla"], "wa2": wa2,
    }
    nc = bacc.Bacc("TRN2", target_bir_lowering=False, num_devices=1)
    args = [nc.dram_tensor(f"in_{k}", a.shape, mybir.dt.from_np(a.dtype), kind="ExternalInput").ap()
            for k, a in arrays.items()]
    out = nc.dram_tensor("out_y", (P, KT, S), F32, kind="ExternalOutput").ap()
    program(nc, *args, out)
    r = run_bass_kernel_spmd(nc, [{f"in_{k}": a for k, a in arrays.items()}], core_ids=[0])
    y = r.results[0]["out_y"]
    return np.ascontiguousarray(y.transpose(1, 0, 2).reshape(D, S).T)[None]
```
